# Optimizing a Trainium2 kernel written in Bass

```python
import math
import jax, jax.numpy as jnp
from jax import lax
import numpy as np

D_MODEL = 1024
BATCH = 1
SEQ = 128
DEPTH = 2
DEC_BATCH = 1
DEC_SEQ = 256
PAST_LEN = 128

GRID_W = 64
N_EVEN = (DEPTH + 1) // 2
N_ODD = DEPTH // 2
D_A = D_MODEL // 2
D_B = D_MODEL // 2
B_GROUPS = 4
CHUNK = 128
D_EVEN_IN = 3 * D_A + 2 * D_B
D_C = D_MODEL // 4
C_GROUPS = 4
C_GW = D_C // C_GROUPS
N_HEADS = 12
QK_NOPE = 64
QK_ROPE = 32
V_DIM = 64
Q_LORA = 384
KV_LORA = 256
D_ODD_IN = D_C + Q_LORA + KV_LORA + QK_ROPE
ROPE_BASE = 10000.0
Q_BLOCK = 128
N_GROUPS_MOE = 4
EXPERTS_PER_GROUP = 4
N_EXPERTS = N_GROUPS_MOE * EXPERTS_PER_GROUP
TOP_K = 2
D_EXPERT = 256
EPS = 1e-6
MOD_SCALE = 0.5

kernel_name = "hybrid_diffusion_prefix_step"

def rms_norm(x, g):
    xf = x.astype(jnp.float32)
    y = xf * lax.rsqrt(jnp.mean(xf * xf, axis=-1, keepdims=True) + EPS)
    return (y * g.astype(jnp.float32)).astype(x.dtype)

def adaln_params(cond, w, b):
    m = (jax.nn.silu(cond) @ w + b)[:, None, :]
    return jnp.split(m, 6, axis=-1)

def grid_positions(n_tokens):
    rows = n_tokens // GRID_W
    row = jnp.repeat(jnp.arange(rows), GRID_W)
    col = jnp.tile(jnp.arange(GRID_W), rows)
    return row, col

def axial_rope(x, row, col):
    half = QK_ROPE // 2
    nf = half // 2
    inv = ROPE_BASE ** (-jnp.arange(nf, dtype=jnp.float32) / nf)
    parts = []
    for pos, xq in ((row, x[..., :half]), (col, x[..., half:])):
        ang = pos.astype(jnp.float32)[:, None] * inv[None, :]
        if x.ndim == 4:
            ang = ang[:, None, :]
        cos = jnp.cos(ang).astype(x.dtype)
        sin = jnp.sin(ang).astype(x.dtype)
        a, b = xq[..., :nf], xq[..., nf:]
        parts += [a * cos - b * sin, b * cos + a * sin]
    return jnp.concatenate(parts, axis=-1)

def short_conv3(z, w):
    zp = jnp.pad(z, ((0, 0), (1, 1), (0, 0)))
    return zp[:, :-2] * w[0] + zp[:, 1:-1] * w[1] + zp[:, 2:] * w[2]

def even_mixer(h, w_in, conv_w, sgu_norm_g, sgu_w, sgu_b, w_out):
    bsz, n, _ = h.shape
    z = h @ w_in
    gate_b, gate_c, xa, u, v = jnp.split(z, [D_A, 2 * D_A, 3 * D_A, 3 * D_A + D_B], axis=-1)
    y_a = gate_b * short_conv3(gate_c * xa, conv_w)
    v = rms_norm(v, sgu_norm_g).reshape(bsz, n // CHUNK, CHUNK, B_GROUPS, D_B // B_GROUPS)
    sv = jnp.einsum('gpq,bcqgd->bcpgd', sgu_w, v) + sgu_b.T[:, :, None]
    y_b = u * sv.reshape(bsz, n, D_B)
    return jnp.concatenate([y_a, y_b], axis=-1) @ w_out

def fourier_mix(z):
    bsz, n, _ = z.shape
    zg = z.reshape(bsz, n, C_GROUPS, C_GW).astype(jnp.float32)
    f = jnp.fft.fft2(zg, axes=(1, 3)).real * (1.0 / math.sqrt(n * C_GW))
    return f.reshape(bsz, n, D_C).astype(z.dtype)

def odd_project(h, w_in, q_norm_g, w_uq, kv_norm_g):
    bsz, n, _ = h.shape
    z = h @ w_in
    zc, qc, kvc, k_pe = jnp.split(z, [D_C, D_C + Q_LORA, D_C + Q_LORA + KV_LORA], axis=-1)
    q = (rms_norm(qc, q_norm_g) @ w_uq).reshape(bsz, n, N_HEADS, QK_NOPE + QK_ROPE)
    return fourier_mix(zc), q[..., :QK_NOPE], q[..., QK_NOPE:], rms_norm(kvc, kv_norm_g), k_pe

def mla_expand(kv_c, w_ukv):
    bsz, n, _ = kv_c.shape
    kv = (kv_c @ w_ukv).reshape(bsz, n, N_HEADS, QK_NOPE + V_DIM)
    return kv[..., :QK_NOPE], kv[..., QK_NOPE:]

def mla_attend(q_nope, q_pe, k_nope, k_pe, v):
    bsz, nq = q_nope.shape[:2]
    nb = nq // Q_BLOCK
    scale = 1.0 / math.sqrt(QK_NOPE + QK_ROPE)

    def to_blocks(t):
        return jnp.moveaxis(t.reshape(bsz, nb, Q_BLOCK, *t.shape[2:]), 1, 0)

    def block(qs):
        qn, qp = qs
        s = jnp.einsum('bqhd,bkhd->bhqk', qn, k_nope) + jnp.einsum('bqhr,bkr->bhqk', qp, k_pe)
        p = jax.nn.softmax(s.astype(jnp.float32) * scale, axis=-1).astype(v.dtype)
        return jnp.einsum('bhqk,bkhd->bqhd', p, v)

    o = lax.map(block, (to_blocks(q_nope), to_blocks(q_pe)))
    return jnp.moveaxis(o, 0, 1).reshape(bsz, nq, N_HEADS * V_DIM)

def hier_moe(h, wg, bg, we, be, w1, w3, w2):
    g_logits = (jnp.einsum('bld,dg->blg', h, wg) + bg).astype(jnp.float32)
    g_prob = jax.nn.softmax(g_logits, axis=-1)
    g_idx = jnp.argmax(g_logits, axis=-1)
    g_w = jnp.take_along_axis(g_prob, g_idx[..., None], axis=-1)
    e_logits = jnp.einsum('bld,dge->blge', h, we) + be
    e_sel = jnp.take_along_axis(e_logits, g_idx[..., None, None], axis=2)[..., 0, :].astype(jnp.float32)
    top_v, top_i = lax.top_k(e_sel, TOP_K)
    w_k = jax.nn.softmax(top_v, axis=-1) * g_w
    e_idx = g_idx[..., None] * EXPERTS_PER_GROUP + top_i
    gates = jnp.sum(jax.nn.one_hot(e_idx, N_EXPERTS, dtype=jnp.float32) * w_k[..., None], axis=-2).astype(h.dtype)
    hid = jax.nn.silu(jnp.einsum('bld,edf->blef', h, w1)) * jnp.einsum('bld,edf->blef', h, w3)
    return jnp.einsum('blef,efd->bld', hid * gates[..., None], w2)

def setup_inputs(seed: int = 0) -> dict:
    key = jax.random.key(seed)
    ks = jax.random.split(key, 32)

    def nrm(k, shape, scale):
        return jax.random.normal(k, shape, jnp.float32) * scale

    d = D_MODEL
    return {
        "x_prompt": nrm(ks[0], (BATCH, SEQ, d), 1.0),
        "x_sample": nrm(ks[1], (DEC_BATCH, DEC_SEQ, d), 1.0),
        "cache_ckv": nrm(ks[2], (DEC_BATCH, N_ODD, PAST_LEN, KV_LORA), 1.0),
        "cache_kpe": nrm(ks[3], (DEC_BATCH, N_ODD, PAST_LEN, QK_ROPE), 1.0),
        "c": nrm(ks[4], (DEC_BATCH, d), 1.0),
        "c_ctx": nrm(ks[5], (d,), 1.0),
        "mod_w": nrm(ks[6], (DEPTH, d, 6 * d), MOD_SCALE * d ** -0.5),
        "mod_b": nrm(ks[7], (DEPTH, 6 * d), 0.02),
        "norm1_g": 1.0 + nrm(ks[8], (DEPTH, d), 0.02),
        "norm2_g": 1.0 + nrm(ks[9], (DEPTH, d), 0.02),
        "ev_w_in": nrm(ks[10], (N_EVEN, d, D_EVEN_IN), d ** -0.5),
        "ev_conv_w": nrm(ks[11], (N_EVEN, 3, D_A), 3 ** -0.5),
        "ev_sgu_norm_g": 1.0 + nrm(ks[12], (N_EVEN, D_B), 0.02),
        "ev_sgu_w": nrm(ks[13], (N_EVEN, B_GROUPS, CHUNK, CHUNK), CHUNK ** -0.5),
        "ev_sgu_b": 1.0 + nrm(ks[14], (N_EVEN, B_GROUPS, CHUNK), 0.02),
        "ev_w_out": nrm(ks[15], (N_EVEN, D_A + D_B, d), (D_A + D_B) ** -0.5),
        "od_w_in": nrm(ks[16], (N_ODD, d, D_ODD_IN), d ** -0.5),
        "od_q_norm_g": 1.0 + nrm(ks[17], (N_ODD, Q_LORA), 0.02),
        "od_w_uq": nrm(ks[18], (N_ODD, Q_LORA, N_HEADS * (QK_NOPE + QK_ROPE)), Q_LORA ** -0.5),
        "od_kv_norm_g": 1.0 + nrm(ks[19], (N_ODD, KV_LORA), 0.02),
        "od_w_ukv": nrm(ks[20], (N_ODD, KV_LORA, N_HEADS * (QK_NOPE + V_DIM)), KV_LORA ** -0.5),
        "od_w_out": nrm(ks[21], (N_ODD, D_C + N_HEADS * V_DIM, d), (D_C + N_HEADS * V_DIM) ** -0.5),
        "moe_wg": nrm(ks[22], (DEPTH, d, N_GROUPS_MOE), d ** -0.5),
        "moe_bg": nrm(ks[23], (DEPTH, N_GROUPS_MOE), 0.01),
        "moe_we": nrm(ks[24], (DEPTH, d, N_GROUPS_MOE, EXPERTS_PER_GROUP), d ** -0.5),
        "moe_be": nrm(ks[25], (DEPTH, N_GROUPS_MOE, EXPERTS_PER_GROUP), 0.01),
        "moe_w1": nrm(ks[26], (DEPTH, N_EXPERTS, d, D_EXPERT), d ** -0.5),
        "moe_w3": nrm(ks[27], (DEPTH, N_EXPERTS, d, D_EXPERT), d ** -0.5),
        "moe_w2": nrm(ks[28], (DEPTH, N_EXPERTS, D_EXPERT, d), D_EXPERT ** -0.5),
        "final_norm_g": 1.0 + nrm(ks[29], (d,), 0.02),
    }

def reference(x_prompt, x_sample, cache_ckv, cache_kpe, c, c_ctx, mod_w, mod_b, norm1_g, norm2_g,
              ev_w_in, ev_conv_w, ev_sgu_norm_g, ev_sgu_w, ev_sgu_b, ev_w_out,
              od_w_in, od_q_norm_g, od_w_uq, od_kv_norm_g, od_w_ukv, od_w_out,
              moe_wg, moe_bg, moe_we, moe_be, moe_w1, moe_w3, moe_w2, final_norm_g):
    xp, xs = x_prompt, x_sample
    bp, n_p, _ = xp.shape
    bs, n_s, _ = xs.shape
    row, col = grid_positions(n_s)
    new_ckv, new_kpe = [], []
    for l in range(DEPTH):
        j = l // 2
        sh1p, sc1p, ga1p, sh2p, sc2p, ga2p = adaln_params(c_ctx[None, :], mod_w[l], mod_b[l])
        sh1s, sc1s, ga1s, sh2s, sc2s, ga2s = adaln_params(c, mod_w[l], mod_b[l])
        hp = rms_norm(xp, norm1_g[l]) * (1.0 + sc1p) + sh1p
        hs = rms_norm(xs, norm1_g[l]) * (1.0 + sc1s) + sh1s
        if l % 2 == 0:
            op = even_mixer(hp, ev_w_in[j], ev_conv_w[j], ev_sgu_norm_g[j], ev_sgu_w[j], ev_sgu_b[j], ev_w_out[j])
            os_ = even_mixer(hs, ev_w_in[j], ev_conv_w[j], ev_sgu_norm_g[j], ev_sgu_w[j], ev_sgu_b[j], ev_w_out[j])
        else:
            fp, qn_p, qp_p, kvc_p, kpe_p = odd_project(hp, od_w_in[j], od_q_norm_g[j], od_w_uq[j], od_kv_norm_g[j])
            kn_p, v_p = mla_expand(kvc_p, od_w_ukv[j])
            ap = mla_attend(qn_p, qp_p, kn_p, kpe_p, v_p)
            op = jnp.concatenate([fp, ap], axis=-1) @ od_w_out[j]
            new_ckv.append(kvc_p)
            new_kpe.append(kpe_p)
            fs, qn_s, qp_s, kvc_s, kpe_s = odd_project(hs, od_w_in[j], od_q_norm_g[j], od_w_uq[j], od_kv_norm_g[j])
            qp_s = axial_rope(qp_s, row, col)
            kpe_s = axial_rope(kpe_s, row, col)
            kvc_all = jnp.concatenate([cache_ckv[:, j], kvc_s], axis=1)
            kpe_all = jnp.concatenate([cache_kpe[:, j], kpe_s], axis=1)
            kn_s, v_s = mla_expand(kvc_all, od_w_ukv[j])
            a_s = mla_attend(qn_s, qp_s, kn_s, kpe_all, v_s)
            os_ = jnp.concatenate([fs, a_s], axis=-1) @ od_w_out[j]
        xp = xp + ga1p * op
        xs = xs + ga1s * os_
        hp = rms_norm(xp, norm2_g[l]) * (1.0 + sc2p) + sh2p
        hs = rms_norm(xs, norm2_g[l]) * (1.0 + sc2s) + sh2s
        xp = xp + ga2p * hier_moe(hp, moe_wg[l], moe_bg[l], moe_we[l], moe_be[l], moe_w1[l], moe_w3[l], moe_w2[l])
        xs = xs + ga2s * hier_moe(hs, moe_wg[l], moe_bg[l], moe_we[l], moe_be[l], moe_w1[l], moe_w3[l], moe_w2[l])
    y_prompt = rms_norm(xp, final_norm_g)
    y_sample = rms_norm(xs, final_norm_g)
    new_ckv_arr = jnp.stack(new_ckv, axis=1)
    new_kpe_arr = jnp.stack(new_kpe, axis=1)
    return (y_prompt, y_sample, new_ckv_arr, new_kpe_arr)


_drawn_inputs = setup_inputs


def setup_inputs(seed=0):
    import zlib

    import numpy as np

    out = dict(_drawn_inputs(seed))
    spreads = {}
    factors = {'cache_ckv': 4.219,
     'cache_kpe': 7.967,
     'norm2_g': 3.734,
     'ev_sgu_norm_g': 5.27,
     'ev_sgu_b': 8.0,
     'od_q_norm_g': 8.0,
     'od_kv_norm_g': 7.738,
     'moe_bg': 6.46,
     'moe_be': 7.085,
     'final_norm_g': 8.443}
    for name, (base, spread) in spreads.items():
        noise = np.random.default_rng([zlib.crc32(name.encode()), seed]).standard_normal(out[name].shape)
        drawn = base * np.exp(spread * noise) if base else spread * noise
        out[name] = __import__('jax').numpy.asarray(drawn.astype(out[name].dtype))
    for name, factor in factors.items():
        out[name] = (out[name] * factor).astype(out[name].dtype)
    return out
```

```python
from contextlib import ExitStack

import concourse.bass as bass
from concourse import mybir

F32 = mybir.dt.float32
ALU = mybir.AluOpType
ACT = mybir.ActivationFunctionType
AX = mybir.AxisListType.X

P = 128
D = 1024
DC = D // P
TILES = 3
T = TILES * P
GRID_W = 64
EPS = 1e-6
NH, NOPE, ROPE, VD = 12, 64, 32, 64
QH = NOPE + ROPE
QL, KVL, DCF = 384, 256, 256
Z_Q, Z_KV, Z_PE, Z_END = DCF, DCF + QL, DCF + QL + KVL, DCF + QL + KVL + ROPE
NE, NG, EPG, DE = 16, 4, 4, 256
SLOT = 2048
NSLOT = 12
UNROLL = 4
TURNS = NE // UNROLL
SCALE = float(QH) ** -0.5
NEG = -3.0e38

C_ID, C_CS1, C_CS2, C_CC, C_COS, C_SIN, C_FIRST, C_END = 0, 128, 384, 1408, 1664, 1696, 1728, 1732


def cond_of(tile):
    return 0 if tile == 0 else 1


def program(nc, x_prompt, x_sample, cache_ckv, cache_kpe, c, c_ctx, mod_w, mod_b, norm1_g, norm2_g,
            ev_w_in, ev_conv_w, ev_sgu_norm_g, ev_sgu_w, ev_sgu_b, ev_w_out, od_w_in, od_q_norm_g,
            od_w_uq, od_kv_norm_g, od_w_ukv, od_w_out, moe_wg, moe_bg, moe_we, moe_be, moe_w1,
            moe_w3, moe_w2, final_norm_g, consts, y_prompt, y_sample, new_ckv, new_kpe):
    with ExitStack() as ctx:
        def sb(name, shape):
            return ctx.enter_context(nc.sbuf_tensor(name, shape, F32))

        sems = {}

        def S(name):
            if name not in sems:
                sems[name] = ctx.enter_context(nc.semaphore(name))
            return sems[name]

        TIMES = dict(mod_mm=1, mod_row=1, mod_cmm=1, mod_col=1, norm_root=3, norm_xn=3, norm_tr=3, norm_hT_act=3,
                     norm_hT_dve=3, norm_cols=1, gate_rows=4, gate_rows_mm=4, out_mm=6, x1=3, x2=3, router_mm=1,
                     gdiff=1, gexp=1, ediff=1, eexp=1, up_mm=48, silu=48, hid=50, hid_tr=48, hidT=50, down_mm=48, acc=50)

        def L(k, name, n):
            return S(name), TIMES[name] * k + n

        RING = NSLOT * SLOT
        pool = sb("pool", [P, RING + 8192])
        SCR = RING
        x = sb("x", [P, TILES, D])
        hT = sb("hT", [P, DC, T])
        xn = sb("xn", [P, TILES, D])
        yT = sb("yT", [P, DC, T])
        mrow = [sb(f"mrow{l}", [P, 3, 512]) for l in range(2)]
        ga = sb("ga", [P, 2, D])
        cst = sb("cst", [P, C_END])
        condraw = sb("condraw", [P, 2, DC])
        cs32 = sb("cs32", [P, DC, 32])
        modcol = [sb(f"modcol{l}", [P, 3, DC, 2, 2]) for l in range(2)]
        scg = [sb(f"scg{l}", [P, 2, DC, 2]) for l in range(2)]
        gcol = sb("gcol", [P, 2, 2, DC])
        minus_half = sb("minus_half", [P, 1])
        ss = sb("ss", [P, 2 * TILES])
        rstd = sb("rstd", [P, 2 * TILES])
        convw = sb("convw", [P, 3, 4])
        sgug = sb("sgug", [P, 4])
        qg = sb("qg", [P, 3])
        wg = sb("wg", [P, 2, DC, NG])
        we = sb("we", [P, 2, DC, NE])
        rb = sb("rb", [P, 2, NG + NE])
        gates = sb("gates", [P, TILES, NE])
        rt = sb("rt", [P, 240])
        ps = ctx.enter_context(nc.psum_tensor("ps", [P, 8, 512], F32))

        ident = cst[:, C_ID:C_ID + P]

        def scratch(at, n, base=SCR):
            assert base + at + n <= RING + 8192
            return pool[:, base + at:base + at + n]

        vn = scratch(0, 1536).rearrange("p (t n) -> p t n", t=3)
        gcs = scratch(1536, 384)
        pr = scratch(1920, 384)
        cv = scratch(2304, 384)
        sguw = scratch(2688, 512).rearrange("p (g n) -> p g n", g=4)
        sguT = scratch(3200, 512).rearrange("p (g n) -> p g n", g=4)
        sgub = scratch(3712, 512).rearrange("p (g n) -> p g n", g=4)
        sv = scratch(4224, 384)
        OB = SCR - SLOT
        q = scratch(0, TILES * NH * QH, OB).rearrange("p (t n) -> p t n", t=3)
        z = scratch(3456, 3 * Z_END, OB).rearrange("p (t n) -> p t n", t=3)
        o = scratch(3456, 3 * NH * VD, OB).rearrange("p (t n) -> p t n", t=3)
        qT = scratch(6240, 2 * T, OB).rearrange("p (b n) -> p b n", b=2)
        kT = scratch(7008, 1024, OB).rearrange("p (b n) -> p b n", b=2)
        pr_s = scratch(8032, 896, OB)
        prT = scratch(8928, 896, OB)
        rtmp = scratch(8032, 768, OB).rearrange("p (k n) -> p k n", k=4)
        ckv = scratch(8928, 256, OB)
        kpe = scratch(9184, 4 * ROPE, OB).rearrange("p (t n) -> p t n", t=4)
        kvg = scratch(9904, KVL, OB)
        nmax = scratch(9824, 3, OB)
        psum_of = scratch(9828, 3, OB)
        pinv = scratch(9832, 3, OB)
        ktmp = scratch(9840, 64, OB).rearrange("p (k n) -> p k n", k=4)
        qnT = hT[:, 0:3, :]
        kvT = hT[:, 3:6, :].rearrange("p a b -> p (a b)")[:, 0:1024].rearrange("p (c n) -> p c n", c=2)
        fmid = [hT[:, :, :].rearrange("p a b -> p (a b)")[:, 2304:3072].rearrange("p (k n) -> p k n", k=2), qT]
        vv = xn[:, :, :].rearrange("p a b -> p (a b)").rearrange("p (t n) -> p t n", t=4)
        acc = scratch(0, 3072).rearrange("p (t n) -> p t n", t=3)
        sil = scratch(3072, 512).rearrange("p (b n) -> p b n", b=2)
        hid = scratch(3584, 512).rearrange("p (b n) -> p b n", b=2)
        hidT = scratch(4096, 512).rearrange("p (b c n) -> p b c n", b=2, c=2)
        finalg = scratch(6144, 1024)


        def scores(t):
            return (ps[:, 2, 0:P], ps[:, 2, P:512], ps[:, 3, 0:T])[t]

        def probs(t):
            return pr_s[:, (0, P, P + T)[t]:(P, P + T, P + 2 * T)[t]]

        R, at = {}, 0
        for name, n in (("logits", 20), ("gmax", 1), ("gdiff", 4), ("gexp", 4), ("cand", 4), ("cmax", 1), ("ghot", 4),
                        ("esel4", 16), ("esel", 4), ("top1", 1), ("hot1", 4), ("rest", 4), ("top2", 1), ("ediff", 1),
                        ("hot2", 4), ("eexp", 1), ("gsum", 1), ("den", 1), ("w1", 1), ("w2", 1)):
            R[name] = rt[:, at:at + TILES * n].rearrange("p (t n) -> p t n", t=TILES)
            at += TILES * n
        R["esel4"] = R["esel4"].rearrange("p t (g e) -> p t g e", g=NG)
        first = cst[:, C_FIRST:C_END].unsqueeze(1)

        landed, loads, owner, count, cursor = {}, [], {}, [0] * NSLOT, [0]

        def item(name, n, src, shape, used, limit=NSLOT):
            s0 = cursor[0] if cursor[0] + n <= limit else 0
            cursor[0] = s0 + n
            waits = {}
            for s in range(s0, s0 + n):
                if s in owner:
                    waits[owner[s][0]] = max(waits.get(owner[s][0], 0), owner[s][1])
                owner[s] = used
            count[s0] += 1
            landed[name] = (s0, 16 * count[s0])
            loads.append((s0, src, shape, waits))

        def mod_items(l, i, limit=NSLOT):
            for j in range(4):
                b = 4 * i + j
                item(f"mod{l}.{b}", 2, mod_w[l, :, b * 512:(b + 1) * 512].rearrange("(p c) n -> p c n", c=DC),
                     (DC, 512), ("mod_mm", 3 * l + i + 1), limit)

        def expert_places(l):
            waits, before = [owner.get(s) for s in range(NSLOT)], list(count)
            for s in range(NSLOT):
                count[s] += TURNS
                owner[s] = ("down_mm", TILES * NE * (l + 1))
            cursor[0] = 0
            return waits, before

        def weight(name, a, b):
            s0 = landed[name][0]
            return pool[:, s0 * SLOT:s0 * SLOT + a * b].rearrange("p (a b) -> p a b", a=a)

        mod_items(0, 0)
        for name, at, used in (("v", 2048, ("v_mm", 3)), ("gate_c", 512, ("conv_mm", 4)), ("xa", 1024, ("conv_mm", 4)),
                               ("gate_b", 0, ("conv_mm", 4)), ("u", 1536, ("sgu_mm", 4))):
            item(name, 2, ev_w_in[0, :, at:at + 512].rearrange("(p c) n -> p c n", c=DC), (DC, 512), used)
        mod_items(0, 1)
        item("out0.0", 2, ev_w_out[0, 0:512, :].rearrange("(p j) n -> p j n", j=4), (4, D), ("out_mm", 6))
        item("out0.1", 2, ev_w_out[0, 512:1024, :].rearrange("(g d) n -> d g n", g=4), (4, D), ("out_mm", 6))
        mod_items(0, 2)
        split = len(loads)
        places = [expert_places(0)]
        ODD = NSLOT - 1
        mod_items(1, 0, ODD)
        for i in range(2):
            item(f"in1.{i}", 2, od_w_in[0].rearrange("(p c) n -> p c n", c=DC)[:, 4 * i:4 * i + 4, :],
                 (4, Z_END), ("z_mm", 6), ODD)
        item("uq", 2, od_w_uq[0].rearrange("(p c) n -> p c n", c=3), (3, NH * QH), ("q_mm", 3), ODD)
        item("ukv", 2, od_w_ukv[0].rearrange("(p c) n -> p c n", c=2), (2, NH * 2 * VD), ("k_mm", NH), ODD)
        mod_items(1, 1, ODD)
        for i in range(2):
            item(f"out1.{i}", 2, od_w_out[0].rearrange("(k p) n -> p k n", p=P)[:, 4 * i:4 * i + 4, :],
                 (4, D), ("out_mm", 12), ODD)
        mod_items(1, 2, ODD)
        owner[NSLOT - 1] = ("qT_tr", NH)
        places.append(expert_places(1))

        def arrived(eng, name):
            s0, value = landed[name]
            eng.wait_ge(S(f"slot{s0}"), value)

        class Chain:

            def __init__(self, eng, name):
                self.eng, self.sem, self.n, self.turn, self.per = eng, S(name), 0, None, 0

            def link(self, ins):
                self.n += 1
                ins.then_inc(self.sem, 1)
                self.eng.wait_ge(self.sem, self.n if self.turn is None else self.turn * self.per + self.n)

            def loop(self, turn, per):
                self.turn, self.per, self.start = turn, per, self.n

            def end(self, turns):
                assert self.n - self.start == self.per
                self.n, self.turn = self.start + self.per * turns, None

        def norm_columns(l, w):
            i, v = ((0, 0), (1, 1))[w]
            return (lambda c, r: scg[l][:, w, c, r:r + 1]), (lambda c, r: modcol[l][:, i, c, v, r:r + 1])

        def bank2(b, n):
            return ps[:, b:b + 2, :].rearrange("p b n -> p (b n)")[:, 0:n]

        N_EARLY, N_LATE = 9, 17
        HT_ACT = 4
        STEPS = TILES * UNROLL
        block = ctx.enter_context(nc.Block())

        @block.sync
        def _(sp):
            def load(n):
                s0, src, (a, b), waits = loads[n]
                for k, v in waits.items():
                    sp.wait_ge(S(k), v)
                sp.dma_start(pool[:, s0 * SLOT:s0 * SLOT + a * b].rearrange("p (a b) -> p a b", a=a), src) \
                    .then_inc(S(f"slot{s0}"), 16)

            def expert_load(l, k, e, u):
                s, w = 3 * u + k, (moe_w1, moe_w3, moe_w2)[k]
                sp.dma_start(pool[:, s * SLOT:(s + 1) * SLOT],
                             w[l, bass.ds(e, 1)].rearrange("a (p c) n -> p (a c n)", p=P)).then_inc(S(f"slot{s}"), 16)

            def experts(l):
                waited = {}
                for s in range(NSLOT):
                    if places[l][0][s]:
                        k, v = places[l][0][s]
                        if waited.get(k, 0) < v:
                            sp.wait_ge(S(k), v)
                            waited[k] = v
                    expert_load(l, s % 3, s // 3, s // 3)
                with sp.Fori(1, TURNS) as i:
                    for u in range(UNROLL):
                        sp.wait_ge(*L(l, "up_mm", i * STEPS + (TILES * (u + 1) - STEPS)))
                        sp.nop()
                        expert_load(l, 0, i * UNROLL + u, u)
                        expert_load(l, 1, i * UNROLL + u, u)
                        sp.wait_ge(*L(l, "down_mm", i * STEPS + (TILES * (u + 1) - STEPS)))
                        sp.nop()
                        expert_load(l, 2, i * UNROLL + u, u)

            for n in range(split):
                load(n)
            experts(0)
            for n in range(split, len(loads)):
                load(n)
            experts(1)

        @block.gpsimd
        def _(gps):
            for l in range(2):
                nc.gpsimd.memset(mrow[l][:, :, :], 0.0).then_inc(S("rows_zero"), 1)
            nc.gpsimd.memset(cs32[:, :, :], 0.0).then_inc(S("cs32_zero"), 1)
            ch = Chain(gps, "gps_chain")
            ch.link(nc.gpsimd.memset(minus_half[:, :], -0.5))

            def root(name, n, at, width):
                gps.wait_ge(S(name + "_ss"), n)
                ch.link(nc.gpsimd.tensor_scalar(rstd[:, at:at + 1], ss[:, at:at + 1], 1.0 / width, EPS, ALU.mult, ALU.add))
                nc.gpsimd.tensor_tensor(rstd[:, at:at + 1], rstd[:, at:at + 1], minus_half[:, :], ALU.pow) \
                    .then_inc(S(name + "_root"), 1)

            for t in range(TILES):
                root("norm", t + 1, t, D)
            for t in range(TILES):
                root("v", t + 1, 3 + t, 512)
            for t in range(TILES):
                root("norm", TILES + t + 1, t, D)
            for t in range(TILES):
                root("norm", 2 * TILES + t + 1, t, D)
            for t in range(TILES):
                root("qc", t + 1, t, QL)
                root("kvc", t + 1, 3 + t, KVL)
            for t in range(TILES):
                root("norm", 3 * TILES + t + 1, t, D)
            for t in range(TILES):
                root("norm", 4 * TILES + t + 1, t, D)

        @block.scalar
        def _(act):
            a_ = nc.scalar
            ch = Chain(act, "act_chain")

            def row(src, n):
                return src.rearrange("(a n) -> a n", a=1).broadcast_to((P, n))

            early = [(x[:, 0, :], x_prompt[0]), (x[:, 1:3, :], x_sample[0].rearrange("(t p) d -> p t d", p=P)),
                     (condraw[:, 0, :], c_ctx.rearrange("(p c) -> p c", c=DC)),
                     (condraw[:, 1, :], c[0].rearrange("(p c) -> p c", c=DC)),
                     (cst[:, :], consts)]
            early += [(gcol[:, l, w, :], g[l].rearrange("(p c) -> p c", c=DC))
                      for l in range(2) for w, g in enumerate((norm1_g, norm2_g))]
            assert len(early) == N_EARLY
            for dst, src in early:
                act.dma_start(dst, src).then_inc(S("early"), 16)
            act.wait_ge(S("rows_zero"), 2)
            for l in range(2):
                for r in range(2):
                    for j in range(4):
                        act.dma_start(mrow[l][32 * j + r:32 * j + r + 1, :, :],
                                      mod_b[l].rearrange("(i j n) -> j i n", i=3, j=4)[j:j + 1]).then_inc(S("bias"), 16)
            late = [(convw[:, k, :], ev_conv_w[0, k].rearrange("(p j) -> p j", j=4)) for k in range(3)]
            late += [(sguw, ev_sgu_w[0].rearrange("g p q -> p g q")),
                     (sgub, row(ev_sgu_b[0].rearrange("g n -> (g n)"), 4 * P).rearrange("p (g n) -> p g n", g=4)),
                     (qg[:, :], od_q_norm_g[0].rearrange("(p c) -> p c", c=3)),
                     (kvg, row(od_kv_norm_g[0], KVL)), (ckv, cache_ckv[0, 0]), (kpe[:, 1, :], cache_kpe[0, 0])]
            for l in range(2):
                late += [(wg[:, l], moe_wg[l].rearrange("(p c) g -> p c g", c=DC)),
                         (we[:, l], moe_we[l].rearrange("(p c) g e -> p c (g e)", c=DC)),
                         (rb[:, l, 0:NG], row(moe_bg[l], NG)),
                         (rb[:, l, NG:], row(moe_be[l].rearrange("g e -> (g e)"), NE))]
            assert len(late) == N_LATE
            for dst, src in late:
                act.dma_start(dst, src).then_inc(S("late"), 16)
            for g in range(4):
                act.dma_start(sgug[:, g:g + 1], ev_sgu_norm_g[0].rearrange("(g d a) -> g d a", g=4, a=1)[g]) \
                    .then_inc(S("late"), 16)

            def squares(name, ready, dst, src, out):
                act.wait_ge(S(ready[0]), ready[1])
                a_.activation(dst, src, ACT.Square, accum_out=out).then_inc(S(name + "_ss"), 1)

            def norm_squares(ready, n):
                for t in range(TILES):
                    squares("norm", (ready, n if ready == "early" else n + t + 1), xn[:, t, :], x[:, t, :], ss[:, t:t + 1])

            def norm_evacuate(l, w):
                scale, shift = norm_columns(l, w)
                act.wait_ge(*L(2 * l + w, "norm_cols", 1))
                for t in range(TILES):
                    act.wait_ge(*L(2 * l + w, "norm_tr", t + 1))
                    for cc in range(HT_ACT):
                        ins = a_.activation(hT[:, cc, t * P:(t + 1) * P], bank2(2 * t, D)[:, cc * P:(cc + 1) * P],
                                            ACT.Identity, bias=shift(cc, cond_of(t)), scale=scale(cc, cond_of(t)))
                    ins.then_inc(S("norm_hT_act"), 1)

            def router_exps(l):
                act.wait_ge(*L(l, "gdiff", 1))
                a_.activation(R["gexp"], R["gdiff"], ACT.Exp).then_inc(S("gexp"), 1)
                act.wait_ge(*L(l, "ediff", 1))
                a_.activation(R["eexp"], R["ediff"], ACT.Exp).then_inc(S("eexp"), 1)

            def experts(l):
                def silu(n, b):
                    act.wait_ge(*L(l, "up_mm", n + 1))
                    a_.activation(sil[:, b, :], ps[:, b, 0:DE], ACT.Silu).then_inc(S("silu"), 1)

                def hidT_copy(n, b):
                    act.wait_ge(*L(l, "hid_tr", n + 1))
                    a_.activation(hidT[:, b], ps[:, 2 + b, 0:DE].rearrange("p (c n) -> p c n", c=2), ACT.Copy) \
                        .then_inc(S("hidT"), 1)

                act.wait_ge(*L(l, "eexp", 1))
                for _ in range(2):
                    act.sem_inc(S("hidT"), 1)
                with act.Fori(0, TURNS) as i:
                    for s in range(STEPS):
                        silu(i * STEPS + s, s % 2)
                        if s:
                            hidT_copy(i * STEPS + s - 1, (s - 1) % 2)
                    hidT_copy(i * STEPS + STEPS - 1, (STEPS - 1) % 2)

            def gate_rows(l, k):
                for n in range(4):
                    act.wait_ge(*L(2 * l + k, "gate_rows_mm", n + 1))
                    a_.activation(ga[:, n // 2, (n % 2) * 512:(n % 2 + 1) * 512], ps[:, 6 + n % 2, :], ACT.Copy) \
                        .then_inc(S("gate_rows"), 1)

            act.wait_ge(S("early"), 16 * N_EARLY)
            act.wait_ge(S("cs32_zero"), 1)
            a_.activation(cs32[:, :, 0:2], condraw[:, :, :].rearrange("p r c -> p c r"), ACT.Silu).then_inc(S("cs32"), 1)
            norm_squares("early", 16 * N_EARLY)
            norm_evacuate(0, 0)
            for t in range(TILES):
                squares("v", ("v_mm", t + 1), vn[:, t, :], ps[:, t, :], ss[:, 3 + t:4 + t])
            for j in range(4):
                act.wait_ge(S("conv_mm"), j + 1)
                if j:
                    act.wait_ge(S("gated"), j)
                a_.activation(gcs, ps[:, (3, 6)[j % 2], 0:T], ACT.Copy).then_inc(S("gate_c"), 1)
            act.wait_ge(S("sgu_tr"), 1)
            a_.activation(sguT, ps[:, 1, :].rearrange("p (g n) -> p g n", g=4), ACT.Copy).then_inc(S("sguT"), 1)
            gate_rows(0, 0)
            norm_squares("x1", 0)
            norm_evacuate(0, 1)
            router_exps(0)
            experts(0)
            gate_rows(0, 1)
            norm_squares("x2", 0)
            norm_evacuate(1, 0)
            for t in range(TILES):
                act.wait_ge(S("z_mm"), 2 * t + 2)
                ch.link(a_.activation(z[:, t, 512:Z_END], ps[:, 2 * t + 1, 0:Z_END - 512], ACT.Copy))
                act.sem_inc(S("z_high"), 1)
                squares("qc", ("z_low", t + 1), xn[:, t, 0:QL], z[:, t, Z_Q:Z_KV], ss[:, t:t + 1])
                squares("kvc", ("z_low", t + 1), xn[:, t, QL:QL + KVL], z[:, t, Z_KV:Z_PE], ss[:, 3 + t:4 + t])
            act.wait_ge(S("kvn"), 3)
            act.dma_start(new_ckv[0, 0], z[:, 0, Z_KV:Z_PE]).then_inc(S("new_kv"), 16)
            act.dma_start(new_kpe[0, 0], z[:, 0, Z_PE:Z_END]).then_inc(S("new_kv"), 16)
            for cc in range(3):
                act.wait_ge(S("qn_tr"), cc + 1)
                a_.activation(qnT[:, cc, :], ps[:, cc, 0:T], ACT.Copy, scale=qg[:, cc:cc + 1]).then_inc(S("qnT"), 1)
            for t in range(TILES):
                act.wait_ge(S("q_mm"), t + 1)
                for n, w in ((0, 512), (1, 512), (2, 128)):
                    ins = a_.activation(q[:, t, n * 512:n * 512 + w], ps[:, 3 * (t % 2) + n, 0:w], ACT.Copy)
                ins.then_inc(S("q_out"), 1)
            for h in range(NH):
                act.wait_ge(S("k_mm"), h + 1)
                a_.activation(kT[0:NOPE, h % 2, :], ps[0:NOPE, 0, :], ACT.Copy).then_inc(S("kT"), 1)
                act.wait_ge(S("nmax"), h + 1)
                for t in range(TILES):
                    s_ap, p_ap = scores(t), probs(t)
                    ins = a_.activation(p_ap, s_ap, ACT.Exp, bias=nmax[:, t:t + 1], scale=SCALE,
                                        accum_out=psum_of[:, t:t + 1])
                ins.then_inc(S("probs"), 1)
            gate_rows(1, 0)
            norm_squares("x1", TILES)
            norm_evacuate(1, 1)
            router_exps(1)
            experts(1)
            act.dma_start(finalg, row(final_norm_g, D)).then_inc(S("finalg"), 16)
            gate_rows(1, 1)
            norm_squares("x2", TILES)
            for t in range(TILES):
                act.wait_ge(S("y"), t + 1)
                act.dma_start(y_prompt[0] if t == 0 else y_sample[0, (t - 1) * P:t * P, :], xn[:, t, :]) \
                    .then_inc(S("stored"), 16)
            act.wait_ge(S("new_kv"), 32)
            act.wait_ge(S("stored"), 48)

        @block.vector
        def _(dve):
            v_ = nc.vector
            ch = Chain(dve, "dve_chain")
            link = ch.link

            def mod_round(l, i):
                dve.wait_ge(*L(3 * l + i, "mod_mm", 1))
                if l == 0 and i == 0:
                    dve.wait_ge(S("bias"), 16 * 16)
                v_.tensor_tensor(mrow[l][:, i, :], ps[:, 7, :], mrow[l][:, i, :], ALU.add).then_inc(S("mod_row"), 1)
                dve.wait_ge(*L(3 * l + i, "mod_cmm", 1))
                link(v_.tensor_copy(modcol[l][:, i].rearrange("p c v r -> p (c v r)"), ps[:, 6, 0:4 * DC]))
                dve.sem_inc(S("mod_col"), 1)
                if i != 1:
                    w, v = ((0, 1), None, (1, 0))[i]
                    v_.scalar_tensor_tensor(scg[l][:, w], modcol[l][:, i, :, v, :], 1.0,
                                            gcol[:, l, w, :].unsqueeze(2).broadcast_to((P, DC, 2)), ALU.add, ALU.mult) \
                        .then_inc(S("norm_cols"), 1)

            def normalise(k):
                for t in range(TILES):
                    dve.wait_ge(*L(k, "norm_root", t + 1))
                    v_.tensor_scalar(xn[:, t, :], x[:, t, :], rstd[:, t:t + 1], None, ALU.mult).then_inc(S("norm_xn"), 1)

            def norm_evacuate(l, w):
                scale, shift = norm_columns(l, w)
                dve.wait_ge(*L(2 * l + w, "norm_cols", 1))
                for t in range(TILES):
                    dve.wait_ge(*L(2 * l + w, "norm_tr", t + 1))
                    for cc in range(HT_ACT, DC):
                        ins = v_.tensor_scalar(hT[:, cc, t * P:(t + 1) * P], bank2(2 * t, D)[:, cc * P:(cc + 1) * P],
                                               scale(cc, cond_of(t)), shift(cc, cond_of(t)), ALU.mult, ALU.add)
                    ins.then_inc(S("norm_hT_dve"), 1)

            def project_out(l):
                dve.wait_ge(*L(2 * l + 0, "gate_rows", 4))
                for t in range(TILES):
                    for n in range(2):
                        dve.wait_ge(*L(l, "out_mm", 2 * t + n + 1))
                        link(v_.tensor_tensor(xn[:, t, n * 512:n * 512 + 512], ps[:, 2 * t + n, :],
                                              ga[:, cond_of(t), n * 512:n * 512 + 512], ALU.mult))
                    v_.tensor_tensor(x[:, t, :], x[:, t, :], xn[:, t, :], ALU.add).then_inc(S("x1"), 1)

            def first_of(dst, values, top):
                b = (P, TILES, 4)
                link(v_.tensor_tensor(R["cand"], values, top.broadcast_to(b), ALU.is_equal))
                link(v_.tensor_tensor(R["cand"], R["cand"], first.broadcast_to(b), ALU.mult))
                link(v_.tensor_reduce(R["cmax"], R["cand"], AX, ALU.max))
                link(v_.tensor_tensor(dst, R["cand"], R["cmax"].broadcast_to(b), ALU.is_equal))

            def router(l):
                b, b44 = (P, TILES, 4), (P, TILES, 4, 4)
                dve.wait_ge(*L(l, "router_mm", 1))
                link(v_.tensor_tensor(R["logits"], ps[:, 6, 0:TILES * 20].rearrange("p (t n) -> p t n", t=TILES),
                                      rb[:, l, :].unsqueeze(1).broadcast_to((P, TILES, 20)), ALU.add))
                glog, elog = R["logits"][:, :, 0:NG], R["logits"][:, :, NG:].rearrange("p t (g e) -> p t g e", g=NG)
                link(v_.tensor_reduce(R["gmax"], glog, AX, ALU.max))
                v_.tensor_tensor(R["gdiff"], glog, R["gmax"].broadcast_to(b), ALU.subtract).then_inc(S("gdiff"), 1)
                first_of(R["ghot"], glog, R["gmax"])
                link(v_.tensor_tensor(R["esel4"], elog, R["ghot"].unsqueeze(3).broadcast_to(b44), ALU.mult))
                link(v_.tensor_reduce(R["esel"], R["esel4"].rearrange("p t g e -> p t e g"), AX, ALU.add))
                link(v_.tensor_reduce(R["top1"], R["esel"], AX, ALU.max))
                first_of(R["hot1"], R["esel"], R["top1"])
                link(v_.scalar_tensor_tensor(R["rest"], R["hot1"], NEG, R["esel"], ALU.mult, ALU.add))
                link(v_.tensor_reduce(R["top2"], R["rest"], AX, ALU.max))
                v_.tensor_tensor(R["ediff"], R["top2"], R["top1"], ALU.subtract).then_inc(S("ediff"), 1)
                first_of(R["hot2"], R["rest"], R["top2"])
                dve.wait_ge(*L(l, "gexp", 1))
                link(v_.tensor_reduce(R["gsum"], R["gexp"], AX, ALU.add))
                dve.wait_ge(*L(l, "eexp", 1))
                link(v_.scalar_tensor_tensor(R["den"], R["eexp"], 1.0, R["gsum"], ALU.add, ALU.mult))
                link(v_.reciprocal(R["w1"], R["den"]))
                link(v_.tensor_tensor(R["w2"], R["w1"], R["eexp"], ALU.mult))
                link(v_.tensor_tensor(R["hot1"], R["hot1"], R["w1"].broadcast_to(b), ALU.mult))
                link(v_.tensor_tensor(R["hot2"], R["hot2"], R["w2"].broadcast_to(b), ALU.mult))
                link(v_.tensor_tensor(R["hot1"], R["hot1"], R["hot2"], ALU.add))
                link(v_.tensor_tensor(gates[:, :, :].rearrange("p t (g e) -> p t g e", g=NG),
                                      R["ghot"].unsqueeze(3).broadcast_to(b44),
                                      R["hot1"].unsqueeze(2).broadcast_to(b44), ALU.mult))

            def experts(l):
                link(v_.memset(acc, 0.0))
                for _ in range(2):
                    dve.sem_inc(S("hid"), 1)
                    dve.sem_inc(S("acc"), 1)

                def gated_hidden(n, e, t, b):
                    dve.wait_ge(*L(l, "silu", n + 1))
                    v_.scalar_tensor_tensor(hid[:, b, :], ps[:, b, DE:2 * DE], gates[:, t, bass.ds(e, 1)], sil[:, b, :],
                                            ALU.mult, ALU.mult).then_inc(S("hid"), 1)

                def accumulate(n, t, b):
                    dve.wait_ge(*L(l, "down_mm", n + 1))
                    v_.tensor_tensor(acc[:, t, :], bank2(4 + 2 * b, D), acc[:, t, :], ALU.add).then_inc(S("acc"), 1)

                with dve.Fori(0, TURNS) as i:
                    for s in range(STEPS):
                        gated_hidden(i * STEPS + s, i * UNROLL + s // TILES, s % TILES, s % 2)
                        if s >= 2:
                            accumulate(i * STEPS + s - 2, (s - 2) % TILES, s % 2)
                    for s in (STEPS - 2, STEPS - 1):
                        accumulate(i * STEPS + s, s % TILES, s % 2)

            def experts_out(l):
                dve.wait_ge(*L(2 * l + 1, "gate_rows", 4))
                for t in range(TILES):
                    link(v_.tensor_tensor(acc[:, t, :], acc[:, t, :], ga[:, cond_of(t), :], ALU.mult))
                    v_.tensor_tensor(x[:, t, :], x[:, t, :], acc[:, t, :], ALU.add).then_inc(S("x2"), 1)

            dve.wait_ge(S("early"), 16 * N_EARLY)
            normalise(0)
            mod_round(0, 0)
            norm_evacuate(0, 0)
            for t in range(TILES):
                dve.wait_ge(S("v_root"), t + 1)
                v_.tensor_scalar(vn[:, t, :], ps[:, t, :], rstd[:, 3 + t:4 + t], None, ALU.mult).then_inc(S("vn"), 1)
            dve.wait_ge(S("late"), 16 * (N_LATE + 4))
            for j in range(4):
                b = (3, 6)[j % 2]
                b1, b2 = b + 1, (b + 2) % 8
                dve.wait_ge(S("gate_c"), j + 1)
                ins = v_.tensor_tensor(pr, gcs, ps[:, b1, 0:T], ALU.mult)
                link(ins)
                dve.sem_inc(S("gated"), 1)
                link(v_.tensor_scalar(cv, pr, convw[:, 1, j:j + 1], None, ALU.mult))
                for a, n in ((0, P), (P, 2 * P)):
                    link(v_.scalar_tensor_tensor(cv[:, a + 1:a + n], pr[:, a:a + n - 1], convw[:, 0, j:j + 1],
                                                 cv[:, a + 1:a + n], ALU.mult, ALU.add))
                    link(v_.scalar_tensor_tensor(cv[:, a:a + n - 1], pr[:, a + 1:a + n], convw[:, 2, j:j + 1],
                                                 cv[:, a:a + n - 1], ALU.mult, ALU.add))
                v_.tensor_tensor(yT[:, j, :], cv, ps[:, b2, 0:T], ALU.mult).then_inc(S("y_conv"), 1)
            for g in range(4):
                dve.wait_ge(S("sgu_mm"), g + 1)
                link(v_.scalar_tensor_tensor(sv.rearrange("p (t n) -> p t n", t=TILES),
                                             ps[:, (1, 4)[g % 2], 0:T].rearrange("p (t n) -> p t n", t=TILES),
                                             sgug[:, g:g + 1], sgub[:, g, :].unsqueeze(1).broadcast_to((P, TILES, P)),
                                             ALU.mult, ALU.add))
                link(v_.tensor_tensor(yT[:, 4 + g, :], sv, ps[:, (2, 3)[g % 2], 0:T], ALU.mult))
                dve.sem_inc(S("y_sgu"), 1)
            mod_round(0, 1)
            project_out(0)
            mod_round(0, 2)
            normalise(1)
            norm_evacuate(0, 1)
            router(0)
            experts(0)
            experts_out(0)
            mod_round(1, 0)
            normalise(2)
            norm_evacuate(1, 0)

            for t in range(TILES):
                dve.wait_ge(S("z_mm"), 2 * t + 1)
                v_.tensor_copy(z[:, t, 0:512], ps[:, 2 * t, :]).then_inc(S("z_low"), 1)
            for t in range(TILES):
                dve.wait_ge(S("qc_root"), t + 1)
                v_.tensor_scalar(z[:, t, Z_Q:Z_KV], z[:, t, Z_Q:Z_KV], rstd[:, t:t + 1], None, ALU.mult).then_inc(S("qn"), 1)
                dve.wait_ge(S("kvc_root"), t + 1)
                v_.scalar_tensor_tensor(z[:, t, Z_KV:Z_PE], z[:, t, Z_KV:Z_PE], rstd[:, 3 + t:4 + t], kvg, ALU.mult, ALU.mult) \
                    .then_inc(S("kvn"), 1)

            def rotate(dst, src, t, tmp):
                shape = tuple(src.shape[:-2]) + (8,)
                cos = cst[:, C_COS + 16 * (t - 1):C_COS + 16 * t].rearrange("p (k n) -> p k n", k=2)
                sin = cst[:, C_SIN + 16 * (t - 1):C_SIN + 16 * t].rearrange("p (k n) -> p k n", k=2)
                if len(shape) == 4:
                    cos, sin = cos.unsqueeze(1).broadcast_to(shape), sin.unsqueeze(1).broadcast_to(shape)
                    first_half, second_half = src[:, :, :, 0, :], src[:, :, :, 1, :]
                    out1, out2 = dst[:, :, :, 0, :], dst[:, :, :, 1, :]
                else:
                    first_half, second_half, out1, out2 = src[:, :, 0, :], src[:, :, 1, :], dst[:, :, 0, :], dst[:, :, 1, :]
                v_.tensor_tensor(tmp[0], first_half, cos, ALU.mult)
                v_.tensor_tensor(tmp[1], second_half, sin, ALU.mult)
                v_.tensor_tensor(tmp[2], second_half, cos, ALU.mult)
                link(v_.tensor_tensor(tmp[3], first_half, sin, ALU.mult))
                v_.tensor_tensor(out1, tmp[0], tmp[1], ALU.subtract)
                link(v_.tensor_tensor(out2, tmp[2], tmp[3], ALU.add))

            dve.wait_ge(S("z_high"), 3)
            link(v_.tensor_copy(kpe[:, 0, :], z[:, 0, Z_PE:Z_END]))
            for t in (1, 2):
                rotate(kpe[:, t + 1, :].rearrange("p (k a n) -> p k a n", k=2, a=2),
                       z[:, t, Z_PE:Z_END].rearrange("p (k a n) -> p k a n", k=2, a=2), t,
                       [ktmp[:, k, :].rearrange("p (k n) -> p k n", k=2) for k in range(4)])
            dve.sem_inc(S("kpe"), 1)
            for j in range(2):
                dve.wait_ge(S("four_tok_mm"), j + 1)
                b = (6, 4)[j]
                v_.tensor_copy(fmid[j][:, :, 0:P], ps[:, b, 0:2 * P].rearrange("p (k n) -> p k n", k=2))
                v_.tensor_copy(fmid[j][:, :, P:T], ps[:, b + 1, :].rearrange("p (k n) -> p k n", k=2)) \
                    .then_inc(S("fmid"), 1)
            for cc in range(2):
                dve.wait_ge(S("kv_tr"), cc + 1)
                v_.tensor_copy(kvT[:, cc, :], ps[:, 3 + cc, :]).then_inc(S("kvT"), 1)
            dve.wait_ge(S("kpe_tr"), 1)
            dve.wait_ge(S("four_mm"), 1)
            for b in range(2):
                ins = v_.tensor_copy(kT[NOPE:QH, b, :], ps[NOPE:QH, 5, :])
            ins.then_inc(S("kpeT"), 1)
            for j in range(2):
                ins = v_.tensor_copy(yT[:, j, :], ps[:, 6 + j, 0:T])
            ins.then_inc(S("y_four"), 1)
            for t in (1, 2):
                dve.wait_ge(S("q_out"), t + 1)
                qpe = q[:, t, :].rearrange("p (h n) -> p h n", h=NH)[:, :, NOPE:QH].rearrange("p h (k a n) -> p h k a n", k=2, a=2)
                for k in range(2):
                    cos = cst[:, C_COS + 16 * (t - 1) + 8 * k:C_COS + 16 * (t - 1) + 8 * k + 8].unsqueeze(1).broadcast_to((P, NH, 8))
                    sin = cst[:, C_SIN + 16 * (t - 1) + 8 * k:C_SIN + 16 * (t - 1) + 8 * k + 8].unsqueeze(1).broadcast_to((P, NH, 8))
                    one, two = qpe[:, :, k, 0, :], qpe[:, :, k, 1, :]
                    tmp = [rtmp[:, m, 0:96].rearrange("p (h n) -> p h n", h=NH) for m in range(4)]
                    v_.tensor_tensor(tmp[0], one, cos, ALU.mult)
                    v_.tensor_tensor(tmp[1], two, sin, ALU.mult)
                    v_.tensor_tensor(tmp[2], two, cos, ALU.mult)
                    link(v_.tensor_tensor(tmp[3], one, sin, ALU.mult))
                    v_.tensor_tensor(one, tmp[0], tmp[1], ALU.subtract)
                    link(v_.tensor_tensor(two, tmp[2], tmp[3], ALU.add))
            dve.sem_inc(S("q_rot"), 1)
            for kt in range(4):
                dve.wait_ge(S("v2_mm"), kt + 1)
                v_.tensor_copy(vv[:, kt, :], bank2((6, 3)[kt % 2], NH * VD)).then_inc(S("vv"), 1)

            def head_probs_out(h):
                dve.wait_ge(S("probs"), h + 1)
                if h:
                    dve.wait_ge(S("o_out"), h)
                v_.reciprocal(pinv, psum_of)
                dve.wait_ge(S("p_tr"), h + 1)
                v_.tensor_copy(prT, bank2(4, 7 * P)).then_inc(S("pT"), 1)

            def head_out(h):
                dve.wait_ge(S("o_mm"), h + 1)
                v_.tensor_tensor(o[:, :, h * VD:(h + 1) * VD], ps[:, 6 + h % 2, 0:3 * VD].rearrange("p (t n) -> p t n", t=3),
                                 pinv.unsqueeze(2).broadcast_to((P, 3, VD)), ALU.mult).then_inc(S("o_out"), 1)

            dve.wait_ge(S("new_kv"), 32)
            for h in range(NH):
                dve.wait_ge(S("qT_tr"), h + 1)
                v_.tensor_copy(qT[0:QH, h % 2, :], ps[0:QH, 1, 0:T]).then_inc(S("qT"), 1)
                if h:
                    head_probs_out(h - 1)
                dve.wait_ge(S("s_mm"), h + 1)
                for t in range(TILES):
                    ins = v_.tensor_reduce(nmax[:, t:t + 1], scores(t), AX, ALU.max)
                link(ins)
                v_.tensor_scalar(nmax, nmax, -SCALE, None, ALU.mult).then_inc(S("nmax"), 1)
                if h:
                    head_out(h - 1)
            head_probs_out(NH - 1)
            head_out(NH - 1)
            mod_round(1, 1)
            for t in range(TILES):
                dve.wait_ge(S("o_tr"), t + 1)
                v_.tensor_copy(yT[:, 2:DC, t * P:(t + 1) * P], bank2(2 * t, 6 * P).rearrange("p (k n) -> p k n", k=6)) \
                    .then_inc(S("y_att"), 1)
            project_out(1)
            mod_round(1, 2)
            normalise(3)
            norm_evacuate(1, 1)
            router(1)
            experts(1)
            experts_out(1)
            dve.wait_ge(S("finalg"), 16)
            for t in range(TILES):
                dve.wait_ge(*L(4, "norm_root", t + 1))
                v_.scalar_tensor_tensor(xn[:, t, :], x[:, t, :], rstd[:, t:t + 1], finalg, ALU.mult, ALU.mult) \
                    .then_inc(S("y"), 1)

        @block.tensor
        def _(pe):
            mm, tr = nc.tensor.matmul, nc.tensor.transpose

            def mod_round(l, i):
                for j in range(4):
                    arrived(pe, f"mod{l}.{4 * i + j}")
                w = [weight(f"mod{l}.{4 * i + j}", DC, 512) for j in range(4)]
                for cc in range(DC):
                    for j in range(4):
                        ins = mm(ps[32 * j:32 * j + 32, 7, :], cs32[:, cc, :], w[j][:, cc, :], start=cc == 0, stop=cc == DC - 1)
                ins.then_inc(S("mod_mm"), 1)
                pe.wait_ge(*L(3 * l + i, "mod_row", 1))
                pick = ident.rearrange("p (v h a) -> p h v a", v=2, h=2)
                for cc in range(DC):
                    for h in range(2):
                        ins = mm(ps[64 * h:64 * h + 64, 6, 4 * cc:4 * cc + 4], mrow[l][:, i, cc::DC], pick[:, h, :, 0:2],
                                 start=True, stop=True)
                ins.then_inc(S("mod_cmm"), 1)

            def norm_transposes(l, w):
                for t in range(TILES):
                    pe.wait_ge(*L(2 * l + w, "norm_xn", t + 1))
                    for cc in range(DC):
                        ins = tr(bank2(2 * t, D)[:, cc * P:(cc + 1) * P], xn[:, t, cc::DC], ident)
                    ins.then_inc(S("norm_tr"), 1)

            def wait_hT(l, w, n=TILES):
                pe.wait_ge(*L(2 * l + w, "norm_hT_act", n))
                pe.wait_ge(*L(2 * l + w, "norm_hT_dve", n))

            def gate_rows(l, k):
                i, v = ((1, 0), (2, 1))[k]
                for n in range(4):
                    r, half = n // 2, n % 2
                    if n >= 2:
                        pe.wait_ge(*L(2 * l + k, "gate_rows", n - 1))
                    at = 64 * v + 32 * half + r
                    mm(ps[:, 6 + n % 2, :], ident[:, at:at + 1].broadcast_to((P, P)), mrow[l][:, i, :], start=True, stop=True) \
                        .then_inc(S("gate_rows_mm"), 1)

            def project_out(l, parts):
                for t in range(TILES):
                    for n in range(2):
                        for k in range(DC):
                            ins = mm(ps[:, 2 * t + n, :], yT[:, k, t * P:(t + 1) * P],
                                     weight(parts[k // 4], 4, D)[:, k % 4, n * 512:n * 512 + 512], start=k == 0, stop=k == DC - 1)
                        ins.then_inc(S("out_mm"), 1)

            def router(l):
                pe.wait_ge(S("late"), 16 * (N_LATE + 4))
                wait_hT(l, 1)
                for t in range(TILES):
                    for at, w, n in ((0, wg, NG), (NG, we, NE)):
                        for cc in range(DC):
                            ins = mm(ps[:, 6, 20 * t + at:20 * t + at + n], hT[:, cc, t * P:(t + 1) * P], w[:, l, cc, :],
                                     start=cc == 0, stop=cc == DC - 1)
                ins.then_inc(S("router_mm"), 1)

            def experts(l):
                before = places[l][1]

                def arrived_expert(i, s):
                    pe.wait_ge(S(f"slot{s}"), i * 16 + 16 * (before[s] + 1))

                def up(i, s):
                    u, t, b = s // TILES, s % TILES, s % 2
                    if t == 0:
                        arrived_expert(i, 3 * u)
                        arrived_expert(i, 3 * u + 1)
                    w13 = pool[:, 3 * u * SLOT:(3 * u + 2) * SLOT].rearrange("p (k c n) -> p k c n", k=2, c=DC)
                    pe.wait_ge(*L(l, "hid", i * STEPS + s + 1))
                    for cc in range(DC):
                        ins = mm(ps[:, b, :], hT[:, cc, t * P:(t + 1) * P], w13[:, :, cc, :], start=cc == 0, stop=cc == DC - 1)
                    ins.then_inc(S("up_mm"), 1)

                def turn_hidden(i, s):
                    b = s % 2
                    pe.wait_ge(*L(l, "hid", i * STEPS + s + 3))
                    pe.wait_ge(*L(l, "hidT", i * STEPS + s + 1))
                    for cc in range(2):
                        ins = tr(ps[:, 2 + b, cc * P:(cc + 1) * P], hid[:, b, cc::2], ident)
                    ins.then_inc(S("hid_tr"), 1)

                def down(i, s):
                    u, t, b = s // TILES, s % TILES, s % 2
                    if t == 0:
                        arrived_expert(i, 3 * u + 2)
                    w2 = pool[:, (3 * u + 2) * SLOT:(3 * u + 3) * SLOT].rearrange("p (c n) -> p c n", c=2)
                    pe.wait_ge(*L(l, "hidT", i * STEPS + s + 3))
                    pe.wait_ge(*L(l, "acc", i * STEPS + s + 1))
                    for n in range(2):
                        for cc in range(2):
                            ins = mm(ps[:, 4 + 2 * b + n, :], hidT[:, b, cc, :], w2[:, cc, n * 512:n * 512 + 512],
                                     start=cc == 0, stop=cc == 1)
                    ins.then_inc(S("down_mm"), 1)

                with pe.Fori(0, TURNS) as i:
                    for s in range(STEPS):
                        up(i, s)
                        if s >= 1:
                            turn_hidden(i, s - 1)
                        if s >= 2:
                            down(i, s - 2)
                    turn_hidden(i, STEPS - 1)
                    down(i, STEPS - 2)
                    down(i, STEPS - 1)
                pe.wait_ge(*L(l, "acc", TILES * NE + 2))

            pe.wait_ge(S("cs32"), 1)
            mod_round(0, 0)
            norm_transposes(0, 0)
            wait_hT(0, 0)
            arrived(pe, "v")
            for t in range(TILES):
                for cc in range(DC):
                    ins = mm(ps[:, t, :], hT[:, cc, t * P:(t + 1) * P], weight("v", DC, 512)[:, cc, :], start=cc == 0, stop=cc == DC - 1)
                ins.then_inc(S("v_mm"), 1)
            pe.wait_ge(*L(0, "mod_col", 1))
            for name in ("gate_c", "xa", "gate_b"):
                arrived(pe, name)
            for j in range(4):
                if j == 1:
                    pe.wait_ge(S("vn"), 1)
                if j >= 2:
                    pe.wait_ge(S("y_conv"), j - 1)
                for k, name in enumerate(("gate_c", "xa", "gate_b")):
                    for cc in range(DC):
                        ins = mm(ps[:, ((3, 6)[j % 2] + k) % 8, 0:T], weight(name, DC, 512)[:, cc, j::4], hT[:, cc, :],
                                 start=cc == 0, stop=cc == DC - 1)
                ins.then_inc(S("conv_mm"), 1)
            pe.wait_ge(S("vn"), 3)
            pe.wait_ge(S("late"), 16 * (N_LATE + 4))
            for g in range(4):
                ins = tr(ps[:, 1, g * P:(g + 1) * P], sguw[:, g, :], ident)
            ins.then_inc(S("sgu_tr"), 1)
            arrived(pe, "u")
            for g in range(4):
                bs, bu = (1, 4)[g % 2], (2, 3)[g % 2]
                if g == 1:
                    pe.wait_ge(S("y_conv"), 3)
                if g >= 2:
                    pe.wait_ge(S("y_sgu"), g - 1)
                for cc in range(DC):
                    mm(ps[:, bu, 0:T], weight("u", DC, 512)[:, cc, g * P:(g + 1) * P], hT[:, cc, :], start=cc == 0, stop=cc == DC - 1)
                pe.wait_ge(S("sguT"), 1)
                for t in range(TILES):
                    ins = mm(ps[:, bs, t * P:(t + 1) * P], vn[:, t, g * P:(g + 1) * P], sguT[:, g, :], start=True, stop=True)
                ins.then_inc(S("sgu_mm"), 1)
            pe.wait_ge(S("y_conv"), 4)
            pe.wait_ge(S("y_sgu"), 4)
            mod_round(0, 1)
            pe.wait_ge(*L(1, "mod_col", 1))
            gate_rows(0, 0)
            arrived(pe, "out0.0")
            arrived(pe, "out0.1")
            project_out(0, ("out0.0", "out0.1"))
            pe.wait_ge(*L(0, "gate_rows", 4))
            mod_round(0, 2)
            norm_transposes(0, 1)
            pe.wait_ge(*L(2, "mod_col", 1))
            router(0)
            experts(0)
            gate_rows(0, 1)
            pe.wait_ge(*L(1, "gate_rows", 4))
            mod_round(1, 0)
            norm_transposes(1, 0)

            wait_hT(1, 0)
            for half in range(2):
                arrived(pe, f"in1.{half}")
                w = weight(f"in1.{half}", 4, Z_END)
                for t in range(TILES):
                    for b, lo, hi in ((2 * t, 0, 512), (2 * t + 1, 512, Z_END)):
                        for k in range(4):
                            cc = 4 * half + k
                            ins = mm(ps[:, b, 0:hi - lo], hT[:, cc, t * P:(t + 1) * P], w[:, k, lo:hi], start=cc == 0, stop=cc == DC - 1)
                        if half:
                            ins.then_inc(S("z_mm"), 1)
            pe.wait_ge(S("z_low"), 3)
            pe.wait_ge(S("z_high"), 3)
            pe.wait_ge(*L(3, "mod_col", 1))
            for j in range(2):
                b = (6, 4)[j]
                mm(ps[:, b, 0:2 * P], z[:, 0, j * P:(j + 1) * P], cst[:, C_CS1:C_CS2], start=True, stop=True)
                for t in (1, 2):
                    ins = mm(ps[:, b + 1, :], z[:, t, j * P:(j + 1) * P], cst[:, C_CS2 + 512 * (t - 1):C_CS2 + 512 * t],
                             start=t == 1, stop=t == 2)
                ins.then_inc(S("four_tok_mm"), 1)
            pe.wait_ge(S("qn"), 3)
            for cc in range(3):
                for t in range(TILES):
                    ins = tr(ps[:, cc, t * P:(t + 1) * P], z[:, t, Z_Q + cc:Z_KV:3], ident)
                ins.then_inc(S("qn_tr"), 1)
            pe.wait_ge(S("kvn"), 3)
            pe.wait_ge(S("fmid"), 2)
            for cc in range(2):
                for kt in range(4):
                    src = ckv[:, cc::2] if kt == 1 else z[:, (0, None, 1, 2)[kt], Z_KV + cc:Z_PE:2]
                    ins = tr(ps[:, 3 + cc, kt * P:(kt + 1) * P], src, ident)
                ins.then_inc(S("kv_tr"), 1)
            pe.wait_ge(S("kpe"), 1)
            for kt in range(4):
                ins = mm(ps[NOPE:QH, 5, kt * P:(kt + 1) * P], kpe[:, kt, :], ident, start=True, stop=True)
            ins.then_inc(S("kpe_tr"), 1)
            for j in range(2):
                for k in range(2):
                    ins = mm(ps[:, 6 + j, 0:T], cst[:, C_CC + P * k:C_CC + P * (k + 1)], fmid[j][:, k, :], start=k == 0, stop=k == 1)
            ins.then_inc(S("four_mm"), 1)
            pe.wait_ge(S("qnT"), 3)
            arrived(pe, "uq")
            for t in range(TILES):
                if t == 1:
                    pe.wait_ge(S("kvT"), 2)
                    pe.wait_ge(S("kpeT"), 1)
                if t == 2:
                    pe.wait_ge(S("q_out"), 1)
                for n, w in ((0, 512), (1, 512), (2, 128)):
                    for cc in range(3):
                        ins = mm(ps[:, 3 * (t % 2) + n, 0:w], qnT[:, cc, t * P:(t + 1) * P],
                                 weight("uq", 3, NH * QH)[:, cc, n * 512:n * 512 + w], start=cc == 0, stop=cc == 2)
                ins.then_inc(S("q_mm"), 1)
            arrived(pe, "ukv")
            ukv = weight("ukv", 2, NH * 2 * VD).rearrange("p c (h n) -> p c h n", h=NH)
            pe.wait_ge(S("y_four"), 1)
            for kt in range(4):
                if kt == 1:
                    pe.wait_ge(S("q_out"), 2)
                if kt >= 2:
                    pe.wait_ge(S("vv"), kt - 1)
                for n, h0, h1 in ((0, 0, 8), (1, 8, NH)):
                    for cc in range(2):
                        ins = mm(ps[:, (6, 3)[kt % 2] + n, 0:(h1 - h0) * VD], kvT[:, cc, kt * P:(kt + 1) * P],
                                 ukv[:, cc, h0:h1, NOPE:NOPE + VD], start=cc == 0, stop=cc == 1)
                ins.then_inc(S("v2_mm"), 1)
            pe.wait_ge(S("q_rot"), 1)
            pe.wait_ge(S("q_out"), 3)
            pe.wait_ge(S("vv"), 4)
            pe.wait_ge(S("kpeT"), 1)

            def head_probs(h):
                pe.wait_ge(S("probs"), h + 1)
                for m in range(7):
                    ins = tr(bank2(4, 7 * P)[:, m * P:(m + 1) * P], pr_s[:, m * P:(m + 1) * P], ident)
                ins.then_inc(S("p_tr"), 1)

            def head_values(h):
                pe.wait_ge(S("pT"), h + 1)
                if h >= 2:
                    pe.wait_ge(S("o_out"), h - 1)
                for t in range(TILES):
                    keys = ((0, 0),) if t == 0 else tuple((1 + k, 1 + 3 * (t - 1) + k) for k in range(3))
                    for n, (kt, m) in enumerate(keys):
                        ins = mm(ps[:, 6 + h % 2, t * VD:(t + 1) * VD], prT[:, m * P:(m + 1) * P],
                                 vv[:, kt, h * VD:(h + 1) * VD], start=n == 0, stop=n == len(keys) - 1)
                ins.then_inc(S("o_mm"), 1)

            for h in range(NH):
                if h:
                    pe.wait_ge(S("kT"), h)
                for cc in range(2):
                    ins = mm(ps[0:NOPE, 0, :], ukv[:, cc, h, 0:NOPE], kvT[:, cc, :], start=cc == 0, stop=cc == 1)
                ins.then_inc(S("k_mm"), 1)
                if h:
                    pe.wait_ge(S("qT"), h)
                for t in range(TILES):
                    ins = tr(ps[0:QH, 1, t * P:(t + 1) * P], q[:, t, h * QH:(h + 1) * QH], ident)
                ins.then_inc(S("qT_tr"), 1)
                if h:
                    head_probs(h - 1)
                pe.wait_ge(S("kT"), h + 1)
                pe.wait_ge(S("qT"), h + 1)
                for t in range(TILES):
                    ins = mm(scores(t), qT[0:QH, h % 2, t * P:(t + 1) * P], kT[0:QH, h % 2, 0:P] if t == 0 else kT[0:QH, h % 2, P:512],
                             start=True, stop=True)
                ins.then_inc(S("s_mm"), 1)
                if h:
                    head_values(h - 1)
            head_probs(NH - 1)
            head_values(NH - 1)
            pe.wait_ge(S("o_out"), NH)
            mod_round(1, 1)
            for t in range(TILES):
                for k in range(6):
                    ins = tr(bank2(2 * t, 6 * P)[:, k * P:(k + 1) * P], o[:, t, k * P:(k + 1) * P], ident)
                ins.then_inc(S("o_tr"), 1)
            pe.wait_ge(*L(4, "mod_col", 1))
            gate_rows(1, 0)
            pe.wait_ge(S("y_att"), 3)
            arrived(pe, "out1.0")
            arrived(pe, "out1.1")
            project_out(1, ("out1.0", "out1.1"))
            pe.wait_ge(*L(2, "gate_rows", 4))
            mod_round(1, 2)
            norm_transposes(1, 1)
            pe.wait_ge(*L(5, "mod_col", 1))
            router(1)
            experts(1)
            gate_rows(1, 1)


def constants():
    import numpy as np

    out = np.zeros((P, C_END), np.float64)
    out[:, C_ID:C_ID + P] = np.eye(P)
    p = np.arange(P)
    gw = DCF // 4
    for at, n, tiles in ((C_CS1, P, 1), (C_CS2, 2 * P, 2)):
        for k in range(tiles):
            ang = 2 * np.pi * ((np.outer(p + k * P, np.arange(n))) % n) / n
            scale = 1.0 / np.sqrt(n * gw)
            out[:, at + 2 * n * k:at + 2 * n * k + n] = np.cos(ang) * scale
            out[:, at + 2 * n * k + n:at + 2 * n * (k + 1)] = np.sin(ang) * scale
    ang = 2 * np.pi * (np.outer(p, p) % gw) / gw
    same = (p[:, None] // gw) == (p[None, :] // gw)
    out[:, C_CC:C_CC + P] = np.cos(ang) * same
    out[:, C_CC + P:C_CC + 2 * P] = -np.sin(ang) * same
    nf = ROPE // 4
    inv = (10000.0 ** (-np.arange(nf, dtype=np.float32) / np.float32(nf))).astype(np.float32)
    for t in range(2):
        tok = t * P + p
        for k, pos in enumerate((tok // GRID_W, tok % GRID_W)):
            ang = (pos.astype(np.float32)[:, None] * inv[None, :]).astype(np.float32)
            out[:, C_COS + 16 * t + 8 * k:C_COS + 16 * t + 8 * k + 8] = np.cos(ang)
            out[:, C_SIN + 16 * t + 8 * k:C_SIN + 16 * t + 8 * k + 8] = np.sin(ang)
    out[:, C_FIRST:C_END] = np.arange(4, 0, -1)
    return out.astype(np.float32)


INS = ["x_prompt", "x_sample", "cache_ckv", "cache_kpe", "c", "c_ctx", "mod_w", "mod_b", "norm1_g", "norm2_g",
       "ev_w_in", "ev_conv_w", "ev_sgu_norm_g", "ev_sgu_w", "ev_sgu_b", "ev_w_out", "od_w_in", "od_q_norm_g",
       "od_w_uq", "od_kv_norm_g", "od_w_ukv", "od_w_out", "moe_wg", "moe_bg", "moe_we", "moe_be", "moe_w1",
       "moe_w3", "moe_w2", "final_norm_g"]
OUTS = [(1, P, D), (1, 2 * P, D), (1, 1, P, KVL), (1, 1, P, ROPE)]


def kernel(**inputs):
    import numpy as np
    import concourse.bacc as bacc
    from concourse.bass_utils import run_bass_kernel_spmd

    nc = bacc.Bacc("TRN2", target_bir_lowering=False, num_devices=1)
    arrays, args = {}, []
    for name in INS:
        a = np.ascontiguousarray(inputs[name])
        arrays[f"in_{name}"] = a
        args.append(nc.dram_tensor(f"in_{name}", a.shape, F32, kind="ExternalInput").ap())
    arrays["in_consts"] = constants()
    args.append(nc.dram_tensor("in_consts", (P, C_END), F32, kind="ExternalInput").ap())
    for i, shape in enumerate(OUTS):
        args.append(nc.dram_tensor(f"out_{i}", shape, F32, kind="ExternalOutput").ap())
    program(nc, *args)
    r = run_bass_kernel_spmd(nc, [arrays], core_ids=[0])
    return tuple(r.results[0][f"out_{i}"] for i in range(len(OUTS)))
```

```python
from contextlib import ExitStack

import concourse.bass as bass
from concourse import mybir

F32 = mybir.dt.float32
I32 = mybir.dt.int32
ALU = mybir.AluOpType
ACT = mybir.ActivationFunctionType
AX = mybir.AxisListType.X

P = 128
D = 1024
DC = D // P
TILES = 3
T = TILES * P
GRID_W = 64
EPS = 1e-6
NH, NOPE, ROPE, VD = 12, 64, 32, 64
QH = NOPE + ROPE
QL, KVL, DCF = 384, 256, 256
Z_Q, Z_KV, Z_PE, Z_END = DCF, DCF + QL, DCF + QL + KVL, DCF + QL + KVL + ROPE
NE, NG, EPG, DE = 16, 4, 4, 256
SLOT = 2048
NSLOT = 12
HALF = P // 2
PAIRS = NE // 2
UNROLL = 2
TURNS = PAIRS // UNROLL
STEPS = PAIRS + (2 * T - PAIRS) // HALF + 1
T_CUM, T_ALL, T_ROUNDS, T_END = 0, 8, 9, 17
SCALE = float(QH) ** -0.5
NEG = -3.0e38

C_ID, C_CS1, C_CS2, C_CC, C_COS, C_SIN, C_FIRST = 0, 128, 384, 1408, 1664, 1696, 1728
C_TRI, C_IOTA, C_TOK, C_HALF, C_ONE, C_END = 1732, 1860, 1988, 1991, 2007, 2008


def cond_of(tile):
    return 0 if tile == 0 else 1


def program(nc, x_prompt, x_sample, cache_ckv, cache_kpe, c, c_ctx, mod_w, mod_b, norm1_g, norm2_g,
            ev_w_in, ev_conv_w, ev_sgu_norm_g, ev_sgu_w, ev_sgu_b, ev_w_out, od_w_in, od_q_norm_g,
            od_w_uq, od_kv_norm_g, od_w_ukv, od_w_out, moe_wg, moe_bg, moe_we, moe_be, moe_w1,
            moe_w3, moe_w2, final_norm_g, consts, y_prompt, y_sample, new_ckv, new_kpe):
    with ExitStack() as ctx:
        def sb(name, shape, dtype=F32):
            return ctx.enter_context(nc.sbuf_tensor(name, shape, dtype))

        sems = {}

        def S(name):
            if name not in sems:
                sems[name] = ctx.enter_context(nc.semaphore(name))
            return sems[name]

        TIMES = dict(mod_mm=1, mod_row=1, mod_cmm=1, mod_col=1, norm_root=3, norm_xn=3, norm_tr=3, norm_hT_act=3,
                     norm_hT_dve=3, norm_cols=1, gate_rows=4, gate_rows_mm=4, out_mm=6, x1=3, x2=3, router_mm=1,
                     gdiff=1, gexp=1, ediff=1, eexp=1, h_tr=3, h_act=3, h_dve=3, mask=1, rank_mm=1, table=1, onehot=1,
                     meta_mm=1, meta=1, all_stored=1, y_rows=6 * 16)

        def L(k, name, n):
            return S(name), TIMES[name] * k + n

        RING = NSLOT * SLOT
        pool = sb("pool", [P, RING + 8112])
        SCR = RING
        x = sb("x", [P, TILES, D])
        hT = sb("hT", [P, DC, T])
        xn = sb("xn", [P, TILES, D])
        yT = sb("yT", [P, DC, T])
        mrow = [sb(f"mrow{l}", [P, 3, 512]) for l in range(2)]
        ga = sb("ga", [P, 2, D])
        cst = sb("cst", [P, C_END])
        cs32 = sb("cs32", [P, DC, 32])
        modcol = [sb(f"modcol{l}", [P, 3, DC, 2, 2]) for l in range(2)]
        scg = [sb(f"scg{l}", [P, 2, DC, 2]) for l in range(2)]
        gcol = sb("gcol", [P, 2, 2, DC])
        minus_half = sb("minus_half", [P, 1])
        ss = sb("ss", [P, 2 * TILES])
        rstd = sb("rstd", [P, 2 * TILES])
        convw = sb("convw", [P, 3, 4])
        sgug = sb("sgug", [P, 4])
        qg = sb("qg", [P, 3])
        wg = sb("wg", [P, 2, DC, NG])
        we = sb("we", [P, 2, DC, NE])
        rb = sb("rb", [P, 2, NG + NE])
        idx = sb("idx", [P, STEPS], I32)
        idx_now = sb("idx_now", [P, 1], I32)
        slot_of = sb("slot_of", [P, 2 * TILES], I32)
        table = sb("table", [P, 2, T_END], I32)
        h_rows = nc.dram_tensor("h_rows", (T, D), F32, kind="Internal").ap()
        y_rows = nc.dram_tensor("y_rows", (STEPS * P, D), F32, kind="Internal").ap()
        ps = ctx.enter_context(nc.psum_tensor("ps", [P, 8, 512], F32))

        ident = cst[:, C_ID:C_ID + P]

        def scratch(at, n, base=SCR):
            assert base + at + n <= RING + 8112
            return pool[:, base + at:base + at + n]

        vn = scratch(0, 1536).rearrange("p (t n) -> p t n", t=3)
        gcs = scratch(1536, 384)
        pr = scratch(1920, 384)
        cv = scratch(2304, 384)
        sguw = scratch(2688, 512).rearrange("p (g n) -> p g n", g=4)
        sguT = scratch(3200, 512).rearrange("p (g n) -> p g n", g=4)
        sgub = scratch(3712, 512).rearrange("p (g n) -> p g n", g=4)
        sv = scratch(4224, 384)
        OB = SCR - SLOT
        q = scratch(0, TILES * NH * QH, OB).rearrange("p (t n) -> p t n", t=3)
        z = scratch(3456, 3 * Z_END, OB).rearrange("p (t n) -> p t n", t=3)
        o = scratch(3456, 3 * NH * VD, OB).rearrange("p (t n) -> p t n", t=3)
        qT = scratch(6240, 2 * T, OB).rearrange("p (b n) -> p b n", b=2)
        kT = scratch(7008, 1024, OB).rearrange("p (b n) -> p b n", b=2)
        pr_s = scratch(8032, 896, OB)
        prT = scratch(8928, 896, OB)
        rtmp = scratch(8032, 768, OB).rearrange("p (k n) -> p k n", k=4)
        ckv = scratch(8928, 256, OB)
        kpe = scratch(9184, 4 * ROPE, OB).rearrange("p (t n) -> p t n", t=4)
        kvg = scratch(9904, KVL, OB)
        nmax = scratch(9824, 3, OB)
        psum_of = scratch(9828, 3, OB)
        pinv = scratch(9832, 3, OB)
        ktmp = scratch(9840, 64, OB).rearrange("p (k n) -> p k n", k=4)
        qnT = hT[:, 0:3, :]
        kvT = hT[:, 3:6, :].rearrange("p a b -> p (a b)")[:, 0:1024].rearrange("p (c n) -> p c n", c=2)
        fmid = [hT[:, :, :].rearrange("p a b -> p (a b)")[:, 2304:3072].rearrange("p (k n) -> p k n", k=2), qT]
        vv = xn[:, :, :].rearrange("p a b -> p (a b)").rearrange("p (t n) -> p t n", t=4)
        xg = scratch(0, D)
        hTe = scratch(D, D)
        ys = scratch(2 * D, D)
        sil = scratch(3072, DE)
        hid = scratch(3328, DE)
        hidT = scratch(3584, DE).rearrange("p (c n) -> p c n", c=2)
        condraw = scratch(5900, 2 * DC).rearrange("p (r c) -> p r c", r=2)
        zeros = scratch(4608, D)
        rt = scratch(3840, 1800)
        gate_in = scratch(5700, STEPS)
        yg = [yT[:, :, :].rearrange("p a b -> p (a b)"), scratch(0, 3 * D)]
        finalg = scratch(6144, 1024)


        def scores(t):
            return (ps[:, 2, 0:P], ps[:, 2, P:512], ps[:, 3, 0:T])[t]

        def probs(t):
            return pr_s[:, (0, P, P + T)[t]:(P, P + T, P + 2 * T)[t]]

        R, at = {}, 0
        for name, n in (("logits", 20), ("gmax", 1), ("gdiff", 4), ("gexp", 4), ("cand", 4), ("cmax", 1), ("ghot", 4),
                        ("esel4", 16), ("esel", 4), ("top1", 1), ("hot1", 4), ("rest", 4), ("top2", 1), ("ediff", 1),
                        ("hot2", 4), ("eexp", 1), ("gsum", 1), ("den", 1), ("w1", 1), ("w2", 1), ("weights", 2),
                        ("hot", 32), ("mask", 16), ("prod", 32), ("rank", 2), ("before", 2), ("half", 2), ("round", 2),
                        ("step", 2), ("place", 2), ("row", 2), ("steps_hot", 2 * STEPS), ("steps_rhs", 4 * STEPS)):
            R[name] = rt[:, at:at + TILES * n].rearrange("p (t n) -> p t n", t=TILES)
            at += TILES * n
        assert at + 6 * P <= 1800
        place_hot = rt[:, at:at + 6 * P].rearrange("p (t k n) -> p t k n", t=TILES, k=2)
        R["esel4"] = R["esel4"].rearrange("p t (g e) -> p t g e", g=NG)
        hot = R["hot"].rearrange("p t (k n) -> p t k n", k=2)
        prod = R["prod"].rearrange("p t (k n) -> p t k n", k=2)
        pairs = scratch(5740, 5 * PAIRS).rearrange("p (m q) -> p m q", m=5)
        first = cst[:, C_FIRST:C_TRI].unsqueeze(1)

        landed, loads, owner, count, cursor = {}, [], {}, [0] * NSLOT, [0]

        def item(name, n, src, shape, used, limit=NSLOT):
            s0 = cursor[0] if cursor[0] + n <= limit else 0
            cursor[0] = s0 + n
            waits = {}
            for s in range(s0, s0 + n):
                if s in owner:
                    waits[owner[s][:-1]] = max(waits.get(owner[s][:-1], 0), owner[s][-1])
                owner[s] = used
            count[s0] += 1
            landed[name] = (s0, 16 * count[s0])
            loads.append((s0, src, shape, waits))

        def mod_items(l, i, limit=NSLOT):
            for j in range(4):
                b = 4 * i + j
                item(f"mod{l}.{b}", 2, mod_w[l, :, b * 512:(b + 1) * 512].rearrange("(p c) n -> p c n", c=DC),
                     (DC, 512), ("mod_mm", 3 * l + i + 1), limit)

        def expert_places(l):
            waits, before = [owner.get(s) for s in range(NSLOT)], list(count)
            for s in range(NSLOT):
                count[s] += TURNS
                owner[s] = ("pair", l, T_CUM + PAIRS - 1 if s < NSLOT // 2 else T_ALL)
            cursor[0] = 0
            return waits, before

        def weight(name, a, b):
            s0 = landed[name][0]
            return pool[:, s0 * SLOT:s0 * SLOT + a * b].rearrange("p (a b) -> p a b", a=a)

        mod_items(0, 0)
        for name, at, used in (("v", 2048, ("v_mm", 3)), ("gate_c", 512, ("conv_mm", 4)), ("xa", 1024, ("conv_mm", 4)),
                               ("gate_b", 0, ("conv_mm", 4)), ("u", 1536, ("sgu_mm", 4))):
            item(name, 2, ev_w_in[0, :, at:at + 512].rearrange("(p c) n -> p c n", c=DC), (DC, 512), used)
        mod_items(0, 1)
        item("out0.0", 2, ev_w_out[0, 0:512, :].rearrange("(p j) n -> p j n", j=4), (4, D), ("out_mm", 6))
        item("out0.1", 2, ev_w_out[0, 512:1024, :].rearrange("(g d) n -> d g n", g=4), (4, D), ("out_mm", 6))
        mod_items(0, 2)
        split = len(loads)
        places = [expert_places(0)]
        ODD = NSLOT - 1
        mod_items(1, 0, ODD)
        for i in range(2):
            item(f"in1.{i}", 2, od_w_in[0].rearrange("(p c) n -> p c n", c=DC)[:, 4 * i:4 * i + 4, :],
                 (4, Z_END), ("z_mm", 6), ODD)
        item("uq", 2, od_w_uq[0].rearrange("(p c) n -> p c n", c=3), (3, NH * QH), ("q_mm", 3), ODD)
        item("ukv", 2, od_w_ukv[0].rearrange("(p c) n -> p c n", c=2), (2, NH * 2 * VD), ("k_mm", NH), ODD)
        mod_items(1, 1, ODD)
        for i in range(2):
            item(f"out1.{i}", 2, od_w_out[0].rearrange("(k p) n -> p k n", p=P)[:, 4 * i:4 * i + 4, :],
                 (4, D), ("out_mm", 12), ODD)
        mod_items(1, 2, ODD)
        owner[NSLOT - 1] = ("qT_tr", NH)
        places.append(expert_places(1))

        def arrived(eng, name):
            s0, value = landed[name]
            eng.wait_ge(S(f"slot{s0}"), value)

        class Chain:

            def __init__(self, eng, name):
                self.eng, self.sem, self.n, self.turn, self.per = eng, S(name), 0, None, 0

            def link(self, ins):
                self.n += 1
                ins.then_inc(self.sem, 1)
                self.eng.wait_ge(self.sem, self.n if self.turn is None else self.turn * self.per + self.n)

            def loop(self, turn, per):
                self.turn, self.per, self.start = turn, per, self.n

            def end(self, turns):
                assert self.n - self.start == self.per
                self.n, self.turn = self.start + self.per * turns, None

        def norm_columns(l, w):
            i, v = ((0, 0), (1, 1))[w]
            return (lambda c, r: scg[l][:, w, c, r:r + 1]), (lambda c, r: modcol[l][:, i, c, v, r:r + 1])

        def bank2(b, n):
            return ps[:, b:b + 2, :].rearrange("p b n -> p (b n)")[:, 0:n]

        def token_half(t, half):
            return xn[:, t, half * 512:half * 512 + 512]

        N_EARLY, N_LATE = 9, 17
        HT_ACT = 4
        block = ctx.enter_context(nc.Block())

        @block.sync
        def _(sp):
            def steps_until(l, entry):
                return sp.value_load(table[0:1, l, entry], min_val=1, max_val=STEPS)

            def wait_used(key, v):
                if key[0] == "pair":
                    sp.wait_ge(*L(key[1], "table", 1))
                    sp.wait_ge(S(f"L{key[1]}_down_mm"), steps_until(key[1], slice(v, v + 1)))
                    sp.nop()
                else:
                    sp.wait_ge(S(key[0]), v)

            def load(n):
                s0, src, (a, b), waits = loads[n]
                for k, v in waits.items():
                    wait_used(k, v)
                sp.dma_start(pool[:, s0 * SLOT:s0 * SLOT + a * b].rearrange("p (a b) -> p a b", a=a), src) \
                    .then_inc(S(f"slot{s0}"), 16)

            def expert_load(l, k, e, u):
                s, w = 3 * u + k, (moe_w1, moe_w3, moe_w2)[k]
                sp.dma_start(pool[:, s * SLOT:(s + 1) * SLOT],
                             w[l, bass.ds(e, 1)].rearrange("a (p c) n -> p (a c n)", p=P)).then_inc(S(f"slot{s}"), 16)

            def experts(l):
                waited = {}
                for s in range(NSLOT):
                    if places[l][0][s]:
                        *k, v = places[l][0][s]
                        if waited.get(tuple(k), 0) < v:
                            wait_used(k, v)
                            waited[tuple(k)] = v
                    expert_load(l, s % 3, s // 3, s // 3)
                sp.wait_ge(*L(l, "table", 1))
                with sp.Fori(1, TURNS) as i:
                    for u in range(UNROLL):
                        steps = steps_until(l, bass.ds(i * UNROLL + (u + 1 - UNROLL), 1))
                        sp.wait_ge(S(f"L{l}_up_mm"), steps)
                        sp.nop()
                        for e in range(2):
                            expert_load(l, 0, i * 2 * UNROLL + (2 * u + e), 2 * u + e)
                            expert_load(l, 1, i * 2 * UNROLL + (2 * u + e), 2 * u + e)
                        sp.wait_ge(S(f"L{l}_down_mm"), steps)
                        sp.nop()
                        for e in range(2):
                            expert_load(l, 2, i * 2 * UNROLL + (2 * u + e), 2 * u + e)

            for n in range(split):
                load(n)
            experts(0)
            for n in range(split, len(loads)):
                load(n)
            experts(1)

        @block.gpsimd
        def _(gps):
            for l in range(2):
                nc.gpsimd.memset(mrow[l][:, :, :], 0.0).then_inc(S("rows_zero"), 1)
            nc.gpsimd.memset(cs32[:, :, :], 0.0).then_inc(S("cs32_zero"), 1)
            nc.gpsimd.memset(zeros, 0.0).then_inc(S("zeros"), 1)
            ch = Chain(gps, "gps_chain")
            ch.link(nc.gpsimd.memset(minus_half[:, :], -0.5))

            def root(name, n, at, width):
                gps.wait_ge(S(name + "_ss"), n)
                ch.link(nc.gpsimd.tensor_scalar(rstd[:, at:at + 1], ss[:, at:at + 1], 1.0 / width, EPS, ALU.mult, ALU.add))
                nc.gpsimd.tensor_tensor(rstd[:, at:at + 1], rstd[:, at:at + 1], minus_half[:, :], ALU.pow) \
                    .then_inc(S(name + "_root"), 1)

            def tokens_in_out(l):
                def gather(index):
                    nc.gpsimd.indirect_dma_start(out=xg, out_offset=None, in_=h_rows[:, :],
                                                 in_offset=bass.IndirectOffsetOnAxis(ap=index, axis=0)) \
                        .then_inc(S(f"L{l}_gathered"), 16)

                gps.wait_ge(*L(l, "meta", 1))
                gps.wait_ge(S(f"L{l}_stored"), 16)
                gather(idx[:, 0:1])
                n = gps.value_load(table[0:1, l, T_ALL:T_ALL + 1], min_val=PAIRS, max_val=STEPS - 1)
                with gps.Fori(1, n + 1) as j:
                    gps.wait_ge(S(f"L{l}_x_tr"), j)
                    gps.nop()
                    nc.gpsimd.tensor_copy(idx_now[:, :], idx[:, bass.ds(j, 1)]).then_inc(S(f"L{l}_idx_now"), 1)
                    gps.wait_ge(*L(l, "meta", 1))
                    gps.wait_ge(S(f"L{l}_idx_now"), j)
                    gather(idx_now[:, 0:1])
                gps.wait_ge(S("rows_written"), 16)
                gps.wait_ge(*L(l, "all_stored", 1))
                for t in range(TILES):
                    for k in range(2):
                        nc.gpsimd.indirect_dma_start(out=yg[k][:, t * D:(t + 1) * D], out_offset=None, in_=y_rows[:, :],
                                                     in_offset=bass.IndirectOffsetOnAxis(
                                                         ap=slot_of[:, 2 * t + k:2 * t + k + 1], axis=0)) \
                            .then_inc(S("y_rows"), 16)

            for t in range(TILES):
                root("norm", t + 1, t, D)
            for t in range(TILES):
                root("v", t + 1, 3 + t, 512)
            for t in range(TILES):
                root("norm", TILES + t + 1, t, D)
            tokens_in_out(0)
            for t in range(TILES):
                root("norm", 2 * TILES + t + 1, t, D)
            for t in range(TILES):
                root("qc", t + 1, t, QL)
                root("kvc", t + 1, 3 + t, KVL)
            for t in range(TILES):
                root("norm", 3 * TILES + t + 1, t, D)
            tokens_in_out(1)
            for t in range(TILES):
                root("norm", 4 * TILES + t + 1, t, D)

        @block.scalar
        def _(act):
            a_ = nc.scalar
            ch = Chain(act, "act_chain")

            def row(src, n):
                return src.rearrange("(a n) -> a n", a=1).broadcast_to((P, n))

            early = [(x[:, 0, :], x_prompt[0]), (x[:, 1:3, :], x_sample[0].rearrange("(t p) d -> p t d", p=P)),
                     (condraw[:, 0, :], c_ctx.rearrange("(p c) -> p c", c=DC)),
                     (condraw[:, 1, :], c[0].rearrange("(p c) -> p c", c=DC)),
                     (cst[:, :], consts)]
            early += [(gcol[:, l, w, :], g[l].rearrange("(p c) -> p c", c=DC))
                      for l in range(2) for w, g in enumerate((norm1_g, norm2_g))]
            assert len(early) == N_EARLY
            for dst, src in early:
                act.dma_start(dst, src).then_inc(S("early"), 16)
            act.wait_ge(S("rows_zero"), 2)
            for l in range(2):
                for r in range(2):
                    for j in range(4):
                        act.dma_start(mrow[l][32 * j + r:32 * j + r + 1, :, :],
                                      mod_b[l].rearrange("(i j n) -> j i n", i=3, j=4)[j:j + 1]).then_inc(S("bias"), 16)
            late = [(convw[:, k, :], ev_conv_w[0, k].rearrange("(p j) -> p j", j=4)) for k in range(3)]
            late += [(sguw, ev_sgu_w[0].rearrange("g p q -> p g q")),
                     (sgub, row(ev_sgu_b[0].rearrange("g n -> (g n)"), 4 * P).rearrange("p (g n) -> p g n", g=4)),
                     (qg[:, :], od_q_norm_g[0].rearrange("(p c) -> p c", c=3)),
                     (kvg, row(od_kv_norm_g[0], KVL)), (ckv, cache_ckv[0, 0]), (kpe[:, 1, :], cache_kpe[0, 0])]
            for l in range(2):
                late += [(wg[:, l], moe_wg[l].rearrange("(p c) g -> p c g", c=DC)),
                         (we[:, l], moe_we[l].rearrange("(p c) g e -> p c (g e)", c=DC)),
                         (rb[:, l, 0:NG], row(moe_bg[l], NG)),
                         (rb[:, l, NG:], row(moe_be[l].rearrange("g e -> (g e)"), NE))]
            assert len(late) == N_LATE
            for dst, src in late:
                act.dma_start(dst, src).then_inc(S("late"), 16)
            for g in range(4):
                act.dma_start(sgug[:, g:g + 1], ev_sgu_norm_g[0].rearrange("(g d a) -> g d a", g=4, a=1)[g]) \
                    .then_inc(S("late"), 16)

            def squares(name, ready, dst, src, out):
                act.wait_ge(S(ready[0]), ready[1])
                a_.activation(dst, src, ACT.Square, accum_out=out).then_inc(S(name + "_ss"), 1)

            def norm_squares(ready, n):
                for t in range(TILES):
                    squares("norm", (ready, n if ready == "early" else n + t + 1), xn[:, t, :], x[:, t, :], ss[:, t:t + 1])

            def norm_evacuate(l, w):
                scale, shift = norm_columns(l, w)
                act.wait_ge(*L(2 * l + w, "norm_cols", 1))
                for t in range(TILES):
                    act.wait_ge(*L(2 * l + w, "norm_tr", t + 1))
                    for cc in range(HT_ACT):
                        ins = a_.activation(hT[:, cc, t * P:(t + 1) * P], bank2(2 * t, D)[:, cc * P:(cc + 1) * P],
                                            ACT.Identity, bias=shift(cc, cond_of(t)), scale=scale(cc, cond_of(t)))
                    ins.then_inc(S("norm_hT_act"), 1)

            def router_exps(l):
                act.wait_ge(*L(l, "gdiff", 1))
                a_.activation(R["gexp"], R["gdiff"], ACT.Exp).then_inc(S("gexp"), 1)
                act.wait_ge(*L(l, "ediff", 1))
                a_.activation(R["eexp"], R["ediff"], ACT.Exp).then_inc(S("eexp"), 1)

            def by_tokens(l):
                for t in range(TILES):
                    act.wait_ge(*L(l, "h_tr", t + 1))
                    a_.activation(token_half(t, 0), ps[:, 2 * t, :], ACT.Copy) \
                        .then_inc(S("h_act"), 1)
                act.wait_ge(*L(l, "h_act", 3))
                act.wait_ge(*L(l, "h_dve", 3))
                act.dma_start(h_rows.rearrange("(t p) d -> p t d", p=P), xn[:, :, :]).then_inc(S(f"L{l}_stored"), 16)

            def experts(l):
                def turned_tokens(j):
                    act.wait_ge(S(f"L{l}_x_tr"), j + 1)
                    a_.activation(hTe[:, 0:512], ps[:, 2, :], ACT.Copy).then_inc(S(f"L{l}_hTe_act"), 1)

                turned_tokens(0)
                n = act.value_load(table[0:1, l, T_ALL:T_ALL + 1], min_val=PAIRS, max_val=STEPS - 1)
                with act.Fori(0, n) as j:
                    act.wait_ge(S(f"L{l}_up_mm"), j + 1)
                    a_.activation(sil, ps[:, 0, 0:DE], ACT.Silu).then_inc(S(f"L{l}_silu"), 1)
                    turned_tokens(j + 1)
                    act.wait_ge(S(f"L{l}_hid_tr"), j + 1)
                    a_.activation(hidT, ps[:, 1, 0:DE].rearrange("p (c n) -> p c n", c=2), ACT.Copy) \
                        .then_inc(S(f"L{l}_hidT"), 1)
                    act.wait_ge(S(f"L{l}_ys"), j + 2)
                    act.nop()
                    act.dma_start(y_rows[bass.ds(j * P, P), :], ys).then_inc(S(f"L{l}_stored"), 16)
                act.wait_ge(S(f"L{l}_stored"), n * 16 + 16)
                act.sem_inc(S("all_stored"), 1)

            def gate_rows(l, k):
                for n in range(4):
                    act.wait_ge(*L(2 * l + k, "gate_rows_mm", n + 1))
                    a_.activation(ga[:, n // 2, (n % 2) * 512:(n % 2 + 1) * 512], ps[:, 6 + n % 2, :], ACT.Copy) \
                        .then_inc(S("gate_rows"), 1)

            act.wait_ge(S("early"), 16 * N_EARLY)
            act.wait_ge(S("cs32_zero"), 1)
            a_.activation(cs32[:, :, 0:2], condraw[:, :, :].rearrange("p r c -> p c r"), ACT.Silu).then_inc(S("cs32"), 1)
            norm_squares("early", 16 * N_EARLY)
            norm_evacuate(0, 0)
            for t in range(TILES):
                squares("v", ("v_mm", t + 1), vn[:, t, :], ps[:, t, :], ss[:, 3 + t:4 + t])
            for j in range(4):
                act.wait_ge(S("conv_mm"), j + 1)
                if j == 0:
                    act.wait_ge(S("zeros"), 1)
                    act.dma_start(y_rows[PAIRS * P:, :].rearrange("(s p) d -> p s d", p=P),
                                  zeros.unsqueeze(1).broadcast_to((P, STEPS - PAIRS, D))).then_inc(S("rows_written"), 16)
                if j:
                    act.wait_ge(S("gated"), j)
                a_.activation(gcs, ps[:, (3, 6)[j % 2], 0:T], ACT.Copy).then_inc(S("gate_c"), 1)
            act.wait_ge(S("sgu_tr"), 1)
            a_.activation(sguT, ps[:, 1, :].rearrange("p (g n) -> p g n", g=4), ACT.Copy).then_inc(S("sguT"), 1)
            gate_rows(0, 0)
            norm_squares("x1", 0)
            norm_evacuate(0, 1)
            by_tokens(0)
            router_exps(0)
            experts(0)
            gate_rows(0, 1)
            norm_squares("x2", 0)
            norm_evacuate(1, 0)
            for t in range(TILES):
                act.wait_ge(S("z_mm"), 2 * t + 2)
                ch.link(a_.activation(z[:, t, 512:Z_END], ps[:, 2 * t + 1, 0:Z_END - 512], ACT.Copy))
                act.sem_inc(S("z_high"), 1)
                squares("qc", ("z_low", t + 1), xn[:, t, 0:QL], z[:, t, Z_Q:Z_KV], ss[:, t:t + 1])
                squares("kvc", ("z_low", t + 1), xn[:, t, QL:QL + KVL], z[:, t, Z_KV:Z_PE], ss[:, 3 + t:4 + t])
            act.wait_ge(S("kvn"), 3)
            act.dma_start(new_ckv[0, 0], z[:, 0, Z_KV:Z_PE]).then_inc(S("new_kv"), 16)
            act.dma_start(new_kpe[0, 0], z[:, 0, Z_PE:Z_END]).then_inc(S("new_kv"), 16)
            for cc in range(3):
                act.wait_ge(S("qn_tr"), cc + 1)
                a_.activation(qnT[:, cc, :], ps[:, cc, 0:T], ACT.Copy, scale=qg[:, cc:cc + 1]).then_inc(S("qnT"), 1)
            for t in range(TILES):
                act.wait_ge(S("q_mm"), t + 1)
                for n, w in ((0, 512), (1, 512), (2, 128)):
                    ins = a_.activation(q[:, t, n * 512:n * 512 + w], ps[:, 3 * (t % 2) + n, 0:w], ACT.Copy)
                ins.then_inc(S("q_out"), 1)
            for h in range(NH):
                act.wait_ge(S("k_mm"), h + 1)
                a_.activation(kT[0:NOPE, h % 2, :], ps[0:NOPE, 0, :], ACT.Copy).then_inc(S("kT"), 1)
                act.wait_ge(S("nmax"), h + 1)
                for t in range(TILES):
                    s_ap, p_ap = scores(t), probs(t)
                    ins = a_.activation(p_ap, s_ap, ACT.Exp, bias=nmax[:, t:t + 1], scale=SCALE,
                                        accum_out=psum_of[:, t:t + 1])
                ins.then_inc(S("probs"), 1)
            gate_rows(1, 0)
            norm_squares("x1", TILES)
            norm_evacuate(1, 1)
            by_tokens(1)
            router_exps(1)
            experts(1)
            act.dma_start(finalg, row(final_norm_g, D)).then_inc(S("finalg"), 16)
            gate_rows(1, 1)
            norm_squares("x2", TILES)
            for t in range(TILES):
                act.wait_ge(S("y"), t + 1)
                act.dma_start(y_prompt[0] if t == 0 else y_sample[0, (t - 1) * P:t * P, :], xn[:, t, :]) \
                    .then_inc(S("stored"), 16)
            act.wait_ge(S("new_kv"), 32)
            act.wait_ge(S("stored"), 48)

        @block.vector
        def _(dve):
            v_ = nc.vector
            ch = Chain(dve, "dve_chain")
            link = ch.link

            def mod_round(l, i):
                dve.wait_ge(*L(3 * l + i, "mod_mm", 1))
                if l == 0 and i == 0:
                    dve.wait_ge(S("bias"), 16 * 16)
                v_.tensor_tensor(mrow[l][:, i, :], ps[:, 7, :], mrow[l][:, i, :], ALU.add).then_inc(S("mod_row"), 1)
                dve.wait_ge(*L(3 * l + i, "mod_cmm", 1))
                link(v_.tensor_copy(modcol[l][:, i].rearrange("p c v r -> p (c v r)"), ps[:, 6, 0:4 * DC]))
                dve.sem_inc(S("mod_col"), 1)
                if i != 1:
                    w, v = ((0, 1), None, (1, 0))[i]
                    v_.scalar_tensor_tensor(scg[l][:, w], modcol[l][:, i, :, v, :], 1.0,
                                            gcol[:, l, w, :].unsqueeze(2).broadcast_to((P, DC, 2)), ALU.add, ALU.mult) \
                        .then_inc(S("norm_cols"), 1)

            def normalise(k):
                for t in range(TILES):
                    dve.wait_ge(*L(k, "norm_root", t + 1))
                    v_.tensor_scalar(xn[:, t, :], x[:, t, :], rstd[:, t:t + 1], None, ALU.mult).then_inc(S("norm_xn"), 1)

            def norm_evacuate(l, w):
                scale, shift = norm_columns(l, w)
                dve.wait_ge(*L(2 * l + w, "norm_cols", 1))
                for t in range(TILES):
                    dve.wait_ge(*L(2 * l + w, "norm_tr", t + 1))
                    for cc in range(HT_ACT, DC):
                        ins = v_.tensor_scalar(hT[:, cc, t * P:(t + 1) * P], bank2(2 * t, D)[:, cc * P:(cc + 1) * P],
                                               scale(cc, cond_of(t)), shift(cc, cond_of(t)), ALU.mult, ALU.add)
                    ins.then_inc(S("norm_hT_dve"), 1)

            def project_out(l):
                dve.wait_ge(*L(2 * l + 0, "gate_rows", 4))
                for t in range(TILES):
                    for n in range(2):
                        dve.wait_ge(*L(l, "out_mm", 2 * t + n + 1))
                        link(v_.tensor_tensor(xn[:, t, n * 512:n * 512 + 512], ps[:, 2 * t + n, :],
                                              ga[:, cond_of(t), n * 512:n * 512 + 512], ALU.mult))
                    v_.tensor_tensor(x[:, t, :], x[:, t, :], xn[:, t, :], ALU.add).then_inc(S("x1"), 1)

            def first_of(dst, values, top):
                b = (P, TILES, 4)
                link(v_.tensor_tensor(R["cand"], values, top.broadcast_to(b), ALU.is_equal))
                link(v_.tensor_tensor(R["cand"], R["cand"], first.broadcast_to(b), ALU.mult))
                link(v_.tensor_reduce(R["cmax"], R["cand"], AX, ALU.max))
                link(v_.tensor_tensor(dst, R["cand"], R["cmax"].broadcast_to(b), ALU.is_equal))

            def router(l):
                b, b44 = (P, TILES, 4), (P, TILES, 4, 4)
                dve.wait_ge(S("rows_written"), 16)
                dve.wait_ge(*L(l, "router_mm", 1))
                link(v_.tensor_tensor(R["logits"], ps[:, 6, 0:TILES * 20].rearrange("p (t n) -> p t n", t=TILES),
                                      rb[:, l, :].unsqueeze(1).broadcast_to((P, TILES, 20)), ALU.add))
                glog, elog = R["logits"][:, :, 0:NG], R["logits"][:, :, NG:].rearrange("p t (g e) -> p t g e", g=NG)
                link(v_.tensor_reduce(R["gmax"], glog, AX, ALU.max))
                v_.tensor_tensor(R["gdiff"], glog, R["gmax"].broadcast_to(b), ALU.subtract).then_inc(S("gdiff"), 1)
                first_of(R["ghot"], glog, R["gmax"])
                link(v_.tensor_tensor(R["esel4"], elog, R["ghot"].unsqueeze(3).broadcast_to(b44), ALU.mult))
                link(v_.tensor_reduce(R["esel"], R["esel4"].rearrange("p t g e -> p t e g"), AX, ALU.add))
                link(v_.tensor_reduce(R["top1"], R["esel"], AX, ALU.max))
                first_of(R["hot1"], R["esel"], R["top1"])
                link(v_.scalar_tensor_tensor(R["rest"], R["hot1"], NEG, R["esel"], ALU.mult, ALU.add))
                link(v_.tensor_reduce(R["top2"], R["rest"], AX, ALU.max))
                v_.tensor_tensor(R["ediff"], R["top2"], R["top1"], ALU.subtract).then_inc(S("ediff"), 1)
                first_of(R["hot2"], R["rest"], R["top2"])
                dve.wait_ge(*L(l, "gexp", 1))
                link(v_.tensor_reduce(R["gsum"], R["gexp"], AX, ALU.add))
                dve.wait_ge(*L(l, "eexp", 1))
                link(v_.scalar_tensor_tensor(R["den"], R["eexp"], 1.0, R["gsum"], ALU.add, ALU.mult))
                link(v_.reciprocal(R["w1"], R["den"]))
                link(v_.tensor_tensor(R["w2"], R["w1"], R["eexp"], ALU.mult))
                link(v_.tensor_copy(R["weights"][:, :, 0:1], R["w1"]))
                link(v_.tensor_copy(R["weights"][:, :, 1:2], R["w2"]))

            def place_tokens(l):
                b44, b2n = (P, TILES, 4, 4), (P, TILES, 2, NE)
                for k, name in enumerate(("hot1", "hot2")):
                    link(v_.tensor_tensor(hot[:, :, k].rearrange("p t (g e) -> p t g e", g=NG),
                                          R["ghot"].unsqueeze(3).broadcast_to(b44), R[name].unsqueeze(2).broadcast_to(b44), ALU.mult))
                v_.tensor_tensor(R["mask"], hot[:, :, 0], hot[:, :, 1], ALU.add).then_inc(S("mask"), 1)
                dve.wait_ge(*L(l, "rank_mm", 1))
                most, rounds, s1, s2, s3 = (pairs[:, m, :] for m in range(5))
                link(v_.tensor_reduce(most, ps[:, 7, 48:64].rearrange("p (q e) -> p q e", e=2), AX, ALU.max))
                link(v_.tensor_scalar(rounds, most, float(HALF), 1.0, ALU.is_gt, ALU.add))
                for m in range(2, T // HALF):
                    link(v_.scalar_tensor_tensor(rounds, most, float(m * HALF), rounds, ALU.is_gt, ALU.add))
                for src, dst, d in ((rounds, s1, 1), (s1, s2, 2), (s2, s3, 4)):
                    v_.tensor_copy(dst[:, 0:d], src[:, 0:d])
                    link(v_.tensor_tensor(dst[:, d:], src[:, d:], src[:, 0:PAIRS - d], ALU.add))
                link(v_.tensor_tensor(s1, s3, rounds, ALU.subtract))
                v_.tensor_copy(table[:, l, T_CUM:T_CUM + PAIRS], s1)
                v_.tensor_copy(table[:, l, T_ROUNDS:T_END], rounds)
                v_.tensor_copy(table[:, l, T_ALL:T_ALL + 1], s3[:, PAIRS - 1:PAIRS]).then_inc(S("table"), 1)
                for name, of in (("rank", ps[:, 7, 0:48].rearrange("p (t n) -> p t n", t=TILES).unsqueeze(2).broadcast_to(b2n)),
                                 ("half", cst[:, C_HALF:C_HALF + NE].unsqueeze(1).unsqueeze(1).broadcast_to(b2n))):
                    link(v_.tensor_tensor(prod, hot, of, ALU.mult))
                    link(v_.tensor_reduce(R[name], prod, AX, ALU.add))
                for e in range(2):
                    link(v_.tensor_tensor(prod.rearrange("p t k (q e) -> p t k q e", e=2)[:, :, :, :, e].rearrange("p t k q -> p (t k) q"),
                                          hot.rearrange("p t k (q e) -> p t k q e", e=2)[:, :, :, :, e].rearrange("p t k q -> p (t k) q"),
                                          s1.unsqueeze(1).broadcast_to((P, 2 * TILES, PAIRS)), ALU.mult))
                link(v_.tensor_reduce(R["before"], prod, AX, ALU.add))
                link(v_.tensor_scalar(R["round"], R["rank"], float(HALF), None, ALU.is_ge))
                for m in range(2, T // HALF):
                    link(v_.scalar_tensor_tensor(R["round"], R["rank"], float(m * HALF), R["round"], ALU.is_ge, ALU.add))
                link(v_.tensor_tensor(R["step"], R["before"], R["round"], ALU.add))
                link(v_.scalar_tensor_tensor(R["place"], R["round"], -float(HALF), R["rank"], ALU.mult, ALU.add))
                link(v_.tensor_tensor(R["place"], R["place"], R["half"], ALU.add))
                link(v_.scalar_tensor_tensor(R["row"], R["step"], float(P), R["place"], ALU.mult, ALU.add))
                v_.tensor_copy(slot_of[:, :].rearrange("p (t k) -> p t k", k=2), R["row"])
                link(v_.tensor_tensor(place_hot, cst[:, C_IOTA:C_IOTA + P].unsqueeze(1).unsqueeze(1).broadcast_to((P, TILES, 2, P)),
                                      R["place"].unsqueeze(3).broadcast_to((P, TILES, 2, P)), ALU.is_equal))
                bs = (P, TILES, 2, STEPS)
                steps_hot = R["steps_hot"].rearrange("p t (k n) -> p t k n", k=2)
                rhs = R["steps_rhs"].rearrange("p t (v k n) -> p t v k n", v=2, k=2)
                link(v_.tensor_tensor(steps_hot, cst[:, C_IOTA:C_IOTA + STEPS].unsqueeze(1).unsqueeze(1).broadcast_to(bs),
                                      R["step"].unsqueeze(3).broadcast_to(bs), ALU.is_equal))
                link(v_.tensor_tensor(rhs[:, :, 0], steps_hot,
                                      cst[:, C_TOK:C_TOK + TILES].unsqueeze(2).unsqueeze(3).broadcast_to(bs), ALU.mult))
                v_.tensor_tensor(rhs[:, :, 1], steps_hot, R["weights"].unsqueeze(3).broadcast_to(bs), ALU.mult) \
                    .then_inc(S("onehot"), 1)
                dve.wait_ge(*L(l, "meta_mm", 1))
                v_.tensor_copy(idx[:, :], ps[:, 6, 0:STEPS])
                link(v_.tensor_copy(gate_in, ps[:, 6, STEPS:2 * STEPS]))
                dve.sem_inc(S("meta"), 1)

            def by_tokens(l):
                for t in range(TILES):
                    dve.wait_ge(*L(l, "h_tr", t + 1))
                    v_.tensor_copy(token_half(t, 1), ps[:, 2 * t + 1, :]) \
                        .then_inc(S("h_dve"), 1)

            def experts(l):
                def turned_tokens(j):
                    dve.wait_ge(S(f"L{l}_x_tr"), j + 1)
                    v_.tensor_copy(hTe[:, 512:D], ps[:, 3, :]).then_inc(S(f"L{l}_hTe_dve"), 1)

                turned_tokens(0)
                dve.sem_inc(S(f"L{l}_ys"), 1)
                n = dve.value_load(table[0:1, l, T_ALL:T_ALL + 1], min_val=PAIRS, max_val=STEPS - 1)
                with dve.Fori(0, n) as j:
                    dve.wait_ge(S(f"L{l}_silu"), j + 1)
                    v_.scalar_tensor_tensor(hid, ps[:, 0, DE:2 * DE], gate_in[:, bass.ds(j, 1)], sil, ALU.mult, ALU.mult) \
                        .then_inc(S(f"L{l}_hid"), 1)
                    turned_tokens(j + 1)
                    dve.wait_ge(S(f"L{l}_down_mm"), j + 1)
                    dve.wait_ge(S(f"L{l}_stored"), j * 16 + 16)
                    v_.tensor_copy(ys, bank2(4, D)).then_inc(S(f"L{l}_ys"), 1)

            def experts_out(l):
                dve.wait_ge(*L(2 * l + 1, "gate_rows", 4))
                dve.wait_ge(*L(l, "y_rows", 6 * 16))
                for t in range(TILES):
                    a, b = (yg[k][:, t * D:(t + 1) * D] for k in range(2))
                    link(v_.tensor_tensor(a, a, b, ALU.add))
                    link(v_.tensor_tensor(a, a, ga[:, cond_of(t), :], ALU.mult))
                    v_.tensor_tensor(x[:, t, :], x[:, t, :], a, ALU.add).then_inc(S("x2"), 1)

            dve.wait_ge(S("early"), 16 * N_EARLY)
            normalise(0)
            mod_round(0, 0)
            norm_evacuate(0, 0)
            for t in range(TILES):
                dve.wait_ge(S("v_root"), t + 1)
                v_.tensor_scalar(vn[:, t, :], ps[:, t, :], rstd[:, 3 + t:4 + t], None, ALU.mult).then_inc(S("vn"), 1)
            dve.wait_ge(S("late"), 16 * (N_LATE + 4))
            for j in range(4):
                b = (3, 6)[j % 2]
                b1, b2 = b + 1, (b + 2) % 8
                dve.wait_ge(S("gate_c"), j + 1)
                ins = v_.tensor_tensor(pr, gcs, ps[:, b1, 0:T], ALU.mult)
                link(ins)
                dve.sem_inc(S("gated"), 1)
                link(v_.tensor_scalar(cv, pr, convw[:, 1, j:j + 1], None, ALU.mult))
                for a, n in ((0, P), (P, 2 * P)):
                    link(v_.scalar_tensor_tensor(cv[:, a + 1:a + n], pr[:, a:a + n - 1], convw[:, 0, j:j + 1],
                                                 cv[:, a + 1:a + n], ALU.mult, ALU.add))
                    link(v_.scalar_tensor_tensor(cv[:, a:a + n - 1], pr[:, a + 1:a + n], convw[:, 2, j:j + 1],
                                                 cv[:, a:a + n - 1], ALU.mult, ALU.add))
                v_.tensor_tensor(yT[:, j, :], cv, ps[:, b2, 0:T], ALU.mult).then_inc(S("y_conv"), 1)
            for g in range(4):
                dve.wait_ge(S("sgu_mm"), g + 1)
                link(v_.scalar_tensor_tensor(sv.rearrange("p (t n) -> p t n", t=TILES),
                                             ps[:, (1, 4)[g % 2], 0:T].rearrange("p (t n) -> p t n", t=TILES),
                                             sgug[:, g:g + 1], sgub[:, g, :].unsqueeze(1).broadcast_to((P, TILES, P)),
                                             ALU.mult, ALU.add))
                link(v_.tensor_tensor(yT[:, 4 + g, :], sv, ps[:, (2, 3)[g % 2], 0:T], ALU.mult))
                dve.sem_inc(S("y_sgu"), 1)
            mod_round(0, 1)
            project_out(0)
            mod_round(0, 2)
            normalise(1)
            norm_evacuate(0, 1)
            by_tokens(0)
            router(0)
            place_tokens(0)
            experts(0)
            experts_out(0)
            mod_round(1, 0)
            normalise(2)
            norm_evacuate(1, 0)

            for t in range(TILES):
                dve.wait_ge(S("z_mm"), 2 * t + 1)
                v_.tensor_copy(z[:, t, 0:512], ps[:, 2 * t, :]).then_inc(S("z_low"), 1)
            for t in range(TILES):
                dve.wait_ge(S("qc_root"), t + 1)
                v_.tensor_scalar(z[:, t, Z_Q:Z_KV], z[:, t, Z_Q:Z_KV], rstd[:, t:t + 1], None, ALU.mult).then_inc(S("qn"), 1)
                dve.wait_ge(S("kvc_root"), t + 1)
                v_.scalar_tensor_tensor(z[:, t, Z_KV:Z_PE], z[:, t, Z_KV:Z_PE], rstd[:, 3 + t:4 + t], kvg, ALU.mult, ALU.mult) \
                    .then_inc(S("kvn"), 1)

            def rotate(dst, src, t, tmp):
                shape = tuple(src.shape[:-2]) + (8,)
                cos = cst[:, C_COS + 16 * (t - 1):C_COS + 16 * t].rearrange("p (k n) -> p k n", k=2)
                sin = cst[:, C_SIN + 16 * (t - 1):C_SIN + 16 * t].rearrange("p (k n) -> p k n", k=2)
                if len(shape) == 4:
                    cos, sin = cos.unsqueeze(1).broadcast_to(shape), sin.unsqueeze(1).broadcast_to(shape)
                    first_half, second_half = src[:, :, :, 0, :], src[:, :, :, 1, :]
                    out1, out2 = dst[:, :, :, 0, :], dst[:, :, :, 1, :]
                else:
                    first_half, second_half, out1, out2 = src[:, :, 0, :], src[:, :, 1, :], dst[:, :, 0, :], dst[:, :, 1, :]
                v_.tensor_tensor(tmp[0], first_half, cos, ALU.mult)
                v_.tensor_tensor(tmp[1], second_half, sin, ALU.mult)
                v_.tensor_tensor(tmp[2], second_half, cos, ALU.mult)
                link(v_.tensor_tensor(tmp[3], first_half, sin, ALU.mult))
                v_.tensor_tensor(out1, tmp[0], tmp[1], ALU.subtract)
                link(v_.tensor_tensor(out2, tmp[2], tmp[3], ALU.add))

            dve.wait_ge(S("z_high"), 3)
            link(v_.tensor_copy(kpe[:, 0, :], z[:, 0, Z_PE:Z_END]))
            for t in (1, 2):
                rotate(kpe[:, t + 1, :].rearrange("p (k a n) -> p k a n", k=2, a=2),
                       z[:, t, Z_PE:Z_END].rearrange("p (k a n) -> p k a n", k=2, a=2), t,
                       [ktmp[:, k, :].rearrange("p (k n) -> p k n", k=2) for k in range(4)])
            dve.sem_inc(S("kpe"), 1)
            for j in range(2):
                dve.wait_ge(S("four_tok_mm"), j + 1)
                b = (6, 4)[j]
                v_.tensor_copy(fmid[j][:, :, 0:P], ps[:, b, 0:2 * P].rearrange("p (k n) -> p k n", k=2))
                v_.tensor_copy(fmid[j][:, :, P:T], ps[:, b + 1, :].rearrange("p (k n) -> p k n", k=2)) \
                    .then_inc(S("fmid"), 1)
            for cc in range(2):
                dve.wait_ge(S("kv_tr"), cc + 1)
                v_.tensor_copy(kvT[:, cc, :], ps[:, 3 + cc, :]).then_inc(S("kvT"), 1)
            dve.wait_ge(S("kpe_tr"), 1)
            dve.wait_ge(S("four_mm"), 1)
            for b in range(2):
                ins = v_.tensor_copy(kT[NOPE:QH, b, :], ps[NOPE:QH, 5, :])
            ins.then_inc(S("kpeT"), 1)
            for j in range(2):
                ins = v_.tensor_copy(yT[:, j, :], ps[:, 6 + j, 0:T])
            ins.then_inc(S("y_four"), 1)
            for t in (1, 2):
                dve.wait_ge(S("q_out"), t + 1)
                qpe = q[:, t, :].rearrange("p (h n) -> p h n", h=NH)[:, :, NOPE:QH].rearrange("p h (k a n) -> p h k a n", k=2, a=2)
                for k in range(2):
                    cos = cst[:, C_COS + 16 * (t - 1) + 8 * k:C_COS + 16 * (t - 1) + 8 * k + 8].unsqueeze(1).broadcast_to((P, NH, 8))
                    sin = cst[:, C_SIN + 16 * (t - 1) + 8 * k:C_SIN + 16 * (t - 1) + 8 * k + 8].unsqueeze(1).broadcast_to((P, NH, 8))
                    one, two = qpe[:, :, k, 0, :], qpe[:, :, k, 1, :]
                    tmp = [rtmp[:, m, 0:96].rearrange("p (h n) -> p h n", h=NH) for m in range(4)]
                    v_.tensor_tensor(tmp[0], one, cos, ALU.mult)
                    v_.tensor_tensor(tmp[1], two, sin, ALU.mult)
                    v_.tensor_tensor(tmp[2], two, cos, ALU.mult)
                    link(v_.tensor_tensor(tmp[3], one, sin, ALU.mult))
                    v_.tensor_tensor(one, tmp[0], tmp[1], ALU.subtract)
                    link(v_.tensor_tensor(two, tmp[2], tmp[3], ALU.add))
            dve.sem_inc(S("q_rot"), 1)
            for kt in range(4):
                dve.wait_ge(S("v2_mm"), kt + 1)
                v_.tensor_copy(vv[:, kt, :], bank2((6, 3)[kt % 2], NH * VD)).then_inc(S("vv"), 1)

            def head_probs_out(h):
                dve.wait_ge(S("probs"), h + 1)
                if h:
                    dve.wait_ge(S("o_out"), h)
                v_.reciprocal(pinv, psum_of)
                dve.wait_ge(S("p_tr"), h + 1)
                v_.tensor_copy(prT, bank2(4, 7 * P)).then_inc(S("pT"), 1)

            def head_out(h):
                dve.wait_ge(S("o_mm"), h + 1)
                v_.tensor_tensor(o[:, :, h * VD:(h + 1) * VD], ps[:, 6 + h % 2, 0:3 * VD].rearrange("p (t n) -> p t n", t=3),
                                 pinv.unsqueeze(2).broadcast_to((P, 3, VD)), ALU.mult).then_inc(S("o_out"), 1)

            dve.wait_ge(S("new_kv"), 32)
            for h in range(NH):
                dve.wait_ge(S("qT_tr"), h + 1)
                v_.tensor_copy(qT[0:QH, h % 2, :], ps[0:QH, 1, 0:T]).then_inc(S("qT"), 1)
                if h:
                    head_probs_out(h - 1)
                dve.wait_ge(S("s_mm"), h + 1)
                for t in range(TILES):
                    ins = v_.tensor_reduce(nmax[:, t:t + 1], scores(t), AX, ALU.max)
                link(ins)
                v_.tensor_scalar(nmax, nmax, -SCALE, None, ALU.mult).then_inc(S("nmax"), 1)
                if h:
                    head_out(h - 1)
            head_probs_out(NH - 1)
            head_out(NH - 1)
            mod_round(1, 1)
            for t in range(TILES):
                dve.wait_ge(S("o_tr"), t + 1)
                v_.tensor_copy(yT[:, 2:DC, t * P:(t + 1) * P], bank2(2 * t, 6 * P).rearrange("p (k n) -> p k n", k=6)) \
                    .then_inc(S("y_att"), 1)
            project_out(1)
            mod_round(1, 2)
            normalise(3)
            norm_evacuate(1, 1)
            by_tokens(1)
            router(1)
            place_tokens(1)
            experts(1)
            experts_out(1)
            dve.wait_ge(S("finalg"), 16)
            for t in range(TILES):
                dve.wait_ge(*L(4, "norm_root", t + 1))
                v_.scalar_tensor_tensor(xn[:, t, :], x[:, t, :], rstd[:, t:t + 1], finalg, ALU.mult, ALU.mult) \
                    .then_inc(S("y"), 1)

        @block.tensor
        def _(pe):
            mm, tr = nc.tensor.matmul, nc.tensor.transpose

            def mod_round(l, i):
                for j in range(4):
                    arrived(pe, f"mod{l}.{4 * i + j}")
                w = [weight(f"mod{l}.{4 * i + j}", DC, 512) for j in range(4)]
                for cc in range(DC):
                    for j in range(4):
                        ins = mm(ps[32 * j:32 * j + 32, 7, :], cs32[:, cc, :], w[j][:, cc, :], start=cc == 0, stop=cc == DC - 1)
                ins.then_inc(S("mod_mm"), 1)
                pe.wait_ge(*L(3 * l + i, "mod_row", 1))
                pick = ident.rearrange("p (v h a) -> p h v a", v=2, h=2)
                for cc in range(DC):
                    for h in range(2):
                        ins = mm(ps[64 * h:64 * h + 64, 6, 4 * cc:4 * cc + 4], mrow[l][:, i, cc::DC], pick[:, h, :, 0:2],
                                 start=True, stop=True)
                ins.then_inc(S("mod_cmm"), 1)

            def norm_transposes(l, w):
                for t in range(TILES):
                    pe.wait_ge(*L(2 * l + w, "norm_xn", t + 1))
                    for cc in range(DC):
                        ins = tr(bank2(2 * t, D)[:, cc * P:(cc + 1) * P], xn[:, t, cc::DC], ident)
                    ins.then_inc(S("norm_tr"), 1)

            def wait_hT(l, w, n=TILES):
                pe.wait_ge(*L(2 * l + w, "norm_hT_act", n))
                pe.wait_ge(*L(2 * l + w, "norm_hT_dve", n))

            def gate_rows(l, k):
                i, v = ((1, 0), (2, 1))[k]
                for n in range(4):
                    r, half = n // 2, n % 2
                    if n >= 2:
                        pe.wait_ge(*L(2 * l + k, "gate_rows", n - 1))
                    at = 64 * v + 32 * half + r
                    mm(ps[:, 6 + n % 2, :], ident[:, at:at + 1].broadcast_to((P, P)), mrow[l][:, i, :], start=True, stop=True) \
                        .then_inc(S("gate_rows_mm"), 1)

            def project_out(l, parts):
                for t in range(TILES):
                    for n in range(2):
                        for k in range(DC):
                            ins = mm(ps[:, 2 * t + n, :], yT[:, k, t * P:(t + 1) * P],
                                     weight(parts[k // 4], 4, D)[:, k % 4, n * 512:n * 512 + 512], start=k == 0, stop=k == DC - 1)
                        ins.then_inc(S("out_mm"), 1)

            def router(l):
                pe.wait_ge(S("late"), 16 * (N_LATE + 4))
                for t in range(TILES):
                    for at, w, n in ((0, wg, NG), (NG, we, NE)):
                        for cc in range(DC):
                            ins = mm(ps[:, 6, 20 * t + at:20 * t + at + n], hT[:, cc, t * P:(t + 1) * P], w[:, l, cc, :],
                                     start=cc == 0, stop=cc == DC - 1)
                ins.then_inc(S("router_mm"), 1)

            def by_tokens(l):
                for t in range(TILES):
                    wait_hT(l, 1, t + 1)
                    for cc in range(DC):
                        ins = tr(bank2(2 * t, D)[:, cc * P:(cc + 1) * P], hT[:, cc, t * P:(t + 1) * P], ident)
                    ins.then_inc(S("h_tr"), 1)

            def place_tokens(l):
                pe.wait_ge(*L(l, "mask", 1))
                ones = cst[:, C_ONE:C_ONE + 1].broadcast_to((P, P))
                for t in range(TILES + 1):
                    for s in range(min(t + 1, TILES)):
                        ins = mm(ps[:, 7, NE * t:NE * (t + 1)], cst[:, C_TRI:C_TRI + P] if s == t else ones, R["mask"][:, s, :],
                                 start=s == 0, stop=s == min(t, TILES - 1))
                ins.then_inc(S("rank_mm"), 1)
                pe.wait_ge(*L(l, "onehot", 1))
                rhs = R["steps_rhs"].rearrange("p t (v k n) -> p t v k n", v=2, k=2)
                for t in range(TILES):
                    for k in range(2):
                        ins = mm(ps[:, 6, 0:2 * STEPS], place_hot[:, t, k, :], rhs[:, t, :, k, :],
                                 start=(t, k) == (0, 0), stop=(t, k) == (TILES - 1, 1))
                ins.then_inc(S("meta_mm"), 1)

            def experts(l):
                before = places[l][1]

                def turn_tokens(j):
                    pe.wait_ge(S(f"L{l}_gathered"), j * 16 + 16)
                    for cc in range(DC):
                        ins = tr(bank2(2, D)[:, cc * P:(cc + 1) * P], xg[:, cc * P:(cc + 1) * P], ident)
                    ins.then_inc(S(f"L{l}_x_tr"), 1)

                def step(j, u):
                    w13 = [pool[:, 3 * (2 * u + e) * SLOT:(3 * (2 * u + e) + 2) * SLOT]
                           .rearrange("p (k c n) -> p k c n", k=2, c=DC) for e in range(2)]
                    w2 = [pool[:, (3 * (2 * u + e) + 2) * SLOT:3 * (2 * u + e + 1) * SLOT]
                          .rearrange("p (c n) -> p c n", c=2) for e in range(2)]
                    halves = [slice(e * HALF, (e + 1) * HALF) for e in range(2)]
                    pe.wait_ge(S(f"L{l}_hTe_act"), j + 1)
                    pe.wait_ge(S(f"L{l}_hTe_dve"), j + 1)
                    for cc in range(DC):
                        for e, m in enumerate(halves):
                            ins = mm(ps[m, 0, :], hTe.rearrange("p (c n) -> p c n", c=DC)[:, cc, m], w13[e][:, :, cc, :],
                                     start=cc == 0, stop=cc == DC - 1)
                    ins.then_inc(S(f"L{l}_up_mm"), 1)
                    turn_tokens(j + 1)
                    pe.wait_ge(S(f"L{l}_hid"), j + 1)
                    for cc in range(2):
                        ins = tr(ps[:, 1, cc * P:(cc + 1) * P], hid[:, cc::2], ident)
                    ins.then_inc(S(f"L{l}_hid_tr"), 1)
                    pe.wait_ge(S(f"L{l}_hidT"), j + 1)
                    pe.wait_ge(S(f"L{l}_ys"), j + 1)
                    for n in range(2):
                        for cc in range(2):
                            for e, m in enumerate(halves):
                                ins = mm(ps[m, 4 + n, :], hidT[:, cc, m], w2[e][:, cc, n * 512:n * 512 + 512],
                                         start=cc == 0, stop=cc == 1)
                    ins.then_inc(S(f"L{l}_down_mm"), 1)

                turn_tokens(0)
                with pe.Fori(0, TURNS) as i:
                    for u in range(UNROLL):
                        for s in range(6 * u, 6 * u + 6):
                            pe.wait_ge(S(f"slot{s}"), i * 16 + 16 * (before[s] + 1))
                        pe.nop()
                        so_far = pe.value_load(table[0:1, l, bass.ds(i * UNROLL + (T_CUM + u), 1)], min_val=0, max_val=STEPS)
                        rounds = pe.value_load(table[0:1, l, bass.ds(i * UNROLL + (T_ROUNDS + u), 1)], min_val=1, max_val=T // HALF)
                        with pe.Fori(0, rounds) as r:
                            step(so_far + r, u)
                n = pe.value_load(table[0:1, l, T_ALL:T_ALL + 1], min_val=PAIRS, max_val=STEPS)
                pe.wait_ge(S(f"L{l}_ys"), n + 1)
                pe.nop()

            pe.wait_ge(S("cs32"), 1)
            mod_round(0, 0)
            norm_transposes(0, 0)
            wait_hT(0, 0)
            arrived(pe, "v")
            for t in range(TILES):
                for cc in range(DC):
                    ins = mm(ps[:, t, :], hT[:, cc, t * P:(t + 1) * P], weight("v", DC, 512)[:, cc, :], start=cc == 0, stop=cc == DC - 1)
                ins.then_inc(S("v_mm"), 1)
            pe.wait_ge(*L(0, "mod_col", 1))
            for name in ("gate_c", "xa", "gate_b"):
                arrived(pe, name)
            for j in range(4):
                if j == 1:
                    pe.wait_ge(S("vn"), 1)
                if j >= 2:
                    pe.wait_ge(S("y_conv"), j - 1)
                for k, name in enumerate(("gate_c", "xa", "gate_b")):
                    for cc in range(DC):
                        ins = mm(ps[:, ((3, 6)[j % 2] + k) % 8, 0:T], weight(name, DC, 512)[:, cc, j::4], hT[:, cc, :],
                                 start=cc == 0, stop=cc == DC - 1)
                ins.then_inc(S("conv_mm"), 1)
            pe.wait_ge(S("vn"), 3)
            pe.wait_ge(S("late"), 16 * (N_LATE + 4))
            for g in range(4):
                ins = tr(ps[:, 1, g * P:(g + 1) * P], sguw[:, g, :], ident)
            ins.then_inc(S("sgu_tr"), 1)
            arrived(pe, "u")
            for g in range(4):
                bs, bu = (1, 4)[g % 2], (2, 3)[g % 2]
                if g == 1:
                    pe.wait_ge(S("y_conv"), 3)
                if g >= 2:
                    pe.wait_ge(S("y_sgu"), g - 1)
                for cc in range(DC):
                    mm(ps[:, bu, 0:T], weight("u", DC, 512)[:, cc, g * P:(g + 1) * P], hT[:, cc, :], start=cc == 0, stop=cc == DC - 1)
                pe.wait_ge(S("sguT"), 1)
                for t in range(TILES):
                    ins = mm(ps[:, bs, t * P:(t + 1) * P], vn[:, t, g * P:(g + 1) * P], sguT[:, g, :], start=True, stop=True)
                ins.then_inc(S("sgu_mm"), 1)
            pe.wait_ge(S("y_conv"), 4)
            pe.wait_ge(S("y_sgu"), 4)
            mod_round(0, 1)
            pe.wait_ge(*L(1, "mod_col", 1))
            gate_rows(0, 0)
            arrived(pe, "out0.0")
            arrived(pe, "out0.1")
            project_out(0, ("out0.0", "out0.1"))
            pe.wait_ge(*L(0, "gate_rows", 4))
            mod_round(0, 2)
            norm_transposes(0, 1)
            pe.wait_ge(*L(2, "mod_col", 1))
            by_tokens(0)
            router(0)
            place_tokens(0)
            experts(0)
            gate_rows(0, 1)
            pe.wait_ge(*L(1, "gate_rows", 4))
            mod_round(1, 0)
            norm_transposes(1, 0)

            wait_hT(1, 0)
            for half in range(2):
                arrived(pe, f"in1.{half}")
                w = weight(f"in1.{half}", 4, Z_END)
                for t in range(TILES):
                    for b, lo, hi in ((2 * t, 0, 512), (2 * t + 1, 512, Z_END)):
                        for k in range(4):
                            cc = 4 * half + k
                            ins = mm(ps[:, b, 0:hi - lo], hT[:, cc, t * P:(t + 1) * P], w[:, k, lo:hi], start=cc == 0, stop=cc == DC - 1)
                        if half:
                            ins.then_inc(S("z_mm"), 1)
            pe.wait_ge(S("z_low"), 3)
            pe.wait_ge(S("z_high"), 3)
            pe.wait_ge(*L(3, "mod_col", 1))
            for j in range(2):
                b = (6, 4)[j]
                mm(ps[:, b, 0:2 * P], z[:, 0, j * P:(j + 1) * P], cst[:, C_CS1:C_CS2], start=True, stop=True)
                for t in (1, 2):
                    ins = mm(ps[:, b + 1, :], z[:, t, j * P:(j + 1) * P], cst[:, C_CS2 + 512 * (t - 1):C_CS2 + 512 * t],
                             start=t == 1, stop=t == 2)
                ins.then_inc(S("four_tok_mm"), 1)
            pe.wait_ge(S("qn"), 3)
            for cc in range(3):
                for t in range(TILES):
                    ins = tr(ps[:, cc, t * P:(t + 1) * P], z[:, t, Z_Q + cc:Z_KV:3], ident)
                ins.then_inc(S("qn_tr"), 1)
            pe.wait_ge(S("kvn"), 3)
            pe.wait_ge(S("fmid"), 2)
            for cc in range(2):
                for kt in range(4):
                    src = ckv[:, cc::2] if kt == 1 else z[:, (0, None, 1, 2)[kt], Z_KV + cc:Z_PE:2]
                    ins = tr(ps[:, 3 + cc, kt * P:(kt + 1) * P], src, ident)
                ins.then_inc(S("kv_tr"), 1)
            pe.wait_ge(S("kpe"), 1)
            for kt in range(4):
                ins = mm(ps[NOPE:QH, 5, kt * P:(kt + 1) * P], kpe[:, kt, :], ident, start=True, stop=True)
            ins.then_inc(S("kpe_tr"), 1)
            for j in range(2):
                for k in range(2):
                    ins = mm(ps[:, 6 + j, 0:T], cst[:, C_CC + P * k:C_CC + P * (k + 1)], fmid[j][:, k, :], start=k == 0, stop=k == 1)
            ins.then_inc(S("four_mm"), 1)
            pe.wait_ge(S("qnT"), 3)
            arrived(pe, "uq")
            for t in range(TILES):
                if t == 1:
                    pe.wait_ge(S("kvT"), 2)
                    pe.wait_ge(S("kpeT"), 1)
                if t == 2:
                    pe.wait_ge(S("q_out"), 1)
                for n, w in ((0, 512), (1, 512), (2, 128)):
                    for cc in range(3):
                        ins = mm(ps[:, 3 * (t % 2) + n, 0:w], qnT[:, cc, t * P:(t + 1) * P],
                                 weight("uq", 3, NH * QH)[:, cc, n * 512:n * 512 + w], start=cc == 0, stop=cc == 2)
                ins.then_inc(S("q_mm"), 1)
            arrived(pe, "ukv")
            ukv = weight("ukv", 2, NH * 2 * VD).rearrange("p c (h n) -> p c h n", h=NH)
            pe.wait_ge(S("y_four"), 1)
            for kt in range(4):
                if kt == 1:
                    pe.wait_ge(S("q_out"), 2)
                if kt >= 2:
                    pe.wait_ge(S("vv"), kt - 1)
                for n, h0, h1 in ((0, 0, 8), (1, 8, NH)):
                    for cc in range(2):
                        ins = mm(ps[:, (6, 3)[kt % 2] + n, 0:(h1 - h0) * VD], kvT[:, cc, kt * P:(kt + 1) * P],
                                 ukv[:, cc, h0:h1, NOPE:NOPE + VD], start=cc == 0, stop=cc == 1)
                ins.then_inc(S("v2_mm"), 1)
            pe.wait_ge(S("q_rot"), 1)
            pe.wait_ge(S("q_out"), 3)
            pe.wait_ge(S("vv"), 4)
            pe.wait_ge(S("kpeT"), 1)

            def head_probs(h):
                pe.wait_ge(S("probs"), h + 1)
                for m in range(7):
                    ins = tr(bank2(4, 7 * P)[:, m * P:(m + 1) * P], pr_s[:, m * P:(m + 1) * P], ident)
                ins.then_inc(S("p_tr"), 1)

            def head_values(h):
                pe.wait_ge(S("pT"), h + 1)
                if h >= 2:
                    pe.wait_ge(S("o_out"), h - 1)
                for t in range(TILES):
                    keys = ((0, 0),) if t == 0 else tuple((1 + k, 1 + 3 * (t - 1) + k) for k in range(3))
                    for n, (kt, m) in enumerate(keys):
                        ins = mm(ps[:, 6 + h % 2, t * VD:(t + 1) * VD], prT[:, m * P:(m + 1) * P],
                                 vv[:, kt, h * VD:(h + 1) * VD], start=n == 0, stop=n == len(keys) - 1)
                ins.then_inc(S("o_mm"), 1)

            for h in range(NH):
                if h:
                    pe.wait_ge(S("kT"), h)
                for cc in range(2):
                    ins = mm(ps[0:NOPE, 0, :], ukv[:, cc, h, 0:NOPE], kvT[:, cc, :], start=cc == 0, stop=cc == 1)
                ins.then_inc(S("k_mm"), 1)
                if h:
                    pe.wait_ge(S("qT"), h)
                for t in range(TILES):
                    ins = tr(ps[0:QH, 1, t * P:(t + 1) * P], q[:, t, h * QH:(h + 1) * QH], ident)
                ins.then_inc(S("qT_tr"), 1)
                if h:
                    head_probs(h - 1)
                pe.wait_ge(S("kT"), h + 1)
                pe.wait_ge(S("qT"), h + 1)
                for t in range(TILES):
                    ins = mm(scores(t), qT[0:QH, h % 2, t * P:(t + 1) * P], kT[0:QH, h % 2, 0:P] if t == 0 else kT[0:QH, h % 2, P:512],
                             start=True, stop=True)
                ins.then_inc(S("s_mm"), 1)
                if h:
                    head_values(h - 1)
            head_probs(NH - 1)
            head_values(NH - 1)
            pe.wait_ge(S("o_out"), NH)
            mod_round(1, 1)
            for t in range(TILES):
                for k in range(6):
                    ins = tr(bank2(2 * t, 6 * P)[:, k * P:(k + 1) * P], o[:, t, k * P:(k + 1) * P], ident)
                ins.then_inc(S("o_tr"), 1)
            pe.wait_ge(*L(4, "mod_col", 1))
            gate_rows(1, 0)
            pe.wait_ge(S("y_att"), 3)
            arrived(pe, "out1.0")
            arrived(pe, "out1.1")
            project_out(1, ("out1.0", "out1.1"))
            pe.wait_ge(*L(2, "gate_rows", 4))
            mod_round(1, 2)
            norm_transposes(1, 1)
            pe.wait_ge(*L(5, "mod_col", 1))
            by_tokens(1)
            router(1)
            place_tokens(1)
            experts(1)
            gate_rows(1, 1)


def constants():
    import numpy as np

    out = np.zeros((P, C_END), np.float64)
    out[:, C_ID:C_ID + P] = np.eye(P)
    p = np.arange(P)
    gw = DCF // 4
    for at, n, tiles in ((C_CS1, P, 1), (C_CS2, 2 * P, 2)):
        for k in range(tiles):
            ang = 2 * np.pi * ((np.outer(p + k * P, np.arange(n))) % n) / n
            scale = 1.0 / np.sqrt(n * gw)
            out[:, at + 2 * n * k:at + 2 * n * k + n] = np.cos(ang) * scale
            out[:, at + 2 * n * k + n:at + 2 * n * (k + 1)] = np.sin(ang) * scale
    ang = 2 * np.pi * (np.outer(p, p) % gw) / gw
    same = (p[:, None] // gw) == (p[None, :] // gw)
    out[:, C_CC:C_CC + P] = np.cos(ang) * same
    out[:, C_CC + P:C_CC + 2 * P] = -np.sin(ang) * same
    nf = ROPE // 4
    inv = (10000.0 ** (-np.arange(nf, dtype=np.float32) / np.float32(nf))).astype(np.float32)
    for t in range(2):
        tok = t * P + p
        for k, pos in enumerate((tok // GRID_W, tok % GRID_W)):
            ang = (pos.astype(np.float32)[:, None] * inv[None, :]).astype(np.float32)
            out[:, C_COS + 16 * t + 8 * k:C_COS + 16 * t + 8 * k + 8] = np.cos(ang)
            out[:, C_SIN + 16 * t + 8 * k:C_SIN + 16 * t + 8 * k + 8] = np.sin(ang)
    out[:, C_FIRST:C_TRI] = np.arange(4, 0, -1)
    out[:, C_TRI:C_IOTA] = p[:, None] < p[None, :]
    out[:, C_IOTA:C_TOK] = p
    out[:, C_TOK:C_HALF] = p[:, None] + P * np.arange(TILES)
    out[:, C_HALF:C_ONE] = HALF * (np.arange(NE) % 2)
    out[:, C_ONE] = 1
    return out.astype(np.float32)


INS = ["x_prompt", "x_sample", "cache_ckv", "cache_kpe", "c", "c_ctx", "mod_w", "mod_b", "norm1_g", "norm2_g",
       "ev_w_in", "ev_conv_w", "ev_sgu_norm_g", "ev_sgu_w", "ev_sgu_b", "ev_w_out", "od_w_in", "od_q_norm_g",
       "od_w_uq", "od_kv_norm_g", "od_w_ukv", "od_w_out", "moe_wg", "moe_bg", "moe_we", "moe_be", "moe_w1",
       "moe_w3", "moe_w2", "final_norm_g"]
OUTS = [(1, P, D), (1, 2 * P, D), (1, 1, P, KVL), (1, 1, P, ROPE)]


def kernel(**inputs):
    import numpy as np
    import concourse.bacc as bacc
    from concourse.bass_utils import run_bass_kernel_spmd

    nc = bacc.Bacc("TRN2", target_bir_lowering=False, num_devices=1)
    arrays, args = {}, []
    for name in INS:
        a = np.ascontiguousarray(inputs[name])
        arrays[f"in_{name}"] = a
        args.append(nc.dram_tensor(f"in_{name}", a.shape, F32, kind="ExternalInput").ap())
    arrays["in_consts"] = constants()
    args.append(nc.dram_tensor("in_consts", (P, C_END), F32, kind="ExternalInput").ap())
    for i, shape in enumerate(OUTS):
        args.append(nc.dram_tensor(f"out_{i}", shape, F32, kind="ExternalOutput").ap())
    program(nc, *args)
    r = run_bass_kernel_spmd(nc, [arrays], core_ids=[0])
    return tuple(r.results[0][f"out_{i}"] for i in range(len(OUTS)))
```

```python
from contextlib import ExitStack

import concourse.bass as bass
from concourse import mybir

F32 = mybir.dt.float32
I32 = mybir.dt.int32
ALU = mybir.AluOpType
ACT = mybir.ActivationFunctionType
AX = mybir.AxisListType.X

P = 128
D = 1024
DC = D // P
TILES = 3
T = TILES * P
GRID_W = 64
EPS = 1e-6
NH, NOPE, ROPE, VD = 12, 64, 32, 64
QH = NOPE + ROPE
QL, KVL, DCF = 384, 256, 256
Z_Q, Z_KV, Z_PE, Z_END = DCF, DCF + QL, DCF + QL + KVL, DCF + QL + KVL + ROPE
NE, NG, EPG, DE = 16, 4, 4, 256
SLOT = 2048
NSLOT = 12
HALF = P // 2
PAIRS = NE // 2
UNROLL = 2
TURNS = PAIRS // UNROLL
STEPS = PAIRS + (2 * T - PAIRS) // HALF + 1
T_CUM, T_ALL, T_ROUNDS, T_END = 0, 8, 9, 17
SCALE = float(QH) ** -0.5
NEG = -3.0e38
FAR = 65536.0

C_ID, C_CS1, C_CS2, C_CC, C_COS, C_SIN, C_FIRST = 0, 128, 384, 1408, 1664, 1696, 1728
C_TRI, C_IOTA, C_TOK, C_HALF, C_ONE, C_OVER = 1732, 1860, 1988, 1994, 2010, 2011
C_END = C_OVER + STEPS + 1


def cond_of(tile):
    return 0 if tile == 0 else 1


def program(nc, x_prompt, x_sample, cache_ckv, cache_kpe, c, c_ctx, mod_w, mod_b, norm1_g, norm2_g,
            ev_w_in, ev_conv_w, ev_sgu_norm_g, ev_sgu_w, ev_sgu_b, ev_w_out, od_w_in, od_q_norm_g,
            od_w_uq, od_kv_norm_g, od_w_ukv, od_w_out, moe_wg, moe_bg, moe_we, moe_be, moe_w1,
            moe_w3, moe_w2, final_norm_g, consts, y_prompt, y_sample, new_ckv, new_kpe):
    with ExitStack() as ctx:
        def sb(name, shape, dtype=F32):
            return ctx.enter_context(nc.sbuf_tensor(name, shape, dtype))

        sems = {}

        def S(name):
            if name not in sems:
                sems[name] = ctx.enter_context(nc.semaphore(name))
            return sems[name]

        TIMES = dict(mod_mm=1, mod_row=1, mod_cmm=1, mod_col=1, norm_root=3, norm_xn=3, norm_tr=3, norm_hT_act=3,
                     norm_hT_dve=3, gate_rows=4, gate_rows_mm=4, out_mm=6, x1=3, x2=3, router_mm=1,
                     gdiff=1, gexp=1, ediff=1, eexp=1, h_tr=3, h_act=3, mask=1, rank_mm=1, table=1, onehot=1,
                     meta_mm=1, meta=1, y_sum=2)

        def L(k, name, n):
            return S(name), TIMES[name] * k + n

        RING = NSLOT * SLOT
        pool = sb("pool", [P, RING + 8112])
        SCR = RING
        x = sb("x", [P, TILES, D])
        hT = sb("hT", [P, DC, T])
        xn = sb("xn", [P, TILES, D])
        yT = sb("yT", [P, DC, T])
        mrow = [sb(f"mrow{l}", [P, 3, 512]) for l in range(2)]
        ga = sb("ga", [P, 2, D])
        cst = sb("cst", [P, C_END])
        cs32 = sb("cs32", [P, DC, 32])
        modcol = [sb(f"modcol{l}", [P, 3, DC, 2, 2]) for l in range(2)]
        scg = [sb(f"scg{l}", [P, 2, DC, 2]) for l in range(2)]
        gcol = sb("gcol", [P, 2, 2, DC])
        minus_half = sb("minus_half", [P, 1])
        ss = sb("ss", [P, 2 * TILES])
        rstd = sb("rstd", [P, 2 * TILES])
        convw = sb("convw", [P, 3, 4])
        sgug = sb("sgug", [P, 4])
        qg = sb("qg", [P, 3])
        wr = sb("wr", [P, 2, DC, NG + NE])
        rb = sb("rb", [P, 2, NG + NE])
        idx = sb("idx", [P, STEPS + 2], I32)
        idx_now = sb("idx_now", [P, 1], I32)
        table = sb("table", [P, 2, T_END], I32)
        y_rows = nc.dram_tensor("y_rows", (2 * T, D), F32, kind="Internal").ap()
        ps = ctx.enter_context(nc.psum_tensor("ps", [P, 8, 512], F32))

        ident = cst[:, C_ID:C_ID + P]

        def scratch(at, n, base=SCR):
            assert base + at + n <= RING + 8112
            return pool[:, base + at:base + at + n]

        vn = scratch(0, 1536).rearrange("p (t n) -> p t n", t=3)
        gcs = scratch(1536, 384)
        pr = scratch(1920, 384)
        cv = scratch(2304, 384)
        sguw = scratch(2688, 512).rearrange("p (g n) -> p g n", g=4)
        sguT = scratch(3200, 512).rearrange("p (g n) -> p g n", g=4)
        sgub = scratch(3712, 512).rearrange("p (g n) -> p g n", g=4)
        sv = scratch(4224, 384)
        OB = SCR - SLOT
        q = scratch(0, TILES * NH * QH, OB).rearrange("p (t n) -> p t n", t=3)
        z = scratch(3456, 3 * Z_END, OB).rearrange("p (t n) -> p t n", t=3)
        o = scratch(3456, 3 * NH * VD, OB).rearrange("p (t n) -> p t n", t=3)
        qT = scratch(6240, 2 * T, OB).rearrange("p (b n) -> p b n", b=2)
        kT = scratch(7008, 1024, OB).rearrange("p (b n) -> p b n", b=2)
        pr_s = scratch(8032, 896, OB)
        prT = scratch(8928, 896, OB)
        rtmp = scratch(8032, 768, OB).rearrange("p (k n) -> p k n", k=4)
        ckv = scratch(8928, 256, OB)
        kpe = scratch(9184, 4 * ROPE, OB).rearrange("p (t n) -> p t n", t=4)
        kvg = scratch(9904, KVL, OB)
        nmax = scratch(9824, 6, OB).rearrange("p (b t) -> p b t", b=2)
        psum_of = scratch(9830, 6, OB).rearrange("p (b t) -> p b t", b=2)
        pinv = scratch(9836, 3, OB)
        ktmp = scratch(9840, 64, OB).rearrange("p (k n) -> p k n", k=4)
        qnT = hT[:, 0:3, :]
        kvT = hT[:, 3:6, :].rearrange("p a b -> p (a b)")[:, 0:1024].rearrange("p (c n) -> p c n", c=2)
        fmid = [hT[:, :, :].rearrange("p a b -> p (a b)")[:, 2304:3072].rearrange("p (k n) -> p k n", k=2), qT]
        vv = xn[:, :, :].rearrange("p a b -> p (a b)").rearrange("p (t n) -> p t n", t=4)
        select = scratch(0, TILES * P).rearrange("p (t n) -> p t n", t=TILES)
        other = scratch(TILES * P, TILES * P).rearrange("p (t n) -> p t n", t=TILES)
        hTe = scratch(D, D)
        ys = scratch(2 * D, D)
        sil = scratch(3072, DE)
        hid = scratch(3328, DE)
        hidT = scratch(3584, DE).rearrange("p (c n) -> p c n", c=2)
        condraw = scratch(5900, 2 * DC).rearrange("p (r c) -> p r c", r=2)
        rt = scratch(3840, 1800)
        gate_in = scratch(5700, STEPS)
        yg = [yT[:, :, :].rearrange("p a b -> p (a b)"), scratch(0, 3 * D)]
        finalg = scratch(6144, 1024)

        def scores(h, t):
            b = (2, 6)[h % 2]
            return (ps[:, b, 0:P], ps[:, b, P:512], ps[:, b + 1, 0:T])[t]

        def probs(t):
            return pr_s[:, (0, P, P + T)[t]:(P, P + T, P + 2 * T)[t]]

        R, at = {}, 0
        for name, n in (("logits", 20), ("gmax", 1), ("gdiff", 4), ("gexp", 4), ("cand", 4), ("cmax", 1), ("ghot", 4),
                        ("esel4", 16), ("esel", 4), ("top1", 1), ("hot1", 4), ("rest", 4), ("top2", 1), ("ediff", 1),
                        ("hot2", 4), ("eexp", 1), ("gsum", 1), ("den", 1), ("w1", 1), ("w2", 1), ("weights", 2),
                        ("hot", 32), ("mask", 16), ("prod", 32), ("rank", 2), ("ranks", NE), ("half", 2),
                        ("step", 2), ("place", 2), ("steps_hot", 2 * STEPS + 2), ("steps_rhs", 4 * STEPS)):
            R[name] = rt[:, at:at + TILES * n].rearrange("p (t n) -> p t n", t=TILES)
            at += TILES * n
        assert at + 6 * P <= 1800
        place_hot = rt[:, at:at + 6 * P].rearrange("p (t k n) -> p t k n", t=TILES, k=2)
        R["past"] = R["steps_hot"][:, :, 0:2 * STEPS].rearrange("p t (k m) -> p t k m", k=2)
        R["esel4"] = R["esel4"].rearrange("p t (g e) -> p t g e", g=NG)
        steps_hot = R["steps_hot"].rearrange("p t (k n) -> p t k n", k=2)
        hot = R["hot"].rearrange("p t (k n) -> p t k n", k=2)
        prod = R["prod"].rearrange("p t (k n) -> p t k n", k=2)
        pairs = scratch(5740, 5 * PAIRS).rearrange("p (m q) -> p m q", m=5)
        past = scratch(5780, PAIRS * (T // HALF)).rearrange("p (q m) -> p q m", q=PAIRS)
        before = scratch(5830, NE)
        limits = cst[:, C_OVER:C_END]
        first = cst[:, C_FIRST:C_TRI].unsqueeze(1)

        landed, loads, owner, count, cursor = {}, [], {}, [0] * NSLOT, [0]

        def item(name, n, src, shape, used, limit=NSLOT, at=None):
            s0 = at if at is not None else cursor[0] if cursor[0] + n <= limit else 0
            cursor[0] = s0 + n
            waits = {}
            for s in range(s0, s0 + n):
                if s in owner:
                    waits[owner[s][:-1]] = max(waits.get(owner[s][:-1], 0), owner[s][-1])
                owner[s] = used
            if ("down_mm", 0) in waits:
                waits.pop(("up_mm", 0), None)
            count[s0] += 1
            landed[name] = (s0, 16 * count[s0])
            loads.append((s0, src, shape, waits))

        def mod_items(l, i, limit=NSLOT, at=(None,) * 4):
            for j in range(4):
                b = 4 * i + j
                item(f"mod{l}.{b}", 2, mod_w[l, :, b * 512:(b + 1) * 512].rearrange("(p c) n -> p c n", c=DC),
                     (DC, 512), ("mod_mm", 3 * l + i + 1), limit, at[j])

        def expert_places(l, order):
            waits, before = [owner.get(s) for s in range(NSLOT)], list(count)
            for s in range(NSLOT):
                count[s] += TURNS
                owner[s] = ("down_mm", l, T_CUM + PAIRS - 1) if s < NSLOT // 2 else (("down_mm", "up_mm")[s % 3 < 2], l, T_ALL)
            cursor[0] = 0
            return waits, before, order

        def weight(name, a, b):
            s0 = landed[name][0]
            return pool[:, s0 * SLOT:s0 * SLOT + a * b].rearrange("p (a b) -> p a b", a=a)

        for half in range(2):
            for b in range(4):
                item(f"mod0.{b}.{half}", 1, mod_w[0, :, b * 512:(b + 1) * 512].rearrange("(p c) n -> p c n", c=DC)[:, 4 * half:4 * half + 4],
                     (DC // 2, 512), ("mod_mm", 1), at=2 * b + half)

        def in0_item(name, at, n, used):
            item(name, n // 256, ev_w_in[0, :, at:at + n].rearrange("(p c) n -> p c n", c=DC), (DC, n), used)

        in0_item("v", 2048, 512, ("v_mm", 3))
        for half in range(2):
            for name, at in (("gate_c", 512), ("xa", 1024), ("gate_b", 0)):
                in0_item(f"{name}.{half}", at + 256 * half, 256, ("conv_mm", 2 * half + 2))
        in0_item("u", 1536, 512, ("sgu_mm", 4))
        mod_items(0, 1)
        item("out0.0", 2, ev_w_out[0, 0:512, :].rearrange("(h p b) n -> p h (b n)", h=2, b=2), (2, 2 * D), ("out_mm", 6))
        item("out0.1", 2, ev_w_out[0, 512:1024, :].rearrange("(g d) n -> d g n", g=4), (4, D), ("out_mm", 6))
        mod_items(0, 2)
        mod_items(1, 0, at=(6, 8, 10, 0))
        split = len(loads)
        places = [expert_places(0, (2, 3, 4, 5, 0, 1, 6, 7, 8, 9, 10, 11))]
        mod_items(1, 1)
        ODD = NSLOT - 1
        for i in range(2):
            item(f"in1.{i}", 2, od_w_in[0].rearrange("(p c) n -> p c n", c=DC)[:, 4 * i:4 * i + 4, :],
                 (4, Z_END), ("z_mm", 6), ODD)
        item("uq", 2, od_w_uq[0].rearrange("(p c) n -> p c n", c=3), (3, NH * QH), ("q_mm", 3), ODD)
        item("ukv", 2, od_w_ukv[0].rearrange("(p c) n -> p c n", c=2), (2, NH * 2 * VD), ("k_mm", NH // 2), ODD)
        mod_items(1, 2, ODD)
        cursor[0] = 6
        for i in range(2):
            item(f"out1.{i}", 2, od_w_out[0].rearrange("(k p) n -> p k n", p=P)[:, 4 * i:4 * i + 4, :],
                 (4, D), ("out_mm", 12), ODD)
        owner[NSLOT - 1] = ("qT_tr", NH)
        places.append(expert_places(1, (0, 1, 2, 3, 10, 4, 5, 11, 6, 7, 8, 9)))

        def arrived(eng, name):
            s0, value = landed[name]
            eng.wait_ge(S(f"slot{s0}"), value)

        class Chain:

            def __init__(self, eng, name):
                self.eng, self.sem, self.n = eng, S(name), 0

            def link(self, ins):
                self.n += 1
                ins.then_inc(self.sem, 1)
                self.eng.wait_ge(self.sem, self.n)

        def norm_columns(l, w):
            i, v = ((0, 0), (1, 1))[w]
            return (lambda c, r: scg[l][:, w, c, r:r + 1]), (lambda c, r: modcol[l][:, i, c, v, r:r + 1])

        def bank2(b, n):
            return ps[:, b:b + 2, :].rearrange("p b n -> p (b n)")[:, 0:n]

        N_EARLY, N_LATE = 4, 22

        def row(src, n):
            return src.rearrange("(a n) -> a n", a=1).broadcast_to((P, n))

        HT_ACT = 4
        block = ctx.enter_context(nc.Block())

        @block.sync
        def _(sp):
            def steps_until(l, entry):
                return sp.value_load(table[0:1, l, entry], min_val=1, max_val=STEPS)

            def wait_used(key, v):
                if len(key) == 2:
                    sp.wait_ge(*L(key[1], "table", 1))
                    sp.wait_ge(S(f"L{key[1]}_{key[0]}"), steps_until(key[1], slice(v, v + 1)))
                    sp.nop()
                else:
                    sp.wait_ge(S(key[0]), v)

            def load(n):
                s0, src, (a, b), waits = loads[n]
                for k, v in waits.items():
                    wait_used(k, v)
                sp.dma_start(pool[:, s0 * SLOT:s0 * SLOT + a * b].rearrange("p (a b) -> p a b", a=a), src) \
                    .then_inc(S(f"slot{s0}"), 16)

            def expert_load(l, k, e, u):
                s, w = 3 * u + k, (moe_w1, moe_w3, moe_w2)[k]
                sp.dma_start(pool[:, s * SLOT:(s + 1) * SLOT],
                             w[l, bass.ds(e, 1)].rearrange("a (p c) n -> p (a c n)", p=P)).then_inc(S(f"slot{s}"), 16)

            def experts(l):
                waited = {}
                for s in places[l][2]:
                    if places[l][0][s]:
                        *k, v = places[l][0][s]
                        if waited.get(tuple(k), 0) < v:
                            wait_used(k, v)
                            waited[tuple(k)] = v
                    expert_load(l, s % 3, s // 3, s // 3)
                sp.wait_ge(*L(l, "table", 1))
                with sp.Fori(1, TURNS) as i:
                    for u in range(UNROLL):
                        steps = steps_until(l, bass.ds(i * UNROLL + (u + 1 - UNROLL), 1))
                        sp.wait_ge(S(f"L{l}_up_mm"), steps)
                        sp.nop()
                        for e in range(2):
                            expert_load(l, 0, i * 2 * UNROLL + (2 * u + e), 2 * u + e)
                            expert_load(l, 1, i * 2 * UNROLL + (2 * u + e), 2 * u + e)
                        sp.wait_ge(S(f"L{l}_down_mm"), steps)
                        sp.nop()
                        for e in range(2):
                            expert_load(l, 2, i * 2 * UNROLL + (2 * u + e), 2 * u + e)

            def biases():
                sp.wait_ge(S("rows_zero"), 2)
                for l in range(2):
                    for r in range(2):
                        for j in range(4):
                            sp.dma_start(mrow[l][32 * j + r:32 * j + r + 1, :, :],
                                         mod_b[l].rearrange("(i j n) -> j i n", i=3, j=4)[j:j + 1]).then_inc(S("bias"), 16)

            def constants():
                late = [(cst[:, C_CS1:], consts[:, C_CS1:])]
                late += [(convw[:, k, :].rearrange("p (h b) -> p h b", h=2), ev_conv_w[0, k].rearrange("(h p b) -> p h b", h=2, b=2)) for k in range(3)]
                late += [(sguw, ev_sgu_w[0].rearrange("g p q -> p g q")),
                         (sgub, row(ev_sgu_b[0].rearrange("g n -> (g n)"), 4 * P).rearrange("p (g n) -> p g n", g=4)),
                         (qg[:, :], od_q_norm_g[0].rearrange("(p c) -> p c", c=3)),
                         (kvg, row(od_kv_norm_g[0], KVL)), (ckv, cache_ckv[0, 0]), (kpe[:, 1, :], cache_kpe[0, 0])]
                for l in range(2):
                    late += [(wr[:, l, :, 0:NG], moe_wg[l].rearrange("(p c) g -> p c g", c=DC)),
                             (wr[:, l, :, NG:], moe_we[l].rearrange("(p c) g e -> p c (g e)", c=DC)),
                             (rb[:, l, 0:NG], row(moe_bg[l], NG)),
                             (rb[:, l, NG:], row(moe_be[l].rearrange("g e -> (g e)"), NE))]
                late += [(sgug[:, g:g + 1], ev_sgu_norm_g[0].rearrange("(g d a) -> g d a", g=4, a=1)[g]) for g in range(4)]
                assert len(late) == N_LATE
                for dst, src in late:
                    sp.dma_start(dst, src).then_inc(S("late"), 16)

            for n in range(split):
                load(n)
                if n == 7:
                    biases()
                if n == 9:
                    constants()
            experts(0)
            for n in range(split, len(loads)):
                if n == split + 4:
                    sp.wait_ge(S("y_rows2"), 32)
                load(n)
            experts(1)

        @block.gpsimd
        def _(gps):
            for l in range(2):
                nc.gpsimd.memset(mrow[l][:, :, :], 0.0).then_inc(S("rows_zero"), 1)
            nc.gpsimd.memset(cs32[:, :, :], 0.0).then_inc(S("cs32_zero"), 1)
            ch = Chain(gps, "gps_chain")
            ch.link(nc.gpsimd.memset(minus_half[:, :], -0.5))

            def root(name, n, at, width):
                gps.wait_ge(S(name + "_ss"), n)
                ch.link(nc.gpsimd.tensor_scalar(rstd[:, at:at + 1], ss[:, at:at + 1], 1.0 / width, EPS, ALU.mult, ALU.add))
                nc.gpsimd.tensor_tensor(rstd[:, at:at + 1], rstd[:, at:at + 1], minus_half[:, :], ALU.pow) \
                    .then_inc(S(name + "_root"), 1)

            def rows_out(l):
                row_of = idx[:, :]
                gps.wait_ge(*L(l, "meta", 1))
                nc.gpsimd.tensor_copy(idx_now[:, :], row_of[:, 2:3]).then_inc(S(f"L{l}_idx_now"), 1)
                gps.wait_ge(S(f"L{l}_idx_now"), 1)
                n = gps.value_load(table[0:1, l, T_ALL:T_ALL + 1], min_val=PAIRS, max_val=STEPS - 1)
                with gps.Fori(2, n + 2) as j:
                    gps.wait_ge(S(f"L{l}_ys"), j)
                    gps.nop()
                    nc.gpsimd.tensor_copy(idx_now[:, :], row_of[:, bass.ds(j, 1)]).then_inc(S(f"L{l}_idx_now"), 1)
                    gps.wait_ge(*L(l, "meta", 1))
                    gps.wait_ge(S(f"L{l}_idx_now"), j)
                    nc.gpsimd.indirect_dma_start(out=y_rows[:, :], out_offset=bass.IndirectOffsetOnAxis(ap=idx_now[:, :], axis=0),
                                                 in_=ys, in_offset=None, bounds_check=2 * T - 1, oob_is_err=False) \
                        .then_inc(S(f"L{l}_stored"), 16)

            def row_sums(l):
                for t in range(1, TILES):
                    gps.wait_ge(S(f"y_rows{t}"), 32 * (l + 1))
                    a, b = (yg[k][:, t * D:(t + 1) * D] for k in range(2))
                    nc.gpsimd.tensor_tensor(a, a, b, ALU.add).then_inc(S("y_sum"), 1)

            for t in range(TILES):
                root("norm", t + 1, t, D)
            for t in range(TILES):
                root("v", t + 1, 3 + t, 512)
            for t in range(TILES):
                root("norm", TILES + t + 1, t, D)
            rows_out(0)
            row_sums(0)
            for t in range(TILES):
                root("norm", 2 * TILES + t + 1, t, D)
            for t in range(TILES):
                root("qc", t + 1, t, QL)
                root("kvc", t + 1, 3 + t, KVL)
            for t in range(TILES):
                root("norm", 3 * TILES + t + 1, t, D)
            rows_out(1)
            row_sums(1)
            for t in range(TILES):
                root("norm", 4 * TILES + t + 1, t, D)

        @block.scalar
        def _(act):
            a_ = nc.scalar
            ch = Chain(act, "act_chain")

            def row(src, n):
                return src.rearrange("(a n) -> a n", a=1).broadcast_to((P, n))

            for r, src in enumerate((c_ctx, c[0])):
                act.dma_start(condraw[:, r, :], src.rearrange("(p c) -> p c", c=DC)).then_inc(S("cond"), 16)
            act.dma_start(x[:, 0, :], x_prompt[0]).then_inc(S("x_in"), 16)
            act.dma_start(x[:, 1:3, :], x_sample[0].rearrange("(t p) d -> p t d", p=P)).then_inc(S("x_in"), 16)
            act.dma_start(cst[:, 0:C_CS1], consts[:, 0:C_CS1]).then_inc(S("ident_in"), 16)
            early = [(gcol[:, l, w, :], g[l].rearrange("(p c) -> p c", c=DC))
                      for l in range(2) for w, g in enumerate((norm1_g, norm2_g))]
            assert len(early) == N_EARLY
            for dst, src in early:
                act.dma_start(dst, src).then_inc(S("early"), 16)

            def squares(name, ready, dst, src, out):
                act.wait_ge(S(ready[0]), ready[1])
                a_.activation(dst, src, ACT.Square, accum_out=out).then_inc(S(name + "_ss"), 1)

            def norm_squares(ready, n):
                for t in range(TILES):
                    squares("norm", (ready, n if ready == "x_in" else n + t + 1), xn[:, t, :], x[:, t, :], ss[:, t:t + 1])

            def norm_evacuate(l, w):
                scale, shift = norm_columns(l, w)
                act.wait_ge(S(f"norm_cols{2 * l + w}"), 1)
                for t in range(TILES):
                    act.wait_ge(*L(2 * l + w, "norm_tr", t + 1))
                    for cc in range(HT_ACT):
                        ins = a_.activation(hT[:, cc, t * P:(t + 1) * P], bank2(2 * t, D)[:, cc * P:(cc + 1) * P],
                                            ACT.Identity, bias=shift(cc, cond_of(t)), scale=scale(cc, cond_of(t)))
                    ins.then_inc(S("norm_hT_act"), 1)

            def router_exps(l):
                act.wait_ge(*L(l, "gdiff", 1))
                a_.activation(R["gexp"], R["gdiff"], ACT.Exp).then_inc(S("gexp"), 1)
                act.wait_ge(*L(l, "ediff", 1))
                a_.activation(R["eexp"], R["ediff"], ACT.Exp).then_inc(S("eexp"), 1)

            def by_tokens(l):
                for t in range(TILES):
                    if t == 1:
                        router_exps(l)
                    act.wait_ge(*L(l, "h_tr", t + 1))
                    a_.activation(xn[:, t, :], bank2((0, 2, 0)[t], D), ACT.Copy).then_inc(S("h_act"), 1)

            def experts(l):
                def turned_tokens(j):
                    act.wait_ge(S(f"L{l}_x_3"), j + 1)
                    a_.activation(hTe[:, 0:512], ps[:, 2, :], ACT.Copy).then_inc(S(f"L{l}_hTe_act"), 1)

                turned_tokens(0)
                n = act.value_load(table[0:1, l, T_ALL:T_ALL + 1], min_val=PAIRS, max_val=STEPS - 1)
                with act.Fori(0, n) as j:
                    act.wait_ge(S(f"L{l}_up_mm"), j + 1)
                    a_.activation(sil, ps[:, 0, 0:DE], ACT.Silu).then_inc(S(f"L{l}_silu"), 1)
                    act.wait_ge(S(f"L{l}_hid_tr"), j + 1)
                    a_.activation(hidT, ps[:, 1, 0:DE].rearrange("p (c n) -> p c n", c=2), ACT.Copy) \
                        .then_inc(S(f"L{l}_hidT"), 1)
                    turned_tokens(j + 1)
                act.wait_ge(S(f"L{l}_stored"), n * 16)
                act.wait_ge(S(f"L{l}_select"), n + 2)
                act.wait_ge(S(f"L{l}_hTe_act"), n + 1)
                for t in range(TILES):
                    for k in range(2):
                        act.dma_start(yg[k][:, t * D:(t + 1) * D], y_rows[k * T + t * P:k * T + (t + 1) * P, :]) \
                            .then_inc(S(f"y_rows{t}"), 16)

            def gate_rows(l, k, parts=range(4)):
                for n in parts:
                    act.wait_ge(*L(2 * l + k, "gate_rows_mm", n + 1))
                    a_.activation(ga[:, n // 2, (n % 2) * 512:(n % 2 + 1) * 512], ps[:, 6 + n % 2, :], ACT.Copy) \
                        .then_inc(S("gate_rows"), 1)

            act.wait_ge(S("cond"), 32)
            act.wait_ge(S("cs32_zero"), 1)
            a_.activation(cs32[:, :, 0:2], condraw[:, :, :].rearrange("p r c -> p c r"), ACT.Silu).then_inc(S("cs32"), 1)
            norm_squares("x_in", 32)
            norm_evacuate(0, 0)
            for t in range(TILES):
                squares("v", ("v_mm", t + 1), vn[:, t, :], ps[:, t, :], ss[:, 3 + t:4 + t])
            for j in range(4):
                act.wait_ge(S("conv_mm"), j + 1)
                if j:
                    act.wait_ge(S("gated"), j)
                a_.activation(gcs, ps[:, (3, 6)[j % 2], 0:T], ACT.Copy).then_inc(S("gate_c"), 1)
            act.wait_ge(S("sgu_tr"), 1)
            a_.activation(sguT, ps[:, 1, :].rearrange("p (g n) -> p g n", g=4), ACT.Copy).then_inc(S("sguT"), 1)
            gate_rows(0, 0)
            norm_squares("x1", 0)
            norm_evacuate(0, 1)
            gate_rows(0, 1, (0, 1))
            by_tokens(0)
            gate_rows(0, 1, (2, 3))
            experts(0)
            norm_squares("x2", 0)
            norm_evacuate(1, 0)
            for t in range(TILES):
                act.wait_ge(S("z_mm"), 2 * t + 2)
                ch.link(a_.activation(z[:, t, 512:Z_END], ps[:, 2 * t + 1, 0:Z_END - 512], ACT.Copy))
                act.sem_inc(S("z_high"), 1)
                squares("qc", ("z_low", t + 1), xn[:, t, 0:QL], z[:, t, Z_Q:Z_KV], ss[:, t:t + 1])
                squares("kvc", ("z_low", t + 1), xn[:, t, QL:QL + KVL], z[:, t, Z_KV:Z_PE], ss[:, 3 + t:4 + t])
            act.wait_ge(S("kvn"), 3)
            act.dma_start(new_ckv[0, 0], z[:, 0, Z_KV:Z_PE]).then_inc(S("new_kv"), 16)
            act.dma_start(new_kpe[0, 0], z[:, 0, Z_PE:Z_END]).then_inc(S("new_kv"), 16)
            for cc in range(3):
                act.wait_ge(S("qn_tr"), cc + 1)
                a_.activation(qnT[:, cc, :], ps[:, cc, 0:T], ACT.Copy, scale=qg[:, cc:cc + 1]).then_inc(S("qnT"), 1)
            for t in range(TILES):
                act.wait_ge(S("q_mm"), t + 1)
                for n, w in ((0, 512), (1, 512), (2, 128)):
                    ins = a_.activation(q[:, t, n * 512:n * 512 + w], ps[:, 3 * (t % 2) + n, 0:w], ACT.Copy)
                ins.then_inc(S("q_out"), 1)
            def k_pair(g):
                act.wait_ge(S("k_mm"), g + 1)
                for b in range(2):
                    ins = a_.activation(kT[0:NOPE, b, :], ps[b * NOPE:(b + 1) * NOPE, 0, :], ACT.Copy)
                ins.then_inc(S("kT"), 1)

            k_pair(0)
            for h in range(NH):
                act.wait_ge(S("nmax"), h + 1)
                for t in range(TILES):
                    ins = a_.activation(probs(t), scores(h, t), ACT.Exp, bias=nmax[:, h % 2, t:t + 1], scale=SCALE,
                                        accum_out=psum_of[:, h % 2, t:t + 1])
                ins.then_inc(S("probs"), 1)
                if h % 2 == 0 and h + 2 < NH:
                    k_pair(h // 2 + 1)
                act.wait_ge(S("p_tr"), h + 1)
                a_.activation(prT[:, 0:512], ps[:, 4, :], ACT.Copy).then_inc(S("pT_act"), 1)
            gate_rows(1, 0)
            norm_squares("x1", TILES)
            norm_evacuate(1, 1)
            gate_rows(1, 1, (0, 1))
            act.dma_start(finalg, row(final_norm_g, D)).then_inc(S("finalg"), 16)
            by_tokens(1)
            gate_rows(1, 1, (2, 3))
            experts(1)
            norm_squares("x2", TILES)
            for t in range(TILES):
                act.wait_ge(S("y"), t + 1)
                act.dma_start(y_prompt[0] if t == 0 else y_sample[0, (t - 1) * P:t * P, :], xn[:, t, :]) \
                    .then_inc(S("stored"), 16)
            act.wait_ge(S("new_kv"), 32)
            act.wait_ge(S("stored"), 48)

        @block.vector
        def _(dve):
            v_ = nc.vector
            ch = Chain(dve, "dve_chain")
            link = ch.link

            def mod_round(l, i):
                mod_rows(l, i)
                mod_columns(l, i)

            def mod_rows(l, i):
                dve.wait_ge(*L(3 * l + i, "mod_mm", 1))
                if l == 0 and i == 0:
                    dve.wait_ge(S("bias"), 16 * 16)
                v_.tensor_tensor(mrow[l][:, i, :], ps[:, 7, :], mrow[l][:, i, :], ALU.add).then_inc(S("mod_row"), 1)

            def mod_columns(l, i):
                dve.wait_ge(*L(3 * l + i, "mod_cmm", 1))
                link(v_.tensor_copy(modcol[l][:, i].rearrange("p c v r -> p (c v r)"), ps[:, 6, 0:4 * DC]))
                dve.sem_inc(S("mod_col"), 1)
                if i != 1:
                    w, v = ((0, 1), None, (1, 0))[i]
                    v_.scalar_tensor_tensor(scg[l][:, w], modcol[l][:, i, :, v, :], 1.0,
                                            gcol[:, l, w, :].unsqueeze(2).broadcast_to((P, DC, 2)), ALU.add, ALU.mult) \
                        .then_inc(S(f"norm_cols{2 * l + w}"), 1)

            def normalise(k):
                for t in range(TILES):
                    dve.wait_ge(*L(k, "norm_root", t + 1))
                    v_.tensor_scalar(xn[:, t, :], x[:, t, :], rstd[:, t:t + 1], None, ALU.mult).then_inc(S("norm_xn"), 1)

            def norm_evacuate(l, w):
                scale, shift = norm_columns(l, w)
                dve.wait_ge(S(f"norm_cols{2 * l + w}"), 1)
                for t in range(TILES):
                    dve.wait_ge(*L(2 * l + w, "norm_tr", t + 1))
                    for cc in range(HT_ACT, DC):
                        ins = v_.tensor_scalar(hT[:, cc, t * P:(t + 1) * P], bank2(2 * t, D)[:, cc * P:(cc + 1) * P],
                                               scale(cc, cond_of(t)), shift(cc, cond_of(t)), ALU.mult, ALU.add)
                    ins.then_inc(S("norm_hT_dve"), 1)

            def project_out(l):
                dve.wait_ge(*L(2 * l + 0, "gate_rows", 4))
                for t in range(TILES):
                    for n in range(2):
                        if (l, t, n) == (0, 1, 1):
                            mod_round(0, 2)
                        dve.wait_ge(*L(l, "out_mm", 2 * t + n + 1))
                        half = slice(n * 512, n * 512 + 512)
                        link(v_.tensor_tensor(xn[:, t, half], ps[:, 2 * t + n, :], ga[:, cond_of(t), half], ALU.mult))
                        ins = v_.tensor_tensor(x[:, t, half], x[:, t, half], xn[:, t, half], ALU.add)
                    ins.then_inc(S("x1"), 1)

            def first_of(dst, values, top):
                b = (P, TILES, 4)
                link(v_.tensor_tensor(R["cand"], values, top.broadcast_to(b), ALU.is_equal))
                link(v_.tensor_tensor(R["cand"], R["cand"], first.broadcast_to(b), ALU.mult))
                link(v_.tensor_reduce(R["cmax"], R["cand"], AX, ALU.max))
                link(v_.tensor_tensor(dst, R["cand"], R["cmax"].broadcast_to(b), ALU.is_equal))

            def router(l):
                b, b44 = (P, TILES, 4), (P, TILES, 4, 4)
                dve.wait_ge(*L(l, "router_mm", 1))
                link(v_.tensor_tensor(R["logits"], ps[:, 0, 0:TILES * 20].rearrange("p (t n) -> p t n", t=TILES),
                                      rb[:, l, :].unsqueeze(1).broadcast_to((P, TILES, 20)), ALU.add))
                glog, elog = R["logits"][:, :, 0:NG], R["logits"][:, :, NG:].rearrange("p t (g e) -> p t g e", g=NG)
                link(v_.tensor_reduce(R["gmax"], glog, AX, ALU.max))
                v_.tensor_tensor(R["gdiff"], glog, R["gmax"].broadcast_to(b), ALU.subtract).then_inc(S("gdiff"), 1)
                first_of(R["ghot"], glog, R["gmax"])
                link(v_.tensor_tensor(R["esel4"], elog, R["ghot"].unsqueeze(3).broadcast_to(b44), ALU.mult))
                link(v_.tensor_reduce(R["esel"], R["esel4"].rearrange("p t g e -> p t e g"), AX, ALU.add))
                link(v_.tensor_reduce(R["top1"], R["esel"], AX, ALU.max))
                first_of(R["hot1"], R["esel"], R["top1"])
                link(v_.scalar_tensor_tensor(R["rest"], R["hot1"], NEG, R["esel"], ALU.mult, ALU.add))
                link(v_.tensor_reduce(R["top2"], R["rest"], AX, ALU.max))
                v_.tensor_tensor(R["ediff"], R["top2"], R["top1"], ALU.subtract).then_inc(S("ediff"), 1)
                first_of(R["hot2"], R["rest"], R["top2"])

            def select_tokens(l, at, ready):
                for k in range(2):
                    out = (select, other)[k]
                    ins = v_.tensor_tensor(out, place_hot[:, :, k, :], steps_hot[:, :, k, at].broadcast_to((P, TILES, P)), ALU.mult)
                ins.then_inc(S(f"L{l}_select_parts"), 1)
                dve.wait_ge(S(f"L{l}_select_parts"), ready)
                v_.tensor_tensor(select, select, other, ALU.add).then_inc(S(f"L{l}_select"), 1)

            def place_tokens(l):
                b44, b2n = (P, TILES, 4, 4), (P, TILES, 2, NE)
                for k, name in enumerate(("hot1", "hot2")):
                    link(v_.tensor_tensor(hot[:, :, k].rearrange("p t (g e) -> p t g e", g=NG),
                                          R["ghot"].unsqueeze(3).broadcast_to(b44), R[name].unsqueeze(2).broadcast_to(b44), ALU.mult))
                v_.tensor_tensor(R["mask"], hot[:, :, 0], hot[:, :, 1], ALU.add).then_inc(S("mask"), 1)
                dve.wait_ge(*L(l, "gexp", 1))
                link(v_.tensor_reduce(R["gsum"], R["gexp"], AX, ALU.add))
                dve.wait_ge(*L(l, "eexp", 1))
                link(v_.scalar_tensor_tensor(R["den"], R["eexp"], 1.0, R["gsum"], ALU.add, ALU.mult))
                link(v_.reciprocal(R["w1"], R["den"]))
                link(v_.tensor_tensor(R["w2"], R["w1"], R["eexp"], ALU.mult))
                link(v_.tensor_copy(R["weights"][:, :, 0:1], R["w1"]))
                link(v_.tensor_copy(R["weights"][:, :, 1:2], R["w2"]))
                link(v_.tensor_tensor(prod, hot, cst[:, C_HALF:C_HALF + NE].unsqueeze(1).unsqueeze(1).broadcast_to(b2n), ALU.mult))
                link(v_.tensor_reduce(R["half"], prod, AX, ALU.add))
                dve.wait_ge(*L(l, "rank_mm", 1))
                most, rounds, s1, s2, s3 = (pairs[:, m, :] for m in range(5))
                link(v_.tensor_reduce(most, ps[:, 5, 48:64].rearrange("p (q e) -> p q e", e=2), AX, ALU.max))
                over = (P, PAIRS, T // HALF)
                link(v_.tensor_tensor(past, most.unsqueeze(2).broadcast_to(over), limits[:, 0:T // HALF].unsqueeze(1).broadcast_to(over), ALU.is_gt))
                link(v_.tensor_reduce(rounds, past, AX, ALU.add))
                for src, dst, d in ((rounds, s1, 1), (s1, s2, 2), (s2, s3, 4)):
                    v_.tensor_copy(dst[:, 0:d], src[:, 0:d])
                    link(v_.tensor_tensor(dst[:, d:], src[:, d:], src[:, 0:PAIRS - d], ALU.add))
                link(v_.tensor_tensor(s1, s3, rounds, ALU.subtract))
                v_.tensor_scalar(before.rearrange("p (q e) -> p q e", e=2), s1.unsqueeze(2).broadcast_to((P, PAIRS, 2)), float(HALF), None, ALU.mult)
                v_.tensor_copy(table[:, l, T_CUM:T_CUM + PAIRS], s1)
                v_.tensor_copy(table[:, l, T_ROUNDS:T_END], rounds)
                v_.tensor_copy(table[:, l, T_ALL:T_ALL + 1], s3[:, PAIRS - 1:PAIRS]).then_inc(S("table"), 1)
                dve.wait_ge(*L(l, "table", 1))
                link(v_.tensor_tensor(R["ranks"], before.unsqueeze(1).broadcast_to((P, TILES, NE)),
                                      ps[:, 5, 0:48].rearrange("p (t n) -> p t n", t=TILES), ALU.add))
                link(v_.tensor_tensor(prod, hot, R["ranks"].unsqueeze(2).broadcast_to(b2n), ALU.mult))
                link(v_.tensor_reduce(R["rank"], prod, AX, ALU.add))
                over = (P, TILES, 2, STEPS)
                link(v_.tensor_tensor(R["past"], R["rank"].unsqueeze(3).broadcast_to(over),
                                      limits[:, 1:].unsqueeze(1).unsqueeze(1).broadcast_to(over), ALU.is_ge))
                link(v_.tensor_reduce(R["step"], R["past"], AX, ALU.add))
                link(v_.scalar_tensor_tensor(R["place"], R["step"], -float(HALF), R["rank"], ALU.mult, ALU.add))
                link(v_.tensor_tensor(R["place"], R["place"], R["half"], ALU.add))
                link(v_.tensor_tensor(place_hot, cst[:, C_IOTA:C_IOTA + P].unsqueeze(1).unsqueeze(1).broadcast_to((P, TILES, 2, P)),
                                      R["place"].unsqueeze(3).broadcast_to((P, TILES, 2, P)), ALU.is_equal))
                bs1 = (P, TILES, 2, STEPS + 1)
                link(v_.tensor_tensor(steps_hot, cst[:, C_IOTA:C_IOTA + STEPS + 1].unsqueeze(1).unsqueeze(1).broadcast_to(bs1),
                                      R["step"].unsqueeze(3).broadcast_to(bs1), ALU.is_equal))
                select_tokens(l, slice(0, 1), 1)

            def step_contents(l):
                bs, steps_now = (P, TILES, 2, STEPS), steps_hot[:, :, :, 0:STEPS]
                rhs = R["steps_rhs"].rearrange("p t (v k n) -> p t v k n", v=2, k=2)
                numbers = cst[:, C_TOK:C_HALF].rearrange("p (t k) -> p t k", k=2)
                v_.tensor_tensor(rhs[:, :, 0], steps_now, numbers.unsqueeze(3).broadcast_to(bs), ALU.mult)
                v_.tensor_tensor(rhs[:, :, 1], steps_now, R["weights"].unsqueeze(3).broadcast_to(bs), ALU.mult) \
                    .then_inc(S("onehot"), 1)

            def contents_out(l):
                dve.wait_ge(*L(l, "meta_mm", 1))
                v_.tensor_copy(gate_in, ps[:, 4, STEPS:2 * STEPS])
                none = R["steps_rhs"].rearrange("p t n -> p (t n)")[:, 0:STEPS]
                found = ps[:, 4, 0:STEPS]
                link(v_.tensor_scalar(none, found, 0.0, FAR, ALU.is_equal, ALU.mult))
                v_.scalar_tensor_tensor(idx[:, 2:], found, -1.0, none, ALU.add, ALU.add) \
                    .then_inc(S("meta"), 1)

            def experts(l):
                def turned_tokens(j):
                    dve.wait_ge(S(f"L{l}_x_7"), j + 1)
                    v_.tensor_copy(hTe[:, 512:D], ps[:, 3, :]).then_inc(S(f"L{l}_hTe_dve"), 1)

                step_contents(l)
                turned_tokens(0)
                select_tokens(l, slice(1, 2), 2)
                contents_out(l)
                dve.sem_inc(S(f"L{l}_ys"), 1)
                n = dve.value_load(table[0:1, l, T_ALL:T_ALL + 1], min_val=PAIRS, max_val=STEPS - 1)
                with dve.Fori(0, n) as j:
                    dve.wait_ge(S(f"L{l}_silu"), j + 1)
                    v_.scalar_tensor_tensor(hid, ps[:, 0, DE:2 * DE], gate_in[:, bass.ds(j, 1)], sil, ALU.mult, ALU.mult) \
                        .then_inc(S(f"L{l}_hid"), 1)
                    dve.wait_ge(S(f"L{l}_down_mm"), j + 1)
                    dve.wait_ge(S(f"L{l}_stored"), j * 16)
                    v_.tensor_copy(ys, bank2(4, D)).then_inc(S(f"L{l}_ys"), 1)
                    turned_tokens(j + 1)
                    select_tokens(l, bass.ds(j + 2, 1), j + 3)

            def experts_out(l):
                dve.wait_ge(*L(2 * l + 1, "gate_rows", 4))
                for t in range(TILES):
                    a, b = (yg[k][:, t * D:(t + 1) * D] for k in range(2))
                    if t == 0:
                        dve.wait_ge(S("y_rows0"), 32 * (l + 1))
                        link(v_.tensor_tensor(a, a, b, ALU.add))
                    else:
                        dve.wait_ge(*L(l, "y_sum", t))
                    link(v_.tensor_tensor(a, a, ga[:, cond_of(t), :], ALU.mult))
                    v_.tensor_tensor(x[:, t, :], x[:, t, :], a, ALU.add).then_inc(S("x2"), 1)

            dve.wait_ge(S("x_in"), 32)
            normalise(0)
            dve.wait_ge(S("early"), 16 * N_EARLY)
            mod_round(0, 0)
            norm_evacuate(0, 0)
            for t in range(TILES):
                dve.wait_ge(S("v_root"), t + 1)
                v_.tensor_scalar(vn[:, t, :], ps[:, t, :], rstd[:, 3 + t:4 + t], None, ALU.mult).then_inc(S("vn"), 1)
            dve.wait_ge(S("late"), 16 * N_LATE)
            for j in range(4):
                b = (3, 6)[j % 2]
                b1, b2 = b + 1, (b + 2) % 8
                dve.wait_ge(S("gate_c"), j + 1)
                ins = v_.tensor_tensor(pr, gcs, ps[:, b1, 0:T], ALU.mult)
                link(ins)
                dve.sem_inc(S("gated"), 1)
                link(v_.tensor_scalar(cv, pr, convw[:, 1, j:j + 1], None, ALU.mult))
                for a, n in ((0, P), (P, 2 * P)):
                    link(v_.scalar_tensor_tensor(cv[:, a + 1:a + n], pr[:, a:a + n - 1], convw[:, 0, j:j + 1],
                                                 cv[:, a + 1:a + n], ALU.mult, ALU.add))
                    link(v_.scalar_tensor_tensor(cv[:, a:a + n - 1], pr[:, a + 1:a + n], convw[:, 2, j:j + 1],
                                                 cv[:, a:a + n - 1], ALU.mult, ALU.add))
                v_.tensor_tensor(yT[:, j, :], cv, ps[:, b2, 0:T], ALU.mult).then_inc(S("y_conv"), 1)
            for g in range(4):
                dve.wait_ge(S("sgu_mm"), g + 1)
                link(v_.scalar_tensor_tensor(sv.rearrange("p (t n) -> p t n", t=TILES),
                                             ps[:, (1, 4)[g % 2], 0:T].rearrange("p (t n) -> p t n", t=TILES),
                                             sgug[:, g:g + 1], sgub[:, g, :].unsqueeze(1).broadcast_to((P, TILES, P)),
                                             ALU.mult, ALU.add))
                link(v_.tensor_tensor(yT[:, 4 + g, :], sv, ps[:, (2, 3)[g % 2], 0:T], ALU.mult))
                dve.sem_inc(S("y_sgu"), 1)
            mod_round(0, 1)
            project_out(0)
            normalise(1)
            mod_round(1, 0)
            norm_evacuate(0, 1)
            router(0)
            place_tokens(0)
            experts(0)
            mod_round(1, 1)
            experts_out(0)
            normalise(2)
            norm_evacuate(1, 0)

            for t in range(TILES):
                dve.wait_ge(S("z_mm"), 2 * t + 1)
                v_.tensor_copy(z[:, t, 0:512], ps[:, 2 * t, :]).then_inc(S("z_low"), 1)
            for t in range(TILES):
                dve.wait_ge(S("qc_root"), t + 1)
                v_.tensor_scalar(z[:, t, Z_Q:Z_KV], z[:, t, Z_Q:Z_KV], rstd[:, t:t + 1], None, ALU.mult).then_inc(S("qn"), 1)
                dve.wait_ge(S("kvc_root"), t + 1)
                v_.scalar_tensor_tensor(z[:, t, Z_KV:Z_PE], z[:, t, Z_KV:Z_PE], rstd[:, 3 + t:4 + t], kvg, ALU.mult, ALU.mult) \
                    .then_inc(S("kvn"), 1)

            def rotate(dst, src, t, tmp):
                shape = tuple(src.shape[:-2]) + (8,)
                cos = cst[:, C_COS + 16 * (t - 1):C_COS + 16 * t].rearrange("p (k n) -> p k n", k=2)
                sin = cst[:, C_SIN + 16 * (t - 1):C_SIN + 16 * t].rearrange("p (k n) -> p k n", k=2)
                if len(shape) == 4:
                    cos, sin = cos.unsqueeze(1).broadcast_to(shape), sin.unsqueeze(1).broadcast_to(shape)
                    first_half, second_half = src[:, :, :, 0, :], src[:, :, :, 1, :]
                    out1, out2 = dst[:, :, :, 0, :], dst[:, :, :, 1, :]
                else:
                    first_half, second_half, out1, out2 = src[:, :, 0, :], src[:, :, 1, :], dst[:, :, 0, :], dst[:, :, 1, :]
                v_.tensor_tensor(tmp[0], first_half, cos, ALU.mult)
                v_.tensor_tensor(tmp[1], second_half, sin, ALU.mult)
                v_.tensor_tensor(tmp[2], second_half, cos, ALU.mult)
                link(v_.tensor_tensor(tmp[3], first_half, sin, ALU.mult))
                v_.tensor_tensor(out1, tmp[0], tmp[1], ALU.subtract)
                link(v_.tensor_tensor(out2, tmp[2], tmp[3], ALU.add))

            dve.wait_ge(S("z_high"), 3)
            link(v_.tensor_copy(kpe[:, 0, :], z[:, 0, Z_PE:Z_END]))
            for t in (1, 2):
                rotate(kpe[:, t + 1, :].rearrange("p (k a n) -> p k a n", k=2, a=2),
                       z[:, t, Z_PE:Z_END].rearrange("p (k a n) -> p k a n", k=2, a=2), t,
                       [ktmp[:, k, :].rearrange("p (k n) -> p k n", k=2) for k in range(4)])
            dve.sem_inc(S("kpe"), 1)
            for j in range(2):
                dve.wait_ge(S("four_tok_mm"), j + 1)
                b = (6, 4)[j]
                v_.tensor_copy(fmid[j][:, :, 0:P], ps[:, b, 0:2 * P].rearrange("p (k n) -> p k n", k=2))
                v_.tensor_copy(fmid[j][:, :, P:T], ps[:, b + 1, :].rearrange("p (k n) -> p k n", k=2)) \
                    .then_inc(S("fmid"), 1)
            for cc in range(2):
                dve.wait_ge(S("kv_tr"), cc + 1)
                v_.tensor_copy(kvT[:, cc, :], ps[:, 3 + cc, :]).then_inc(S("kvT"), 1)
            dve.wait_ge(S("kpe_tr"), 1)
            dve.wait_ge(S("four_mm"), 1)
            for b in range(2):
                ins = v_.tensor_copy(kT[NOPE:QH, b, :], ps[NOPE:QH, 5, :])
            ins.then_inc(S("kpeT"), 1)
            for j in range(2):
                ins = v_.tensor_copy(yT[:, j, :], ps[:, 6 + j, 0:T])
            ins.then_inc(S("y_four"), 1)
            for t in (1, 2):
                dve.wait_ge(S("q_out"), t + 1)
                qpe = q[:, t, :].rearrange("p (h n) -> p h n", h=NH)[:, :, NOPE:QH].rearrange("p h (k a n) -> p h k a n", k=2, a=2)
                for k in range(2):
                    cos = cst[:, C_COS + 16 * (t - 1) + 8 * k:C_COS + 16 * (t - 1) + 8 * k + 8].unsqueeze(1).broadcast_to((P, NH, 8))
                    sin = cst[:, C_SIN + 16 * (t - 1) + 8 * k:C_SIN + 16 * (t - 1) + 8 * k + 8].unsqueeze(1).broadcast_to((P, NH, 8))
                    one, two = qpe[:, :, k, 0, :], qpe[:, :, k, 1, :]
                    tmp = [rtmp[:, m, 0:96].rearrange("p (h n) -> p h n", h=NH) for m in range(4)]
                    v_.tensor_tensor(tmp[0], one, cos, ALU.mult)
                    v_.tensor_tensor(tmp[1], two, sin, ALU.mult)
                    v_.tensor_tensor(tmp[2], two, cos, ALU.mult)
                    link(v_.tensor_tensor(tmp[3], one, sin, ALU.mult))
                    v_.tensor_tensor(one, tmp[0], tmp[1], ALU.subtract)
                    link(v_.tensor_tensor(two, tmp[2], tmp[3], ALU.add))
            dve.sem_inc(S("q_rot"), 1)
            for kt in range(4):
                dve.wait_ge(S("v2_mm"), kt + 1)
                v_.tensor_copy(vv[:, kt, :], bank2((6, 3)[kt % 2], NH * VD)).then_inc(S("vv"), 1)

            def head_probs_out(h):
                dve.wait_ge(S("probs"), h + 1)
                if h:
                    dve.wait_ge(S("o_out"), h)
                v_.reciprocal(pinv, psum_of[:, h % 2])
                dve.wait_ge(S("p_tr"), h + 1)
                v_.tensor_copy(prT[:, 512:7 * P], ps[:, 5, 0:7 * P - 512]).then_inc(S("pT_dve"), 1)

            def head_out(h):
                dve.wait_ge(S("o_mm"), h + 1)
                v_.tensor_tensor(o[:, :, h * VD:(h + 1) * VD], ps[:, 1, 0:3 * VD].rearrange("p (t n) -> p t n", t=3),
                                 pinv.unsqueeze(2).broadcast_to((P, 3, VD)), ALU.mult).then_inc(S("o_out"), 1)

            dve.wait_ge(S("new_kv"), 32)
            def head_q(h):
                dve.wait_ge(S("qT_tr"), h + 1)
                v_.tensor_copy(qT[0:QH, h % 2, :], ps[0:QH, 0, 0:T]).then_inc(S("qT"), 1)

            def head_maxima(h):
                dve.wait_ge(S("s_mm"), h + 1)
                for t in range(TILES):
                    ins = v_.tensor_reduce(nmax[:, h % 2, t:t + 1], scores(h, t), AX, ALU.max)
                link(ins)
                v_.tensor_scalar(nmax[:, h % 2], nmax[:, h % 2], -SCALE, None, ALU.mult).then_inc(S("nmax"), 1)

            mod_round(1, 2)
            head_q(0)
            head_maxima(0)
            head_q(1)
            for h in range(NH):
                if h + 1 < NH:
                    head_maxima(h + 1)
                if h % 2 and h + 2 < NH:
                    head_q(h + 2)
                if h:
                    head_out(h - 1)
                if h % 2 == 0 and h + 2 < NH:
                    head_q(h + 2)
                head_probs_out(h)
            head_out(NH - 1)
            for t in range(TILES):
                dve.wait_ge(S("o_tr"), t + 1)
                v_.tensor_copy(yT[:, 2:DC, t * P:(t + 1) * P], bank2(2 * t, 6 * P).rearrange("p (k n) -> p k n", k=6)) \
                    .then_inc(S("y_att"), 1)
            project_out(1)
            normalise(3)
            norm_evacuate(1, 1)
            router(1)
            place_tokens(1)
            experts(1)
            experts_out(1)
            dve.wait_ge(S("finalg"), 16)
            for t in range(TILES):
                dve.wait_ge(*L(4, "norm_root", t + 1))
                v_.scalar_tensor_tensor(xn[:, t, :], x[:, t, :], rstd[:, t:t + 1], finalg, ALU.mult, ALU.mult) \
                    .then_inc(S("y"), 1)

        @block.tensor
        def _(pe):
            mm, tr = nc.tensor.matmul, nc.tensor.transpose

            def mod_round(l, i):
                mod_rows(l, i)
                mod_columns(l, i)

            def mod_rows(l, i, chunks=range(DC), groups=((0, 1, 2, 3),)):
                halves = (l, i) == (0, 0)
                names = [f"mod{l}.{4 * i + j}" for j in range(4)]
                w = [weight(name + ".0" * halves, DC, 512) for name in names]
                for group in groups:
                    for cc in chunks:
                        for j in group:
                            if cc == chunks[0]:
                                arrived(pe, names[j] + f".{cc // 4}" * halves)
                            ins = mm(ps[32 * j:32 * j + 32, 7, :], cs32[:, cc, :], w[j][:, cc, :], start=cc == 0, stop=cc == DC - 1)
                if cc == DC - 1:
                    ins.then_inc(S("mod_mm"), 1)

            def mod_columns(l, i):
                pe.wait_ge(*L(3 * l + i, "mod_row", 1))
                pick = ident.rearrange("p (v h a) -> p h v a", v=2, h=2)
                for cc in range(DC):
                    for h in range(2):
                        ins = mm(ps[64 * h:64 * h + 64, 6, 4 * cc:4 * cc + 4], mrow[l][:, i, cc::DC], pick[:, h, :, 0:2],
                                 start=True, stop=True)
                ins.then_inc(S("mod_cmm"), 1)

            def norm_transposes(l, w):
                for t in range(TILES):
                    pe.wait_ge(*L(2 * l + w, "norm_xn", t + 1))
                    for cc in range(DC):
                        ins = tr(bank2(2 * t, D)[:, cc * P:(cc + 1) * P], xn[:, t, cc::DC], ident)
                    ins.then_inc(S("norm_tr"), 1)

            def wait_hT(l, w, n=TILES):
                pe.wait_ge(*L(2 * l + w, "norm_hT_act", n))
                pe.wait_ge(*L(2 * l + w, "norm_hT_dve", n))

            def gate_rows(l, k, parts=range(4)):
                i, v = ((1, 0), (2, 1))[k]
                for n in parts:
                    r, half = n // 2, n % 2
                    if n >= 2:
                        pe.wait_ge(*L(2 * l + k, "gate_rows", n - 1))
                    at = 64 * v + 32 * half + r
                    mm(ps[:, 6 + n % 2, :], ident[:, at:at + 1].broadcast_to((P, P)), mrow[l][:, i, :], start=True, stop=True) \
                        .then_inc(S("gate_rows_mm"), 1)

            def project_out(l, parts):
                for t in range(TILES):
                    for n in range(2):
                        if (l, t, n) == (0, 1, 1):
                            pe.wait_ge(*L(0, "gate_rows", 4))
                            mod_round(0, 2)
                        for k in range(DC):
                            ins = mm(ps[:, 2 * t + n, :], yT[:, k, t * P:(t + 1) * P],
                                     weight(parts[k // 4], 4, D)[:, k % 4, n * 512:n * 512 + 512], start=k == 0, stop=k == DC - 1)
                        ins.then_inc(S("out_mm"), 1)

            def router(l):
                for t in range(TILES):
                    wait_hT(l, 1, t + 1)
                    for cc in range(DC):
                        ins = mm(ps[:, 0, 20 * t:20 * t + NG + NE], hT[:, cc, t * P:(t + 1) * P], wr[:, l, cc, :],
                                 start=cc == 0, stop=cc == DC - 1)
                ins.then_inc(S("router_mm"), 1)

            def by_tokens(l, tiles):
                for t in tiles:
                    if t == 0:
                        pe.wait_ge(*L(l, "gdiff", 1))
                    if t == 2:
                        pe.wait_ge(*L(l, "h_act", 1))
                    for cc in range(DC):
                        ins = tr(bank2((0, 2, 0)[t], D)[:, cc * P:(cc + 1) * P], hT[:, cc, t * P:(t + 1) * P], ident)
                    ins.then_inc(S("h_tr"), 1)

            def rank_tokens(l):
                pe.wait_ge(*L(l, "mask", 1))
                ones = cst[:, C_ONE:C_ONE + 1].broadcast_to((P, P))
                for s in range(TILES):
                    mm(ps[:, 5, NE * s:NE * (s + 1)], cst[:, C_TRI:C_TRI + P], R["mask"][:, s, :], start=s == 0, stop=s == 0)
                    after = TILES - s
                    ins = mm(ps[:, 5, NE * (s + 1):NE * (TILES + 1)].rearrange("p (t n) -> p t n", t=after), ones,
                             R["mask"][:, s:s + 1, :].broadcast_to((P, after, NE)), start=s == 0, stop=s == TILES - 1)
                ins.then_inc(S("rank_mm"), 1)

            def step_contents(l):
                pe.wait_ge(*L(l, "onehot", 1))
                rhs = R["steps_rhs"].rearrange("p t (v k n) -> p t v k n", v=2, k=2)
                for t in range(TILES):
                    for k in range(2):
                        ins = mm(ps[:, 4, 0:2 * STEPS], place_hot[:, t, k, :], rhs[:, t, :, k, :],
                                 start=(t, k) == (0, 0), stop=(t, k) == (TILES - 1, 1))
                ins.then_inc(S("meta_mm"), 1)

            def experts(l):
                before = places[l][1]

                def turn_tokens(chunks):
                    for cc in chunks:
                        for t in range(TILES):
                            ins = mm(bank2(2, D)[:, cc * P:(cc + 1) * P], xn[:, t, cc * P:(cc + 1) * P], select[:, t, :],
                                     start=t == 0, stop=t == TILES - 1)
                        if cc in (3, 7):
                            ins.then_inc(S(f"L{l}_x_{cc}"), 1)

                def up_slots(u):
                    return [s for s in range(6 * u, 6 * u + 6) if s % 3 < 2]

                def step(j, u, i):
                    w13 = [pool[:, 3 * (2 * u + e) * SLOT:(3 * (2 * u + e) + 2) * SLOT]
                           .rearrange("p (k c n) -> p k c n", k=2, c=DC) for e in range(2)]
                    w2 = [pool[:, (3 * (2 * u + e) + 2) * SLOT:3 * (2 * u + e + 1) * SLOT]
                          .rearrange("p (c n) -> p c n", c=2) for e in range(2)]
                    halves = [slice(e * HALF, (e + 1) * HALF) for e in range(2)]
                    pe.wait_ge(S(f"L{l}_hTe_act"), j + 1)
                    for cc in range(DC):
                        if cc == 4:
                            pe.wait_ge(S(f"L{l}_hTe_dve"), j + 1)
                        for e, m in enumerate(halves):
                            ins = mm(ps[m, 0, :], hTe.rearrange("p (c n) -> p c n", c=DC)[:, cc, m], w13[e][:, :, cc, :],
                                     start=cc == 0, stop=cc == DC - 1)
                    ins.then_inc(S(f"L{l}_up_mm"), 1)
                    pe.wait_ge(S(f"L{l}_select"), j + 2)
                    turn_tokens((0, 1))
                    pe.wait_ge(S(f"L{l}_hid"), j + 1)
                    for cc in range(2):
                        ins = tr(ps[:, 1, cc * P:(cc + 1) * P], hid[:, cc::2], ident)
                    ins.then_inc(S(f"L{l}_hid_tr"), 1)
                    turn_tokens((2, 3))
                    for e in range(2):
                        s = 3 * (2 * u + e) + 2
                        pe.wait_ge(S(f"slot{s}"), i * 16 + 16 * (before[s] + 1))
                    pe.wait_ge(S(f"L{l}_hidT"), j + 1)
                    pe.wait_ge(S(f"L{l}_ys"), j + 1)
                    for n in range(2):
                        for cc in range(2):
                            for e, m in enumerate(halves):
                                ins = mm(ps[m, 4 + n, :], hidT[:, cc, m], w2[e][:, cc, n * 512:n * 512 + 512],
                                         start=cc == 0, stop=cc == 1)
                    ins.then_inc(S(f"L{l}_down_mm"), 1)
                    turn_tokens(range(4, DC))

                pe.wait_ge(*L(l, "h_act", 3))
                pe.wait_ge(S(f"L{l}_select"), 1)
                turn_tokens(range(DC))
                step_contents(l)
                with pe.Fori(0, TURNS) as i:
                    for u in range(UNROLL):
                        for s in up_slots(u):
                            pe.wait_ge(S(f"slot{s}"), i * 16 + 16 * (before[s] + 1))
                        pe.nop()
                        so_far = pe.value_load(table[0:1, l, bass.ds(i * UNROLL + (T_CUM + u), 1)], min_val=0, max_val=STEPS)
                        rounds = pe.value_load(table[0:1, l, bass.ds(i * UNROLL + (T_ROUNDS + u), 1)], min_val=1, max_val=T // HALF)
                        with pe.Fori(0, rounds) as r:
                            step(so_far + r, u, i)
                n = pe.value_load(table[0:1, l, T_ALL:T_ALL + 1], min_val=PAIRS, max_val=STEPS)
                pe.wait_ge(S(f"L{l}_ys"), n + 1)
                pe.nop()

            pe.wait_ge(S("cs32"), 1)
            mod_rows(0, 0, range(0, 4))
            pe.wait_ge(S("ident_in"), 16)
            norm_transposes(0, 0)
            mod_rows(0, 0, range(4, DC), ((0, 1), (2, 3)))
            mod_columns(0, 0)
            arrived(pe, "v")
            for t in range(TILES):
                wait_hT(0, 0, t + 1)
                for cc in range(DC):
                    ins = mm(ps[:, t, :], hT[:, cc, t * P:(t + 1) * P], weight("v", DC, 512)[:, cc, :], start=cc == 0, stop=cc == DC - 1)
                ins.then_inc(S("v_mm"), 1)
            pe.wait_ge(*L(0, "mod_col", 1))
            for j in range(4):
                if j % 2 == 0:
                    for name in ("gate_c", "xa", "gate_b"):
                        arrived(pe, f"{name}.{j // 2}")
                if j == 1:
                    pe.wait_ge(S("vn"), 1)
                if j >= 2:
                    pe.wait_ge(S("y_conv"), j - 1)
                for k, name in enumerate(("gate_c", "xa", "gate_b")):
                    for cc in range(DC):
                        ins = mm(ps[:, ((3, 6)[j % 2] + k) % 8, 0:T], weight(f"{name}.{j // 2}", DC, 256)[:, cc, j % 2::2], hT[:, cc, :],
                                 start=cc == 0, stop=cc == DC - 1)
                ins.then_inc(S("conv_mm"), 1)
            pe.wait_ge(S("vn"), 3)
            pe.wait_ge(S("late"), 16 * N_LATE)
            for g in range(4):
                ins = tr(ps[:, 1, g * P:(g + 1) * P], sguw[:, g, :], ident)
            ins.then_inc(S("sgu_tr"), 1)
            arrived(pe, "u")
            for g in range(4):
                bs, bu = (1, 4)[g % 2], (2, 3)[g % 2]
                if g == 1:
                    pe.wait_ge(S("y_conv"), 3)
                if g >= 2:
                    pe.wait_ge(S("y_sgu"), g - 1)
                for cc in range(DC):
                    mm(ps[:, bu, 0:T], weight("u", DC, 512)[:, cc, g * P:(g + 1) * P], hT[:, cc, :], start=cc == 0, stop=cc == DC - 1)
                pe.wait_ge(S("sguT"), 1)
                for t in range(TILES):
                    ins = mm(ps[:, bs, t * P:(t + 1) * P], vn[:, t, g * P:(g + 1) * P], sguT[:, g, :], start=True, stop=True)
                ins.then_inc(S("sgu_mm"), 1)
            pe.wait_ge(S("y_conv"), 4)
            pe.wait_ge(S("y_sgu"), 4)
            mod_round(0, 1)
            pe.wait_ge(*L(1, "mod_col", 1))
            gate_rows(0, 0)
            arrived(pe, "out0.0")
            arrived(pe, "out0.1")
            project_out(0, ("out0.0", "out0.1"))
            mod_rows(1, 0)
            norm_transposes(0, 1)
            pe.wait_ge(*L(2, "mod_col", 1))
            mod_columns(1, 0)
            pe.wait_ge(*L(3, "mod_col", 1))
            gate_rows(0, 1, (0, 1))
            router(0)
            by_tokens(0, (0, 1))
            rank_tokens(0)
            by_tokens(0, (2,))
            gate_rows(0, 1, (2, 3))
            experts(0)
            mod_round(1, 1)
            norm_transposes(1, 0)

            for half in range(2):
                arrived(pe, f"in1.{half}")
                w = weight(f"in1.{half}", 4, Z_END)
                for t in range(TILES):
                    if half == 0:
                        wait_hT(1, 0, t + 1)
                    for b, lo, hi in ((2 * t, 0, 512), (2 * t + 1, 512, Z_END)):
                        for k in range(4):
                            cc = 4 * half + k
                            ins = mm(ps[:, b, 0:hi - lo], hT[:, cc, t * P:(t + 1) * P], w[:, k, lo:hi], start=cc == 0, stop=cc == DC - 1)
                        if half:
                            ins.then_inc(S("z_mm"), 1)
            pe.wait_ge(S("z_low"), 3)
            pe.wait_ge(S("z_high"), 3)
            pe.wait_ge(*L(1, "gate_rows", 4))
            for j in range(2):
                b = (6, 4)[j]
                mm(ps[:, b, 0:2 * P], z[:, 0, j * P:(j + 1) * P], cst[:, C_CS1:C_CS2], start=True, stop=True)
                for t in (1, 2):
                    ins = mm(ps[:, b + 1, :], z[:, t, j * P:(j + 1) * P], cst[:, C_CS2 + 512 * (t - 1):C_CS2 + 512 * t],
                             start=t == 1, stop=t == 2)
                ins.then_inc(S("four_tok_mm"), 1)
            pe.wait_ge(S("qn"), 3)
            for cc in range(3):
                for t in range(TILES):
                    ins = tr(ps[:, cc, t * P:(t + 1) * P], z[:, t, Z_Q + cc:Z_KV:3], ident)
                ins.then_inc(S("qn_tr"), 1)
            pe.wait_ge(S("kvn"), 3)
            pe.wait_ge(S("fmid"), 2)
            for cc in range(2):
                for kt in range(4):
                    src = ckv[:, cc::2] if kt == 1 else z[:, (0, None, 1, 2)[kt], Z_KV + cc:Z_PE:2]
                    ins = tr(ps[:, 3 + cc, kt * P:(kt + 1) * P], src, ident)
                ins.then_inc(S("kv_tr"), 1)
            pe.wait_ge(S("kpe"), 1)
            for kt in range(4):
                ins = mm(ps[NOPE:QH, 5, kt * P:(kt + 1) * P], kpe[:, kt, :], ident, start=True, stop=True)
            ins.then_inc(S("kpe_tr"), 1)
            for j in range(2):
                for k in range(2):
                    ins = mm(ps[:, 6 + j, 0:T], cst[:, C_CC + P * k:C_CC + P * (k + 1)], fmid[j][:, k, :], start=k == 0, stop=k == 1)
            ins.then_inc(S("four_mm"), 1)
            pe.wait_ge(S("qnT"), 3)
            arrived(pe, "uq")
            for t in range(TILES):
                if t == 1:
                    pe.wait_ge(S("kvT"), 2)
                    pe.wait_ge(S("kpeT"), 1)
                if t == 2:
                    pe.wait_ge(S("q_out"), 1)
                for n, w in ((0, 512), (1, 512), (2, 128)):
                    for cc in range(3):
                        ins = mm(ps[:, 3 * (t % 2) + n, 0:w], qnT[:, cc, t * P:(t + 1) * P],
                                 weight("uq", 3, NH * QH)[:, cc, n * 512:n * 512 + w], start=cc == 0, stop=cc == 2)
                ins.then_inc(S("q_mm"), 1)
            arrived(pe, "ukv")
            ukv = weight("ukv", 2, NH * 2 * VD).rearrange("p c (h n) -> p c h n", h=NH)
            pe.wait_ge(S("y_four"), 1)
            for kt in range(4):
                if kt == 1:
                    pe.wait_ge(S("q_out"), 2)
                if kt >= 2:
                    pe.wait_ge(S("vv"), kt - 1)
                for n, h0, h1 in ((0, 0, 8), (1, 8, NH)):
                    for cc in range(2):
                        ins = mm(ps[:, (6, 3)[kt % 2] + n, 0:(h1 - h0) * VD], kvT[:, cc, kt * P:(kt + 1) * P],
                                 ukv[:, cc, h0:h1, NOPE:NOPE + VD], start=cc == 0, stop=cc == 1)
                ins.then_inc(S("v2_mm"), 1)
            pe.wait_ge(S("q_rot"), 1)
            pe.wait_ge(S("q_out"), 3)
            pe.wait_ge(S("vv"), 4)
            pe.wait_ge(S("kpeT"), 1)

            def head_probs(h):
                pe.wait_ge(S("probs"), h + 1)
                for m in range(7):
                    ins = tr(bank2(4, 7 * P)[:, m * P:(m + 1) * P], pr_s[:, m * P:(m + 1) * P], ident)
                ins.then_inc(S("p_tr"), 1)

            def head_values(h):
                pe.wait_ge(S("pT_act"), h + 1)
                pe.wait_ge(S("pT_dve"), h + 1)
                if h:
                    pe.wait_ge(S("o_out"), h)
                for t in range(TILES):
                    keys = ((0, 0),) if t == 0 else tuple((1 + k, 1 + 3 * (t - 1) + k) for k in range(3))
                    for n, (kt, m) in enumerate(keys):
                        ins = mm(ps[:, 1, t * VD:(t + 1) * VD], prT[:, m * P:(m + 1) * P],
                                 vv[:, kt, h * VD:(h + 1) * VD], start=n == 0, stop=n == len(keys) - 1)
                ins.then_inc(S("o_mm"), 1)

            def k_pair(g):
                if g:
                    pe.wait_ge(S("qT"), 2 * g)
                for cc in range(2):
                    for b in range(2):
                        ins = mm(ps[b * NOPE:(b + 1) * NOPE, 0, :], ukv[:, cc, 2 * g + b, 0:NOPE], kvT[:, cc, :],
                                 start=cc == 0, stop=cc == 1)
                ins.then_inc(S("k_mm"), 1)

            def head_q(h):
                if h:
                    pe.wait_ge(S("qT"), h)
                pe.wait_ge(S("kT"), h // 2 + 1)
                for t in range(TILES):
                    ins = tr(ps[0:QH, 0, t * P:(t + 1) * P], q[:, t, h * QH:(h + 1) * QH], ident)
                ins.then_inc(S("qT_tr"), 1)

            def head_scores(h):
                pe.wait_ge(S("kT"), h // 2 + 1)
                pe.wait_ge(S("qT"), h + 1)
                for t in range(TILES):
                    ins = mm(scores(h, t), qT[0:QH, h % 2, t * P:(t + 1) * P], kT[0:QH, h % 2, 0:P] if t == 0 else kT[0:QH, h % 2, P:512],
                             start=True, stop=True)
                ins.then_inc(S("s_mm"), 1)

            mod_rows(1, 2)
            k_pair(0)
            mod_columns(1, 2)
            head_q(0)
            pe.wait_ge(*L(5, "mod_col", 1))
            head_scores(0)
            head_q(1)
            for h in range(NH):
                if h + 1 < NH:
                    head_scores(h + 1)
                if h % 2 == 0 and h + 2 < NH:
                    k_pair(h // 2 + 1)
                elif h + 2 < NH:
                    head_q(h + 2)
                if h:
                    head_values(h - 1)
                if h % 2 == 0 and h + 2 < NH:
                    head_q(h + 2)
                head_probs(h)
            head_values(NH - 1)
            pe.wait_ge(S("o_out"), NH)
            for t in range(TILES):
                for k in range(6):
                    ins = tr(bank2(2 * t, 6 * P)[:, k * P:(k + 1) * P], o[:, t, k * P:(k + 1) * P], ident)
                ins.then_inc(S("o_tr"), 1)
            pe.wait_ge(*L(4, "mod_col", 1))
            gate_rows(1, 0)
            pe.wait_ge(S("y_att"), 3)
            arrived(pe, "out1.0")
            arrived(pe, "out1.1")
            project_out(1, ("out1.0", "out1.1"))
            pe.wait_ge(*L(2, "gate_rows", 4))
            norm_transposes(1, 1)
            gate_rows(1, 1, (0, 1))
            router(1)
            by_tokens(1, (0, 1))
            rank_tokens(1)
            by_tokens(1, (2,))
            gate_rows(1, 1, (2, 3))
            experts(1)


def constants():
    import numpy as np

    out = np.zeros((P, C_END), np.float64)
    out[:, C_ID:C_ID + P] = np.eye(P)
    p = np.arange(P)
    gw = DCF // 4
    for at, n, tiles in ((C_CS1, P, 1), (C_CS2, 2 * P, 2)):
        for k in range(tiles):
            ang = 2 * np.pi * ((np.outer(p + k * P, np.arange(n))) % n) / n
            scale = 1.0 / np.sqrt(n * gw)
            out[:, at + 2 * n * k:at + 2 * n * k + n] = np.cos(ang) * scale
            out[:, at + 2 * n * k + n:at + 2 * n * (k + 1)] = np.sin(ang) * scale
    ang = 2 * np.pi * (np.outer(p, p) % gw) / gw
    same = (p[:, None] // gw) == (p[None, :] // gw)
    out[:, C_CC:C_CC + P] = np.cos(ang) * same
    out[:, C_CC + P:C_CC + 2 * P] = -np.sin(ang) * same
    nf = ROPE // 4
    inv = (10000.0 ** (-np.arange(nf, dtype=np.float32) / np.float32(nf))).astype(np.float32)
    for t in range(2):
        tok = t * P + p
        for k, pos in enumerate((tok // GRID_W, tok % GRID_W)):
            ang = (pos.astype(np.float32)[:, None] * inv[None, :]).astype(np.float32)
            out[:, C_COS + 16 * t + 8 * k:C_COS + 16 * t + 8 * k + 8] = np.cos(ang)
            out[:, C_SIN + 16 * t + 8 * k:C_SIN + 16 * t + 8 * k + 8] = np.sin(ang)
    out[:, C_FIRST:C_TRI] = np.arange(4, 0, -1)
    out[:, C_TRI:C_IOTA] = p[:, None] < p[None, :]
    out[:, C_IOTA:C_TOK] = p
    for t in range(TILES):
        out[:, C_TOK + 2 * t:C_TOK + 2 * t + 2] = p[:, None] + P * t + 1 + np.array([0, T])
    out[:, C_HALF:C_ONE] = HALF * (np.arange(NE) % 2)
    out[:, C_ONE] = 1
    out[:, C_OVER:C_END] = HALF * np.arange(STEPS + 1)
    out[:, C_OVER] = -1
    return out.astype(np.float32)


INS = ["x_prompt", "x_sample", "cache_ckv", "cache_kpe", "c", "c_ctx", "mod_w", "mod_b", "norm1_g", "norm2_g",
       "ev_w_in", "ev_conv_w", "ev_sgu_norm_g", "ev_sgu_w", "ev_sgu_b", "ev_w_out", "od_w_in", "od_q_norm_g",
       "od_w_uq", "od_kv_norm_g", "od_w_ukv", "od_w_out", "moe_wg", "moe_bg", "moe_we", "moe_be", "moe_w1",
       "moe_w3", "moe_w2", "final_norm_g"]
OUTS = [(1, P, D), (1, 2 * P, D), (1, 1, P, KVL), (1, 1, P, ROPE)]


def kernel(**inputs):
    import numpy as np
    import concourse.bacc as bacc
    from concourse.bass_utils import run_bass_kernel_spmd

    nc = bacc.Bacc("TRN2", target_bir_lowering=False, num_devices=1)
    arrays, args = {}, []
    for name in INS:
        a = np.ascontiguousarray(inputs[name])
        arrays[f"in_{name}"] = a
        args.append(nc.dram_tensor(f"in_{name}", a.shape, F32, kind="ExternalInput").ap())
    arrays["in_consts"] = constants()
    args.append(nc.dram_tensor("in_consts", (P, C_END), F32, kind="ExternalInput").ap())
    for i, shape in enumerate(OUTS):
        args.append(nc.dram_tensor(f"out_{i}", shape, F32, kind="ExternalOutput").ap())
    program(nc, *args)
    r = run_bass_kernel_spmd(nc, [arrays], core_ids=[0])
    return tuple(r.results[0][f"out_{i}"] for i in range(len(OUTS)))
```
